# Optimizing a Trainium2 kernel written in Bass

```python
import jax
import jax.numpy as jnp
from jax import lax
import numpy as np

D_MODEL = 1024
BATCH = 1
SEQ = 256
DEPTH = 4
DEC_BATCH = 8
DEC_SEQ = 8
PAST_LEN = 1024
PAGE_SIZE = 128

N_HEADS = 16
HEAD_DIM = D_MODEL // N_HEADS
D_FF = 2816
RMS_EPS = 1e-6
ROPE_THETA = 10000.0
N_MIXERS = 4
LAYER_PATTERN = ('chunk_mlp', 'swa', 'short_conv', 'nsa')
CM_WIDTH = D_MODEL
CM_CHUNK = 128
CM_GROUPS = 4
SWA_KV_HEADS = 2
SWA_WINDOW = 128
SC_WIDTH = D_MODEL
SC_CONV_W = 3
NSA_KV_HEADS = 2
NSA_CMP_LEN = 32
NSA_CMP_STRIDE = 16
NSA_CMP_HIDDEN = 256
NSA_SEL_LEN = 64
NSA_SEL_TOP = 16
NSA_WINDOW = 128
NSA_Q_BLOCK_PROMPT = 64
NSA_Q_BLOCK_SAMPLE = 1
NEG_INF = -1e30
FORCE_SCORE = 1e9

kernel_name = 'hybrid_chunkmlp_swa_shortconv_nsa_decode_step'

def _rmsnorm(x, g):
    xf = x.astype(jnp.float32)
    xf = xf * lax.rsqrt(jnp.mean(xf * xf, axis=-1, keepdims=True) + RMS_EPS)
    return (xf * g.astype(jnp.float32)).astype(x.dtype)

def _swiglu(x, w_in, w_out):
    gate, up = jnp.split(x @ w_in, 2, axis=-1)
    return (jax.nn.silu(gate) * up) @ w_out

def _rope(x, pos):
    half = x.shape[-1] // 2
    inv = jnp.power(jnp.float32(ROPE_THETA), -jnp.arange(half, dtype=jnp.float32) / half)
    ang = pos.astype(jnp.float32)[:, None] * inv[None, :]
    cos = jnp.cos(ang)[None, :, None, :]
    sin = jnp.sin(ang)[None, :, None, :]
    xf = x.astype(jnp.float32)
    x1, x2 = xf[..., :half], xf[..., half:]
    return jnp.concatenate([x1 * cos - x2 * sin, x2 * cos + x1 * sin], axis=-1).astype(x.dtype)

def _softmax_masked(s, mask, sink=None):
    s = jnp.where(mask, s, NEG_INF)
    if sink is None:
        return jax.nn.softmax(s, axis=-1)
    g, r = s.shape[-4], s.shape[-3]
    sk = jnp.broadcast_to(sink.astype(jnp.float32).reshape(g, r, 1, 1), s.shape[:-1] + (1,))
    return jax.nn.softmax(jnp.concatenate([s, sk], axis=-1), axis=-1)[..., :-1]

def _band_attn_prompt(q, k, v, window, sink):
    b, t, h, d = q.shape
    g = k.shape[2]
    r = h // g
    nb = t // window
    qb = q.reshape(b, nb, window, g, r, d)

    def with_prev(a):
        a = a.reshape(b, nb, window, g, d)
        prev = jnp.pad(a, ((0, 0), (1, 0), (0, 0), (0, 0), (0, 0)))[:, :-1]
        return jnp.concatenate([prev, a], axis=2)

    kk, vv = with_prev(k), with_prev(v)
    s = jnp.einsum('bcigrd,bcjgd->bcgrij', qb, kk).astype(jnp.float32) * (d ** -0.5)
    i = jnp.arange(window)[:, None]
    j = jnp.arange(2 * window)[None, :]
    blk = jnp.arange(nb)[:, None, None]
    mask = (j >= i) & (j <= i + window) & ((blk > 0) | (j >= window))
    p = _softmax_masked(s, mask[None, :, None, None], sink)
    o = jnp.einsum('bcgrij,bcjgd->bcigrd', p.astype(v.dtype), vv)
    return o.reshape(b, t, h, d)

def _band_attn_sample(q, k_buf, v_buf, k_new, v_new, window, sink):
    b, s_len, h, d = q.shape
    g = k_new.shape[2]
    r = h // g
    kk = jnp.concatenate([k_buf.astype(k_new.dtype), k_new], axis=1)
    vv = jnp.concatenate([v_buf.astype(v_new.dtype), v_new], axis=1)
    s = jnp.einsum('bigrd,bjgd->bgrij', q.reshape(b, s_len, g, r, d), kk).astype(jnp.float32) * (d ** -0.5)
    i = jnp.arange(s_len)[:, None]
    j = jnp.arange(window + s_len)[None, :]
    mask = (j >= i) & (j <= i + window)
    p = _softmax_masked(s, mask, sink)
    o = jnp.einsum('bgrij,bjgd->bigrd', p.astype(vv.dtype), vv)
    return o.reshape(b, s_len, h, d), kk, vv

def _mixer_chunk_mlp(xn, chunk_len, w_in, norm_g, w_s, b_s, w_out):
    b, t, _ = xn.shape
    u, v = jnp.split(jax.nn.gelu(xn @ w_in), 2, axis=-1)
    v = _rmsnorm(v, norm_g)
    nc = t // chunk_len
    dg = CM_WIDTH // CM_GROUPS
    causal = jnp.tril(jnp.ones((chunk_len, chunk_len), dtype=bool))
    ws = jnp.where(causal, w_s[:, :chunk_len, :chunk_len], 0.0).astype(v.dtype)
    vc = v.reshape(b, nc, chunk_len, CM_GROUPS, dg)
    mixed = jnp.einsum('gji,bcigd->bcjgd', ws, vc) + b_s[:, :chunk_len].T[:, :, None]
    y = u * mixed.reshape(b, t, CM_WIDTH)
    return y @ w_out, v

def _mixer_short_conv(xn, prev, w_in, conv_w, w_out):
    t = xn.shape[1]
    gb, gc, h = jnp.split(xn @ w_in, 3, axis=-1)
    z = jnp.concatenate([prev.astype(xn.dtype), gc * h], axis=1)
    conv = sum(conv_w[k] * z[:, k:k + t] for k in range(SC_CONV_W))
    return (gb * conv) @ w_out, z[:, -(SC_CONV_W - 1):]

def _mixer_swa(xn, pos, buf, w_qkv, sinks, w_o):
    b, t, _ = xn.shape
    qd = N_HEADS * HEAD_DIM
    kvd = SWA_KV_HEADS * HEAD_DIM
    qkv = xn @ w_qkv
    q = _rope(qkv[..., :qd].reshape(b, t, N_HEADS, HEAD_DIM), pos)
    k = _rope(qkv[..., qd:qd + kvd].reshape(b, t, SWA_KV_HEADS, HEAD_DIM), pos)
    v = qkv[..., qd + kvd:].reshape(b, t, SWA_KV_HEADS, HEAD_DIM)
    if buf is None:
        o = _band_attn_prompt(q, k, v, SWA_WINDOW, sinks)
        new = jnp.stack([k, v], axis=2)[:, -SWA_WINDOW:]
    else:
        o, kk, vv = _band_attn_sample(q, buf[:, :, 0], buf[:, :, 1], k, v, SWA_WINDOW, sinks)
        new = jnp.stack([kk, vv], axis=2)[:, -SWA_WINDOW:]
    return o.reshape(b, t, qd) @ w_o, new

def _nsa_compress(kf, w1, pe, w2):
    b, tk, g, d = kf.shape
    n_parts = NSA_CMP_LEN // NSA_CMP_STRIDE
    n_cmp = (tk - NSA_CMP_LEN) // NSA_CMP_STRIDE + 1
    n_sub = n_cmp + n_parts - 1
    sub = kf[:, :n_sub * NSA_CMP_STRIDE].reshape(b, n_sub, NSA_CMP_STRIDE, g, d)
    hid = 0.0
    for m in range(n_parts):
        rows = slice(m * NSA_CMP_STRIDE, (m + 1) * NSA_CMP_STRIDE)
        part = jnp.einsum('bnpgd,pdh->bngh', sub + pe[rows][:, None, :], w1[rows])
        hid = hid + part[:, m:m + n_cmp]
    return jax.nn.gelu(hid) @ w2

def _nsa_query_block(q_plain, q_rot, qpos, k_cmp, v_cmp, k_sel, v_sel):
    b, qb, h, d = q_plain.shape
    g = k_cmp.shape[2]
    r = h // g
    n_cmp = k_cmp.shape[1]
    n_sel = k_sel.shape[2]
    scale = d ** -0.5
    s_c = jnp.einsum('bqgrd,bngd->bqgrn', q_plain.reshape(b, qb, g, r, d), k_cmp).astype(jnp.float32) * scale
    c_end = jnp.arange(n_cmp) * NSA_CMP_STRIDE + (NSA_CMP_LEN - 1)
    c_ok = (c_end[None, :] <= qpos[:, None])[None, :, None, None, :]
    p_c = jnp.where(c_ok, _softmax_masked(s_c, c_ok), 0.0)
    o_cmp = jnp.einsum('bqgrn,bngd->bqgrd', p_c.astype(v_cmp.dtype), v_cmp)
    lead = NSA_CMP_LEN // NSA_CMP_STRIDE - 1
    per_blk = NSA_SEL_LEN // NSA_CMP_STRIDE
    imp = jnp.pad(p_c.sum(axis=3), ((0, 0), (0, 0), (0, 0), (lead, per_blk * (n_sel + 1) - lead - n_cmp)))
    imp = imp.reshape(b, qb, g, n_sel + 1, per_blk)
    score = imp[..., :n_sel, :].sum(-1) + imp[..., 1:, :lead].sum(-1)
    blk = jnp.arange(n_sel)[None, :]
    cur = (qpos // NSA_SEL_LEN)[:, None]
    forced = ((blk == 0) | (blk == cur) | (blk == cur - 1))[None, :, None, :]
    causal = (blk * NSA_SEL_LEN <= qpos[:, None])[None, :, None, :]
    score = jnp.where(causal, jnp.where(forced, FORCE_SCORE, score), NEG_INF)
    n_top = min(NSA_SEL_TOP, n_sel)
    _, idx = lax.top_k(score, n_top)
    bi = jnp.arange(b)[:, None, None, None]
    gi = jnp.arange(g)[None, None, :, None]
    k_g = k_sel[bi, gi, idx]
    v_g = v_sel[bi, gi, idx]
    k_pos = idx[..., None] * NSA_SEL_LEN + jnp.arange(NSA_SEL_LEN)
    k_ok = (k_pos <= qpos[None, :, None, None, None])[:, :, :, None]
    s_s = jnp.einsum('bqgrd,bqgkld->bqgrkl', q_rot.reshape(b, qb, g, r, d), k_g).astype(jnp.float32) * scale
    s_s = jnp.where(k_ok, s_s, NEG_INF).reshape(b, qb, g, r, n_top * NSA_SEL_LEN)
    p_s = jax.nn.softmax(s_s, axis=-1)
    o_sel = jnp.einsum('bqgrm,bqgmd->bqgrd', p_s.astype(v_g.dtype), v_g.reshape(b, qb, g, n_top * NSA_SEL_LEN, d))
    return o_cmp.reshape(b, qb, h, d), o_sel.reshape(b, qb, h, d)

def _nsa_cmp_sel(q_plain, q_rot, pos, k_cmp, v_cmp, k_sel, v_sel, q_block):
    b, t, h, d = q_plain.shape
    nq = t // q_block

    def split(a):
        return a.reshape(b, nq, q_block, h, d).swapaxes(0, 1)

    def body(args):
        qp, qr, qpos = args
        return _nsa_query_block(qp, qr, qpos, k_cmp, v_cmp, k_sel, v_sel)

    o_c, o_s = lax.map(body, (split(q_plain), split(q_rot), pos.reshape(nq, q_block)))

    def merge(a):
        return a.swapaxes(0, 1).reshape(b, t, h, d)

    return merge(o_c), merge(o_s)

def _mixer_nsa(xn, pos, q_block, past, win_buf, w_in, cmp_w1, cmp_pe, cmp_w2, w_o):
    b, t, _ = xn.shape
    qd = N_HEADS * HEAD_DIM
    kvd = NSA_KV_HEADS * HEAD_DIM
    proj = xn @ w_in
    q = proj[..., :qd].reshape(b, t, N_HEADS, HEAD_DIM)
    kv4 = proj[..., qd:qd + 4 * kvd].reshape(b, t, 4, NSA_KV_HEADS, HEAD_DIM)
    kvw = proj[..., qd + 4 * kvd:qd + 6 * kvd].reshape(b, t, 2, NSA_KV_HEADS, HEAD_DIM)
    gates = jax.nn.sigmoid(proj[..., qd + 6 * kvd:].astype(jnp.float32)).reshape(b, t, 3, N_HEADS, 1)
    q_rot = _rope(q, pos)
    rows = jnp.stack([kv4[:, :, 0], kv4[:, :, 1], _rope(kv4[:, :, 2], pos), kv4[:, :, 3]], axis=2)
    k_win = _rope(kvw[:, :, 0], pos)
    v_win = kvw[:, :, 1]
    full = rows if past is None else jnp.concatenate([past.astype(rows.dtype), rows], axis=1)
    tk = full.shape[1]
    k_cmp = _nsa_compress(full[:, :, 0], cmp_w1[0], cmp_pe[0], cmp_w2[0])
    v_cmp = _nsa_compress(full[:, :, 1], cmp_w1[1], cmp_pe[1], cmp_w2[1])
    n_sel = -(-tk // NSA_SEL_LEN)
    sel = jnp.pad(full[:, :, 2:], ((0, 0), (0, n_sel * NSA_SEL_LEN - tk), (0, 0), (0, 0), (0, 0)))
    sel = sel.reshape(b, n_sel, NSA_SEL_LEN, 2, NSA_KV_HEADS, HEAD_DIM).transpose(3, 0, 4, 1, 2, 5)
    o_cmp, o_sel = _nsa_cmp_sel(q, q_rot, pos, k_cmp, v_cmp, sel[0], sel[1], q_block)
    if win_buf is None:
        o_win = _band_attn_prompt(q_rot, k_win, v_win, NSA_WINDOW, None)
        new_win = jnp.stack([k_win, v_win], axis=2)[:, -NSA_WINDOW:]
    else:
        o_win, kk, vv = _band_attn_sample(q_rot, win_buf[:, :, 0], win_buf[:, :, 1], k_win, v_win, NSA_WINDOW, None)
        new_win = jnp.stack([kk, vv], axis=2)[:, -NSA_WINDOW:]
    o = gates[:, :, 0] * o_cmp + gates[:, :, 1] * o_sel + gates[:, :, 2] * o_win
    return o.astype(xn.dtype).reshape(b, t, qd) @ w_o, (rows, new_win)

def _trunk(x, pos, chunk_len, q_block, swa_buf, conv_prev, nsa_past, nsa_win_buf, w):
    states = []
    for i in range(DEPTH):
        x = x + 0.5 * _swiglu(_rmsnorm(x, w['norm_g'][i, 0]), w['ffn_in'][i, 0], w['ffn_out'][i, 0])
        h = _rmsnorm(x, w['norm_g'][i, 1])
        kind = LAYER_PATTERN[i % N_MIXERS]
        if kind == 'chunk_mlp':
            m, st = _mixer_chunk_mlp(h, chunk_len, w['cm_w_in'], w['cm_norm_g'], w['cm_w_s'], w['cm_b_s'], w['cm_w_out'])
        elif kind == 'swa':
            m, st = _mixer_swa(h, pos, swa_buf, w['swa_w_qkv'], w['swa_sinks'], w['swa_w_o'])
        elif kind == 'short_conv':
            m, st = _mixer_short_conv(h, conv_prev, w['sc_w_in'], w['sc_conv_w'], w['sc_w_out'])
        else:
            m, st = _mixer_nsa(h, pos, q_block, nsa_past, nsa_win_buf, w['nsa_w_in'], w['nsa_cmp_w1'], w['nsa_cmp_pe'], w['nsa_cmp_w2'], w['nsa_w_o'])
        states.append(st)
        x = x + m
        x = x + 0.5 * _swiglu(_rmsnorm(x, w['norm_g'][i, 2]), w['ffn_in'][i, 1], w['ffn_out'][i, 1])
    return _rmsnorm(x, w['final_norm_g']), states

def setup_inputs(seed: int = 0) -> dict:
    key = jax.random.key(seed)
    ks = iter(jax.random.split(key, 32))

    def nrm(shape, scale):
        return jax.random.normal(next(ks), shape, jnp.float32) * scale

    n_pages = PAST_LEN // PAGE_SIZE
    n_used = DEC_BATCH * n_pages
    n_pool = n_used + n_used // 4
    qd = N_HEADS * HEAD_DIM
    page_table = jax.random.permutation(next(ks), n_pool)[:n_used].reshape(DEC_BATCH, n_pages).astype(jnp.int32)
    return {
        'x_prompt': nrm((BATCH, SEQ, D_MODEL), 1.0),
        'x_sample': nrm((DEC_BATCH, DEC_SEQ, D_MODEL), 1.0),
        'cache_swa_kv': nrm((DEC_BATCH, SWA_WINDOW, 2, SWA_KV_HEADS, HEAD_DIM), 1.0),
        'state_conv': nrm((DEC_BATCH, SC_CONV_W - 1, SC_WIDTH), 1.0),
        'cache_nsa_kv': nrm((n_pool, PAGE_SIZE, 4, NSA_KV_HEADS, HEAD_DIM), 1.0),
        'cache_nsa_win_kv': nrm((DEC_BATCH, NSA_WINDOW, 2, NSA_KV_HEADS, HEAD_DIM), 1.0),
        'page_table': page_table,
        'norm_g': 1.0 + nrm((DEPTH, 3, D_MODEL), 0.05),
        'final_norm_g': 1.0 + nrm((D_MODEL,), 0.05),
        'ffn_in': nrm((DEPTH, 2, D_MODEL, 2 * D_FF), D_MODEL ** -0.5),
        'ffn_out': nrm((DEPTH, 2, D_FF, D_MODEL), D_FF ** -0.5),
        'cm_w_in': nrm((D_MODEL, 2 * CM_WIDTH), D_MODEL ** -0.5),
        'cm_norm_g': 1.0 + nrm((CM_WIDTH,), 0.05),
        'cm_w_s': nrm((CM_GROUPS, CM_CHUNK, CM_CHUNK), CM_CHUNK ** -0.5),
        'cm_b_s': 1.0 + nrm((CM_GROUPS, CM_CHUNK), 0.1),
        'cm_w_out': nrm((CM_WIDTH, D_MODEL), CM_WIDTH ** -0.5),
        'swa_w_qkv': nrm((D_MODEL, qd + 2 * SWA_KV_HEADS * HEAD_DIM), D_MODEL ** -0.5),
        'swa_sinks': nrm((N_HEADS,), 1.0),
        'swa_w_o': nrm((qd, D_MODEL), qd ** -0.5),
        'sc_w_in': nrm((D_MODEL, 3 * SC_WIDTH), D_MODEL ** -0.5),
        'sc_conv_w': nrm((SC_CONV_W, SC_WIDTH), SC_CONV_W ** -0.5),
        'sc_w_out': nrm((SC_WIDTH, D_MODEL), SC_WIDTH ** -0.5),
        'nsa_w_in': nrm((D_MODEL, qd + 6 * NSA_KV_HEADS * HEAD_DIM + 3 * N_HEADS), D_MODEL ** -0.5),
        'nsa_cmp_w1': nrm((2, NSA_CMP_LEN, HEAD_DIM, NSA_CMP_HIDDEN), (NSA_CMP_LEN * HEAD_DIM) ** -0.5),
        'nsa_cmp_pe': nrm((2, NSA_CMP_LEN, HEAD_DIM), 0.5),
        'nsa_cmp_w2': nrm((2, NSA_CMP_HIDDEN, HEAD_DIM), NSA_CMP_HIDDEN ** -0.5),
        'nsa_w_o': nrm((qd, D_MODEL), qd ** -0.5),
    }

def reference(x_prompt, x_sample, cache_swa_kv, state_conv, cache_nsa_kv, cache_nsa_win_kv, page_table,
              norm_g, final_norm_g, ffn_in, ffn_out,
              cm_w_in, cm_norm_g, cm_w_s, cm_b_s, cm_w_out,
              swa_w_qkv, swa_sinks, swa_w_o,
              sc_w_in, sc_conv_w, sc_w_out,
              nsa_w_in, nsa_cmp_w1, nsa_cmp_pe, nsa_cmp_w2, nsa_w_o):
    w = dict(norm_g=norm_g, final_norm_g=final_norm_g, ffn_in=ffn_in, ffn_out=ffn_out,
             cm_w_in=cm_w_in, cm_norm_g=cm_norm_g, cm_w_s=cm_w_s, cm_b_s=cm_b_s, cm_w_out=cm_w_out,
             swa_w_qkv=swa_w_qkv, swa_sinks=swa_sinks, swa_w_o=swa_w_o,
             sc_w_in=sc_w_in, sc_conv_w=sc_conv_w, sc_w_out=sc_w_out,
             nsa_w_in=nsa_w_in, nsa_cmp_w1=nsa_cmp_w1, nsa_cmp_pe=nsa_cmp_pe, nsa_cmp_w2=nsa_cmp_w2, nsa_w_o=nsa_w_o)
    b_p, seq, _ = x_prompt.shape
    b_s, dec_seq, _ = x_sample.shape
    n_pages = page_table.shape[1]
    past_len = n_pages * cache_nsa_kv.shape[1]

    pos_p = jnp.arange(seq, dtype=jnp.int32)
    conv0 = jnp.zeros((b_p, SC_CONV_W - 1, SC_WIDTH), x_prompt.dtype)
    y_prompt, st_p = _trunk(x_prompt, pos_p, CM_CHUNK, NSA_Q_BLOCK_PROMPT, None, conv0, None, None, w)

    pos_s = past_len + jnp.arange(dec_seq, dtype=jnp.int32)
    past = cache_nsa_kv[page_table].reshape(b_s, past_len, 4, NSA_KV_HEADS, HEAD_DIM)
    y_sample, st_s = _trunk(x_sample, pos_s, dec_seq, NSA_Q_BLOCK_SAMPLE, cache_swa_kv, state_conv, past, cache_nsa_win_kv, w)

    cm_v_sample = st_s[0]
    swa_kv_prompt, swa_kv_sample = st_p[1], st_s[1]
    conv_prompt, conv_sample = st_p[2], st_s[2]
    nsa_kv_prompt, nsa_win_prompt = st_p[3]
    nsa_kv_sample, nsa_win_sample = st_s[3]
    return (y_prompt, y_sample, cm_v_sample, swa_kv_prompt, swa_kv_sample, conv_prompt, conv_sample, nsa_kv_prompt, nsa_kv_sample, nsa_win_prompt, nsa_win_sample)


_drawn_inputs = setup_inputs


def setup_inputs(seed=0):
    import zlib

    import numpy as np

    out = dict(_drawn_inputs(seed))
    spreads = {}
    factors = {}
    for name, (base, spread) in spreads.items():
        noise = np.random.default_rng([zlib.crc32(name.encode()), seed]).standard_normal(out[name].shape)
        drawn = base * np.exp(spread * noise) if base else spread * noise
        out[name] = jnp.asarray(drawn.astype(out[name].dtype))
    for name, factor in factors.items():
        out[name] = (out[name] * factor).astype(out[name].dtype)
    return out
```

```python
from contextlib import ExitStack

import numpy as np

import concourse.bass as bass
from concourse import mybir

F32 = mybir.dt.float32
F32R = mybir.dt.float32r
I32 = mybir.dt.int32
ACT = mybir.ActivationFunctionType
ALU = mybir.AluOpType
AX = mybir.AxisListType

P = 128
D = 1024
KT = D // P
NP_TOK = 256
NS_TOK = 64
T = NP_TOK + NS_TOK
NB, NQ = 8, 8
FF = 2816
FT = FF // P
CW = 256
EPS = 1e-6
HD = 64
SCALE = HD ** -0.5
PAST = 1024
PAGE = 128
NPAGES = PAST // PAGE
NEG = -1e30
RAW = 2
HALVES = 2 * RAW
BANKS = 4
N_CMP_P = 15
N_CMP_S = 63
PRIME = 4


def const_tables():
    c = {}
    eye = np.eye(P, dtype=np.float32)
    c["ident"] = eye
    c["ones"] = np.ones((P, P), np.float32)
    perm = np.zeros((P, P), np.float32)
    for blk in range(2):
        for d in range(32):
            perm[64 * blk + 32 + d, 64 * blk + d] = -1.0
            perm[64 * blk + d, 64 * blk + 32 + d] = 1.0
    c["perm"] = perm
    half = 32
    inv = np.power(np.float32(10000.0), -np.arange(half, dtype=np.float32) / np.float32(half)).astype(np.float32)
    pos = np.concatenate([np.arange(NP_TOK), np.tile(PAST + np.arange(NQ), NB)]).astype(np.float32)
    ang = (pos[None, :] * inv[:, None]).astype(np.float32)
    c["cos"] = np.tile(np.cos(ang), (4, 1)).astype(np.float32)
    c["sin"] = np.tile(np.sin(ang), (4, 1)).astype(np.float32)
    i = np.arange(P)[:, None]
    j = np.arange(P)[None, :]
    causal = np.where(j <= i, 0.0, NEG)
    prev = np.where(j >= i, 0.0, NEG)
    c["m_band"] = np.concatenate([prev, prev, causal, causal], 1)
    s = np.arange(P)[:, None] % NQ
    c["m_old"] = np.where(j >= s, 0.0, NEG)
    k = np.arange(NS_TOK)[None, :]
    c["m_new"] = np.concatenate([np.where((k // NQ == b) & (k % NQ <= s), 0.0, NEG) for b in range(NB)], 1)
    ok = 16 * (np.arange(40)[None, :] - 8) + 31 <= i
    c["m_cmp"] = np.where(ok, 0.0, NEG)
    c["ok_cmp"] = np.where(ok, 1.0, 0.0)
    c["sum_r"] = ((i // 64 == j // 64) & (i % NQ == j % NQ)).astype(np.float32)
    c["bd"] = (i // 64 == j // 64).astype(np.float32)
    c["blk_no"] = np.tile(np.arange(16, dtype=np.float32)[None, :], (P, 1))
    c["tri"] = (i <= j).astype(np.float32)
    r = np.arange(P)
    head_of = 8 * (r // 64) + (r % 64) // NQ
    c["row_of"] = np.concatenate([np.where(np.arange(P)[:, None] == 16 * k + head_of[None, :], 1.0, 0.0) for k in range(3)], 1)
    c["tok_of"] = (np.arange(NS_TOK)[None, :] % NQ == (r % NQ)[:, None]).astype(np.float32)
    c["eps"] = np.full((P, 1), EPS, np.float32)
    at, cols, parts = 0, {}, []
    for name, a in c.items():
        cols[name] = (at, a.shape[1])
        at += a.shape[1]
        parts.append(a.astype(np.float32))
    return np.concatenate(parts, 1), cols


CONST, COLS = const_tables()


HEAD_ORDER = [h * 8 + t for t in range(8) for h in range(2)]
SCHEDULE = [("ffn", 0, 0), ("cm",), ("ffn", 0, 1), ("ffn", 1, 0), ("swa",), ("ffn", 1, 1),
            ("ffn", 2, 0), ("sc",), ("ffn", 2, 1), ("ffn", 3, 0), ("nsa",), ("ffn", 3, 1)]
N_PAIR = PAGE // 2
CMP_BANK = 63 * 2 * 2


def program(nc, A, O, schedule):
    ctx = ExitStack()
    with ctx:
        def sem(name):
            return ctx.enter_context(nc.semaphore(name))

        kinds = {s[0] for s in schedule}
        BASE = (nc.sbuf_base + 63) // 64 * 64
        top = [0]

        def sb(name, shape, dt=F32):
            at = top[0]
            top[0] = (at + int(np.prod(shape[1:])) * 4 + 63) // 64 * 64
            assert BASE + top[0] <= nc.sbuf_usable_end, (name, top[0])
            return nc.alloc_sbuf_tensor_at(name, list(shape), dt, offset=BASE + at)

        raw = sb("w_raw", [P, RAW, KT, CW])
        w_hi = sb("w_hi", [P, HALVES, KT, P], F32R)
        w_lo = sb("w_lo", [P, HALVES, KT, P], F32R)
        x = sb("x", [P, KT, T])
        XH_AT = top[0]
        x_hi = sb("x_hi", [P, KT, T], F32R)
        XL_AT = top[0]
        x_lo = sb("x_lo", [P, KT, T], F32R)
        CONST_AT = top[0]
        const = sb("const", [P, CONST.shape[1]])
        gains = sb("gains", [P, 14, KT])
        ssum = sb("ssum", [P, T])
        sq = sb("sq", [P, T])
        std = sb("std", [P, T])
        rstd = sb("rstd", [P, T])
        gate_in = sb("gate_in", [P, 2, T])
        SILU_AT = top[0]
        silu = sb("silu", [P, 2, T])
        up = sb("up", [P, 2, T])
        HIN_AT = top[0]
        h = sb("h", [P, 2, T])
        kcmp_s = sb("kcmp_s", [P, NB, 64])
        pages = sb("page_table", [1, NB * NPAGES], I32)
        vcmp_s = sb("vcmp_s", [64, NB, P])
        cmp_bias = sb("cmp_bias", [P, 2, 2])
        w2z = sb("w2z", [P, 2, 2, 2, P])
        cmp_pe = sb("cmp_pe", [P, 2, 16])
        sc_w = sb("sc_w", [P, 3, KT])
        sc_prev = sb("sc_prev", [P, KT, 2 * NB])
        H_AT = top[0]
        h_hi = sb("h_hi", [P, FT, T], F32R)
        HL_AT = top[0]
        h_lo = sb("h_lo", [P, FT, T], F32R)
        END = top[0]
        bank = [ctx.enter_context(nc.psum_tensor(f"bank{i}", [P, 512], F32)) for i in range(8)]

        class Area:

            def __init__(self, whole=False):
                lo = 0 if whole else KT * T * 4
                self.free = [[END, nc.sbuf_usable_end - BASE], [H_AT + lo, HL_AT], [HL_AT + lo, END]]
                if whole:
                    self.free = [[H_AT, nc.sbuf_usable_end - BASE]]

            def __call__(self, name, shape, dt=F32):
                size = (int(np.prod(shape[1:])) * 4 + 63) // 64 * 64
                fit = [r for r in self.free if r[1] - r[0] >= size]
                assert fit, (name, size, self.free)
                r = min(fit, key=lambda r: r[1] - r[0])
                at = r[0]
                r[0] += size
                return nc.alloc_sbuf_tensor_at(name, list(shape), dt, offset=BASE + at)

        LIMIT = nc.sbuf_usable_end - BASE

        class Space:

            def __init__(self, at, end):
                self.at, self.end = at, end

            def __call__(self, name, shape, dt=F32):
                at = self.at
                self.at = (at + int(np.prod(shape[1:])) * 4 + 63) // 64 * 64
                assert self.at <= self.end, (name, self.at - self.end)
                return nc.alloc_sbuf_tensor_at(name, list(shape), dt, offset=BASE + at)

        silu_space, h_space = Space(SILU_AT, SILU_AT + 2 * T * 4), Space(HIN_AT, HIN_AT + 2 * T * 4)

        def cst(name):
            a, n = COLS[name]
            return const[:, a:a + n]

        const_landed = sem("const_landed")
        x_landed = sem("x_landed")
        raw_landed = [sem(f"raw_landed{s}") for s in range(RAW)]
        hi_ready = sem("hi_ready")
        lo_ready = sem("lo_ready")
        half_used = sem("half_used")
        evacuated = sem("evacuated")
        xhi_ready = sem("xhi_ready")
        xlo_ready = sem("xlo_ready")
        ssum_step = sem("ssum_step")
        stat_ready = sem("stat_ready")
        std_ready = sem("std_ready")
        rstd_ready = sem("rstd_ready")
        silu_ready = sem("silu_ready")
        prod_ready = sem("prod_ready")
        hhi_ready = sem("hhi_ready")
        hlo_ready = sem("hlo_ready")
        y_ready = sem("y_ready")
        stored = sem("stored")

        stages = []
        n_norm = n_ffn = g = n_chunks = 0

        def stage(kind, chunks, groups, **more):
            nonlocal g, n_chunks
            stages.append(dict(kind=kind, n0=n_chunks, g0=g, chunks=chunks, groups=groups, norm=n_norm, **more))
            n_chunks += chunks
            g += groups

        IN_CHUNKS = {"cm": 8, "swa": 5, "sc": 12, "nsa": 8}
        for s in schedule:
            if s[0] == "ffn":
                stage("ffn_in", FT, 2 * FT, ffn=n_ffn)
                n_norm += 1
                stage("ffn_out", 3 * KT // 2, KT, ffn=n_ffn)
                n_ffn += 1
            else:
                n_in = IN_CHUNKS[s[0]]
                stage(s[0] + "_in", n_in, 2 * n_in)
                n_norm += 1
                stage("mix_out", KT // 2, KT, mixer=s[0])
        final_norm = n_norm
        narrow = {st["n0"] + 7 for st in stages if st["kind"] == "nsa_in"}

        def landed(n):
            return 16 * (n // RAW + 1)

        def sp_chunk(sp, n, i=0, step=0, k=KT):
            if n >= RAW:
                sp.wait_ge(lo_ready, 2 * n - 2 * RAW + 2 + 2 * step * i)
            src = A["stream"][bass.ds(n + step * i, 1)] if step else A["stream"][n:n + 1]
            sp.dma_start(raw[:, n % RAW, 0:k, :].rearrange("p k n -> p (k n)"),
                         src.rearrange("a p n -> p (a n)")[:, 0:k * CW]).then_inc(raw_landed[n % RAW], 16)

        def sp_stream(sp, st):
            n0, chunks = st["n0"], st["chunks"]
            if st["kind"] == "ffn_out":
                with sp.Fori(0, 2) as i:
                    for c in range(6):
                        sp_chunk(sp, n0 + c, i, 6, k=(8, 8, 6)[c % 3])
                return
            peel = RAW if n0 == 0 else 0
            with sp.Fori(0, (chunks - peel) // 2) as i:
                for c in range(2):
                    sp_chunk(sp, n0 + peel + c, i, 2)
            if chunks % 2:
                sp_chunk(sp, n0 + chunks - 1)

        def act_split(act, n, i=0, step=0, k=KT):
            act.wait_ge(raw_landed[n % RAW], landed(n) + 16 * (step // RAW) * i)
            one = n in narrow and not step
            for half in range(1 if one else 2):
                if n >= RAW:
                    act.wait_ge(half_used, 2 * n + half + 1 - HALVES + 2 * step * i)
                act.activation(w_hi[:, (2 * n + half) % HALVES, 0:k, :],
                               raw[:, n % RAW, 0:k, P * half:P * half + P], ACT.Copy).then_inc(hi_ready, 2 if one else 1)

        def dve_split(dve, n, i=0, step=0, k=KT):
            one = n in narrow and not step
            for half in range(1 if one else 2):
                s = (2 * n + half) % HALVES
                dve.wait_ge(hi_ready, 2 * n + half + 1 + 2 * step * i)
                dve.tensor_tensor(w_lo[:, s, 0:k, :], raw[:, n % RAW, 0:k, P * half:P * half + P],
                                  w_hi[:, s, 0:k, :].bitcast(F32), ALU.subtract).then_inc(lo_ready, 2 if one else 1)

        def pe_half(pe, n, half, g, act_hi, act_lo, k0=0, k=KT, i=0, step=0, gstep=0, first=True, last=True,
                    operand=None):
            s = (2 * n + half) % HALVES
            acc = bank[g % BANKS][:, 0:T]
            pe.wait_ge(lo_ready, 2 * n + half + 1 + 2 * step * i)
            if first and g >= BANKS:
                pe.wait_ge(evacuated, g + 1 - BANKS + gstep * i)
            for kk in range(k):
                if operand:
                    operand(kk)
                for w, a in ((w_hi, act_hi), (w_lo, act_hi), (w_hi, act_lo)):
                    mm = pe.matmul(acc, w[:, s, kk, :], a[:, k0 + kk, :],
                                   start=(first and kk == 0 and w is w_hi and a is act_hi),
                                   stop=(last and kk == k - 1 and a is act_lo))
            return mm

        def pe_norm(pe, norm):
            pe.wait_ge(ssum_step, 17 * norm + 17)
            if norm:
                pe.wait_ge(std_ready, norm)
            pe.matmul(bank[4][:, 0:T], cst("ones"), ssum[:, :], start=True, stop=True).then_inc(stat_ready, 1)

        def pe_in(pe, st):
            n0, g0, norm = st["n0"], st["g0"], st["norm"]

            def chunk(c, i=0, operand=None):
                one = n0 + c in narrow
                for half in range(1 if one else 2):
                    n, g = n0 + c, g0 + 2 * c + half
                    mm = pe_half(pe, n, half, g, x_hi, x_lo, i=i, step=2, gstep=4, operand=operand if half == 0 else None)
                    mm.then_inc(half_used, 2 if one else 1)

            chunk(0, operand=lambda k: pe.wait_ge(xlo_ready, KT * norm + k + 1))
            pe_norm(pe, norm)
            chunk(1)
            full = (st["chunks"] - (n0 + st["chunks"] - 1 in narrow)) // 2
            with pe.Fori(1, full) as i:
                chunk(0, i)
                chunk(1, i)
            for c in range(2 * full, st["chunks"]):
                chunk(c)

        def pe_ffn_out(pe, st):
            n0, g0 = st["n0"], st["g0"]
            base = 2 + FT * st["ffn"]

            def body(i):
                for c in range(6):
                    k0, k = 8 * (c % 3), (8, 8, 6)[c % 3]
                    for half in range(2):
                        pe_half(pe, n0 + c, half, g0 + 2 * (c // 3) + half, h_hi, h_lo, k0, k, i=i, step=6, gstep=4,
                                first=c % 3 == 0, last=c % 3 == 2,
                                operand=(lambda kk, k0=k0: pe.wait_ge(hlo_ready, base + k0 + kk + 1)) if half == 0 else None)\
                            .then_inc(half_used, 1)

            with pe.Fori(0, 2) as i:
                body(i)

        def act_std(act, norm):
            act.wait_ge(stat_ready, norm + 1)
            if norm:
                act.wait_ge(rstd_ready, norm)
            act.activation(std[:, :], bank[4][:, 0:T], ACT.Sqrt, bias=cst("eps"), scale=1.0 / D).then_inc(std_ready, 1)

        def act_x_hi(act, norm, m):
            act.activation(x_hi[:, bass.ds(m, 1), :], x[:, bass.ds(m, 1), :], ACT.Copy,
                           scale=gains[:, norm, bass.ds(m, 1)]).then_inc(xhi_ready, 1)

        def act_ffn_in(act, st):
            n0, g0 = st["n0"], st["g0"]
            base = FT * st["ffn"]
            act_std(act, st["norm"])
            with act.Fori(0, FT // 2) as i:
                act_split(act, n0 + 2, i, 2)
                for f in range(2):
                    act.wait_ge(evacuated, g0 + f + 1 + 4 * i)
                    act.wait_ge(prod_ready, base + f + 1 + 2 * i)
                    act.activation(silu[:, f, :], gate_in[:, f, :], ACT.Silu).then_inc(silu_ready, 1)
                act_split(act, n0 + 3, i, 2)
                for f in range(2):
                    act.wait_ge(prod_ready, base + f + 3 + 2 * i)
                    act.activation(h_hi[:, bass.ds(2 * i + f, 1), :], h[:, f:f + 1, :], ACT.Copy).then_inc(hhi_ready, 1)

        def act_ffn_out(act, st):
            n0, g0, norm = st["n0"], st["g0"], st["norm"]
            final = norm == final_norm

            def body(i, c):
                if c % 3 == 2 and not final:
                    for f in range(2):
                        m = 2 * (c // 3) + f
                        act.wait_ge(evacuated, g0 + m + 1 + 4 * i)
                        act_x_hi(act, norm, m + 4 * i)
                if not final or n0 + c + RAW + 6 * i < n_chunks:
                    act_split(act, n0 + c + 2, i, 6, k=(8, 8, 6)[(c + 2) % 3])

            if final:
                for i in range(2):
                    for c in range(6):
                        body(i, c)
            else:
                with act.Fori(0, 2) as i:
                    for c in range(6):
                        body(i, c)

        def dve_rstd(dve, norm):
            dve.wait_ge(std_ready, norm + 1)
            dve.reciprocal(rstd[:, :], std[:, :]).then_inc(rstd_ready, 1)
            dve.wait_ge(rstd_ready, norm + 1)

        def dve_x_lo(dve, norm, m):
            dve.scalar_tensor_tensor(out=x_lo[:, bass.ds(m, 1), :], in0=x[:, bass.ds(m, 1), :],
                                     scalar=gains[:, norm, bass.ds(m, 1)], in1=x_hi[:, bass.ds(m, 1), :].bitcast(F32),
                                     op0=ALU.mult, op1=ALU.subtract).then_inc(xlo_ready, 1)

        def dve_take(dve, n, g, dst, i=0, step=0, gstep=0):
            dve.wait_ge(half_used, 2 * n + g % 2 + 1 + 2 * step * i)
            dve.tensor_tensor(dst, bank[g % BANKS][:, 0:T], rstd[:, :], ALU.mult).then_inc(evacuated, 1)

        def dve_ffn_in(dve, st):
            n0, g0 = st["n0"], st["g0"]
            base = FT * st["ffn"]
            dve_rstd(dve, st["norm"])
            with dve.Fori(0, FT // 2) as i:
                for f in range(2):
                    dve.wait_ge(silu_ready, base + f + 1 + 2 * i)
                    dve_take(dve, n0, g0 + f, gate_in[:, f, :], i, 2, 4)
                dve_split(dve, n0 + 2, i, 2)
                for f in range(2):
                    dve.wait_ge(prod_ready, base + f + 1 + 2 * i)
                    dve_take(dve, n0 + 1, g0 + 2 + f, up[:, f, :], i, 2, 4)
                dve_split(dve, n0 + 3, i, 2)

        def dve_add_x(dve, n, g, m, scale, i=0, step=0):
            dve.wait_ge(half_used, 2 * n + g % 2 + 1 + 2 * step * i)
            xm = x[:, bass.ds(m, 1), :]
            dve.scalar_tensor_tensor(out=xm, in0=bank[g % BANKS][:, 0:T].rearrange("p (a t) -> p a t", a=1),
                                     scalar=scale, in1=xm, op0=ALU.mult, op1=ALU.add).then_inc(evacuated, 1)

        def dve_ffn_out(dve, st):
            n0, g0, norm = st["n0"], st["g0"], st["norm"]
            final = norm == final_norm

            def body(i, c):
                if c % 3 == 2:
                    for f in range(2):
                        m = 2 * (c // 3) + f
                        dve_add_x(dve, n0 + c, g0 + m, m + 4 * i, 0.5, i, 6)
                    for f in range(2 * (not final)):
                        m = 2 * (c // 3) + f
                        dve.wait_ge(evacuated, g0 + m + 1 + 4 * i)
                        dve.wait_ge(xhi_ready, KT * norm + m + 1 + 4 * i)
                        dve_x_lo(dve, norm, m + 4 * i)
                if not final or n0 + c + RAW + 6 * i < n_chunks:
                    dve_split(dve, n0 + c + 2, i, 6, k=(8, 8, 6)[(c + 2) % 3])

            if final:
                for i in range(2):
                    for c in range(6):
                        body(i, c)
            else:
                with dve.Fori(0, 2) as i:
                    for c in range(6):
                        body(i, c)

        def pool_clear_ssum(pool, norm):
            if norm:
                pool.wait_ge(stat_ready, norm)
            pool.memset(ssum[:, :], 0.0).then_inc(ssum_step, 1)

        def pool_square(pool, norm, m):
            pool.wait_ge(ssum_step, 17 * norm + 1 + 2 * m)
            pool.tensor_tensor(sq[:, :].rearrange("p (a t) -> p a t", a=1), x[:, bass.ds(m, 1), :], x[:, bass.ds(m, 1), :],
                               ALU.mult).then_inc(ssum_step, 1)
            pool.wait_ge(ssum_step, 17 * norm + 2 + 2 * m)
            pool.tensor_tensor(ssum[:, :], ssum[:, :], sq[:, :], ALU.add).then_inc(ssum_step, 1)

        def pool_ffn_in(pool, st):
            g0 = st["g0"]
            base = FT * st["ffn"]
            with pool.Fori(0, FT // 2) as i:
                for f in range(2):
                    pool.wait_ge(evacuated, g0 + 2 + f + 1 + 4 * i)
                    pool.wait_ge(silu_ready, base + f + 3 + 2 * i)
                    pool.wait_ge(hlo_ready, base + f + 1 + 2 * i)
                    pool.tensor_tensor(h[:, f, :], silu[:, f, :], up[:, f, :], ALU.mult).then_inc(prod_ready, 1)
                for f in range(2):
                    pool.wait_ge(hhi_ready, base + f + 3 + 2 * i)
                    pool.wait_ge(prod_ready, base + f + 3 + 2 * i)
                    t = bass.ds(2 * i + f, 1)
                    pool.tensor_tensor(h_lo[:, t, :], h[:, f:f + 1, :], h_hi[:, t, :].bitcast(F32),
                                       ALU.subtract).then_inc(hlo_ready, 1)

        def pool_out(pool, st):
            g0, norm = st["g0"], st["norm"]
            pool_clear_ssum(pool, norm)
            with pool.Fori(0, KT) as m:
                pool.wait_ge(evacuated, g0 + 1 + m)
                pool_square(pool, norm, m)

        def act_x_in(act):
            act.wait_ge(const_landed, 32)
            act.wait_ge(x_landed, 16)
            for m in range(KT):
                act_x_hi(act, 0, m)

        def dve_x_in(dve):
            dve.wait_ge(const_landed, 32)
            dve.wait_ge(x_landed, 16)
            for m in range(KT):
                dve.wait_ge(xhi_ready, m + 1)
                dve_x_lo(dve, 0, m)

        def pool_x_in(pool):
            pool_clear_ssum(pool, 0)
            pool.wait_ge(x_landed, 16)
            for m in range(KT):
                pool_square(pool, 0, m)

        def pe_final(pe):
            pe.wait_ge(ssum_step, 17 * final_norm + 17)
            pe.wait_ge(std_ready, final_norm)
            pe.matmul(bank[4][:, 0:T], cst("ones"), ssum[:, :], start=True, stop=True).then_inc(stat_ready, 1)

        def dve_final(dve):
            dve_rstd(dve, final_norm)
            for m in range(KT):
                xm = x[:, m, :]
                dve.scalar_tensor_tensor(out=xm, in0=xm, scalar=gains[:, final_norm, m:m + 1], in1=rstd[:, :],
                                         op0=ALU.mult, op1=ALU.mult).then_inc(y_ready, 1)

        mixer_ready = sem("mixer_ready")
        n_mixer = 0
        for st in stages:
            st["mixer_base"] = KT * n_mixer
            n_mixer += st["kind"] == "mix_out"

        def pe_mix_out(pe, st):
            n0, g0 = st["n0"], st["g0"]

            def chunk(c, i=0, operand=None):
                for half in range(2):
                    pe_half(pe, n0 + c, half, g0 + 2 * c + half, h_hi, h_lo, i=i, step=2, gstep=4,
                            operand=operand if half == 0 else None).then_inc(half_used, 1)

            chunk(0, operand=lambda k: pe.wait_ge(mixer_ready, st["mixer_base"] + k + 1))
            chunk(1)
            with pe.Fori(1, 2) as i:
                chunk(0, i)
                chunk(1, i)

        def act_mix_out(act, st):
            n0, g0, norm = st["n0"], st["g0"], st["norm"]
            for c in range(KT // 2):
                for f in range(2):
                    m = 2 * c + f
                    act.wait_ge(evacuated, g0 + m + 1)
                    act_x_hi(act, norm, m)
                if n0 + c + RAW < n_chunks:
                    act_split(act, n0 + c + RAW)

        def dve_mix_out(dve, st):
            n0, g0, norm = st["n0"], st["g0"], st["norm"]
            for c in range(KT // 2):
                for f in range(2):
                    m = 2 * c + f
                    dve_add_x(dve, n0 + c, g0 + m, m, 1.0)
                for f in range(2):
                    m = 2 * c + f
                    dve.wait_ge(evacuated, g0 + m + 1)
                    dve.wait_ge(xhi_ready, KT * norm + m + 1)
                    dve_x_lo(dve, norm, m)
                if n0 + c + RAW < n_chunks:
                    dve_split(dve, n0 + c + RAW)


        if "cm" in kinds:
            area = Area()
            cm_u = area("cm_u", [P, KT, T])
            cm_v = area("cm_v", [P, KT, T])
            cm_vt = area("cm_vt", [P, 3, D])
            cm_ws = area("cm_ws", [P, 4, P])
            cm_ws_s = area("cm_ws_s", [NS_TOK, 4, NS_TOK])
            cm_bs = area("cm_bs", [1, 4, T])
            vsum = area("vsum", [P, T])
            vsq = area("vsq", [P, T])
            vstd = area("vstd", [P, T])
            vrstd = area("vrstd", [P, T])
            cm_landed = sem("cm_landed")
            gelu_ready = sem("gelu_ready")
            vsum_step = sem("vsum_step")
            vstat_ready = sem("vstat_ready")
            vstd_ready = sem("vstd_ready")
            vrstd_ready = sem("vrstd_ready")
            ws_ready = sem("ws_ready")
            vn_ready = sem("vn_ready")
            vt_turned = sem("vt_turned")
            vt_copied = sem("vt_copied")
            mixed_ready = sem("mixed_ready")
            cy_ready = sem("cy_ready")
            cy_hi = sem("cy_hi")
            cm_banks = [7, 4]

        def sp_cm_load(sp):
            sp.wait_ge(evacuated, cm_st["g0"])
            for dst, name in ((cm_ws, "ws_t"), (cm_ws_s, "ws_s_t"), (cm_bs, "bs")):
                sp.dma_start(dst[:, :, :], A[name]).then_inc(cm_landed, 16)

        def sp_cm_store(sp):
            sp.wait_ge(vn_ready, KT)
            sp.dma_start(O["cm_v"], cm_v[:, :, NP_TOK:T]).then_inc(mix_stored["cm"], 16)

        def act_cm_in(act, st):
            n0, g0 = st["n0"], st["g0"]
            act_std(act, st["norm"])
            for part, dst in enumerate((cm_u, cm_v)):
                with act.Fori(0, 2) as i:
                    for c in range(2):
                        act_split(act, n0 + RAW + 4 * part + c, i, 2)
                        for f in range(2):
                            q = 8 * part + 2 * c + f
                            act.wait_ge(evacuated, g0 + q + 1 + 4 * i)
                            act.activation(dst[:, bass.ds(2 * c + f + 4 * i, 1), :], gate_in[:, f:f + 1, :],
                                           ACT.Gelu_apprx_tanh).then_inc(gelu_ready, 1)
            act.wait_ge(vstat_ready, 1)
            act.activation(vstd[:, :], bank[4][:, 0:T], ACT.Sqrt, bias=cst("eps"), scale=1.0 / D).then_inc(vstd_ready, 1)
            for m in range(KT):
                act.wait_ge(vt_turned, m + 1)
                src = bank[5 + m % 2]
                act.activation(cm_vt[:, 0:2, P * m:P * m + P], src[:, 0:2 * P].rearrange("p (c f) -> p c f", c=2), ACT.Copy)
                act.activation(cm_vt[0:NS_TOK, 2, P * m:P * m + P], src[0:NS_TOK, 2 * P:3 * P], ACT.Copy)\
                    .then_inc(vt_copied, 1)
            for m in range(KT):
                act.wait_ge(cy_ready, m + 1)
                act.activation(h_hi[:, m, :], up[:, m % 2, :], ACT.Copy).then_inc(cy_hi, 1)

        def dve_cm_in(dve, st):
            n0, g0 = st["n0"], st["g0"]
            dve_rstd(dve, st["norm"])
            for part in range(2):
                with dve.Fori(0, 2) as i:
                    for c in range(2):
                        for f in range(2):
                            q = 8 * part + 2 * c + f
                            dve.wait_ge(gelu_ready, q + 1 + 4 * i)
                            dve_take(dve, n0 + 4 * part + c, g0 + q, gate_in[:, f, :], i, 2, 4)
                        dve_split(dve, n0 + RAW + 4 * part + c, i, 2)
            dve.wait_ge(cm_landed, 48)
            dve.tensor_tensor(cm_ws[:, :, :], cm_ws[:, :, :],
                              cst("tri").rearrange("p (a j) -> p a j", a=1).broadcast_to([P, 4, P]), ALU.mult)\
                .then_inc(ws_ready, 1)
            dve.tensor_tensor(cm_ws_s[:, :, :], cm_ws_s[:, :, :],
                              cst("tri")[0:NS_TOK, 0:NS_TOK].rearrange("p (a j) -> p a j", a=1).broadcast_to([NS_TOK, 4, NS_TOK]),
                              ALU.mult).then_inc(ws_ready, 1)
            dve.wait_ge(vstd_ready, 1)
            dve.reciprocal(vrstd[:, :], vstd[:, :]).then_inc(vrstd_ready, 1)
            dve.wait_ge(vrstd_ready, 1)
            for m in range(KT):
                vm = cm_v[:, m, :]
                dve.scalar_tensor_tensor(out=vm, in0=vm, scalar=gains[:, 13, m:m + 1], in1=vrstd[:, :],
                                         op0=ALU.mult, op1=ALU.mult).then_inc(vn_ready, 1)
            for m in range(KT):
                dve.wait_ge(mixed_ready, m + 1)
                if m >= 2:
                    dve.wait_ge(cy_hi, m - 1)
                dve.tensor_tensor(up[:, m % 2, :], bank[cm_banks[m % 2]][:, 0:T], cm_u[:, m, :], ALU.mult).then_inc(cy_ready, 1)
                dve.wait_ge(cy_ready, m + 1)
                dve.wait_ge(cy_hi, m + 1)
                dve.tensor_tensor(h_lo[:, m, :], up[:, m % 2, :], h_hi[:, m, :].bitcast(F32), ALU.subtract)\
                    .then_inc(mixer_ready, 1)

        def pool_cm_in(pool, st):
            pool.wait_ge(evacuated, st["g0"])
            pool.memset(vsum[:, :], 0.0).then_inc(vsum_step, 1)
            with pool.Fori(0, KT) as m:
                pool.wait_ge(gelu_ready, 2 + 8 + 1 + m)
                pool.wait_ge(vsum_step, 1 + 2 * m)
                vm = cm_v[:, bass.ds(m, 1), :]
                pool.tensor_tensor(vsq[:, :].rearrange("p (a t) -> p a t", a=1), vm, vm, ALU.mult).then_inc(vsum_step, 1)
                pool.wait_ge(vsum_step, 2 + 2 * m)
                pool.tensor_tensor(vsum[:, :], vsum[:, :], vsq[:, :], ALU.add).then_inc(vsum_step, 1)

        def pe_cm(pe, st):
            pe_in(pe, st)
            pe.wait_ge(vsum_step, 17)
            pe.matmul(bank[4][:, 0:T], cst("ones"), vsum[:, :], start=True, stop=True).then_inc(vstat_ready, 1)
            for m in range(KT):
                pe.wait_ge(vn_ready, m + 1)
                if m >= 2:
                    pe.wait_ge(vt_copied, m - 1)
                for c in range(3):
                    w = P if c < 2 else NS_TOK
                    t = pe.transpose(bank[5 + m % 2][0:w, P * c:P * c + P], cm_v[:, m, P * c:P * c + w], cst("ident"))
                t.then_inc(vt_turned, 1)
            pe.wait_ge(ws_ready, 2)
            pe.wait_ge(evacuated, st["g0"] + st["groups"])
            for m in range(KT):
                pe.wait_ge(vt_copied, m + 1)
                if m >= 2:
                    pe.wait_ge(cy_ready, m - 1)
                grp, out = m // 2, bank[cm_banks[m % 2]]
                pe.matmul(out[:, 0:T], cst("ones")[0:1, :], cm_bs[0:1, grp, :], start=True, stop=False)
                for c in range(2):
                    pe.matmul(out[:, P * c:P * c + P], cm_vt[:, c, P * m:P * m + P], cm_ws[:, grp, :], start=False, stop=False)
                pe.matmul(out[:, 2 * P:T], cm_vt[0:NS_TOK, 2, P * m:P * m + P], cm_ws_s[:, grp, :],
                          start=False, stop=True).then_inc(mixed_ready, 1)

        Z_COLS = 2 + NP_TOK + NB * (NQ + 2)
        if "sc" in kinds:
            area = Area()
            sc_b = area("sc_b", [P, KT, T])
            sc_z = area("sc_z", [P, KT, Z_COLS])
            sc_c = area("sc_c", [P, 2, T])
            sc_h = area("sc_h", [P, 2, T])
            sc_cv = area("sc_cv", [P, 2, Z_COLS])
            sc_y = area("sc_y", [P, 2, T])
            sc_end = area("sc_end", [P, KT, 2 + 2 * NB])
            sc_landed = sem("sc_landed")
            z_step = sem("z_step")
            Z0 = 16
            sc_hi = sem("sc_hi")
            sc_kept = sem("sc_kept")

        def sp_sc_load(sp):
            sp.dma_start(sc_w[:, :, :], A["conv_w"]).then_inc(sc_landed, 16)
            sp.dma_start(sc_prev[:, :, :], A["conv_prev"]).then_inc(sc_landed, 16)

        def sp_sc_store(sp):
            sp.wait_ge(sc_kept, 2)
            sp.dma_start(O["conv_end"], sc_end[:, :, :]).then_inc(mix_stored["sc"], 16)

        def act_sc_in(act, st):
            n0 = st["n0"]
            act_std(act, st["norm"])
            with act.Fori(0, 2) as i:
                for c in range(6):
                    act_split(act, n0 + RAW + c, i, 6)
                    if c % 3 == 2:
                        for f in range(2):
                            m = 2 * (c // 3) + f
                            act.wait_ge(z_step, Z0 + 7 * m + 7 + 28 * i)
                            act.activation(h_hi[:, bass.ds(m + 4 * i, 1), :], sc_y[:, f:f + 1, :], ACT.Copy).then_inc(sc_hi, 1)

        def dve_sc_in(dve, st):
            n0, g0 = st["n0"], st["g0"]
            dve_rstd(dve, st["norm"])
            with dve.Fori(0, 2) as i:
                for c in range(6):
                    for f in range(2):
                        m = 2 * (c // 3) + f
                        if c % 3:
                            dve.wait_ge(z_step, Z0 + 7 * (m - 2) + 2 + 28 * i)
                        dst = (sc_b[:, bass.ds(m + 4 * i, 1), :], sc_c[:, f:f + 1, :], sc_h[:, f:f + 1, :])[c % 3]
                        g = g0 + 2 * c + f
                        dve.wait_ge(half_used, 2 * (n0 + c) + f + 1 + 12 * i)
                        dve.tensor_tensor(dst, bank[g % BANKS][:, 0:T].rearrange("p (a t) -> p a t", a=1),
                                          rstd[:, :].rearrange("p (a t) -> p a t", a=1), ALU.mult).then_inc(evacuated, 1)
                    dve_split(dve, n0 + RAW + c, i, 6)
                    for f in range(2 * (c % 3 == 2)):
                        m = 2 * (c // 3) + f
                        at = Z0 + 7 * m + 28 * i
                        mi = bass.ds(m + 4 * i, 1)
                        cv = sc_cv[:, f, 0:Z_COLS - 2]
                        for k in range(3):
                            dve.wait_ge(z_step, at + 2 + k)
                            zk = sc_z[:, mi, k:k + Z_COLS - 2].rearrange("p a n -> p (a n)")
                            if k == 0:
                                op = dve.tensor_scalar(cv, zk, sc_w[:, 0, mi], None, ALU.mult)
                            else:
                                op = dve.scalar_tensor_tensor(out=cv, in0=zk, scalar=sc_w[:, k, mi], in1=cv,
                                                              op0=ALU.mult, op1=ALU.add)
                            op.then_inc(z_step, 1)
            dve.wait_ge(z_step, Z0 + 7 * KT)
            dve.tensor_copy(sc_end[:, :, 0:2], sc_z[:, :, NP_TOK:NP_TOK + 2]).then_inc(sc_kept, 1)
            dve.tensor_copy(sc_end[:, :, 2:].rearrange("p m (b s) -> p m b s", s=2),
                            sc_z[:, :, 2 + NP_TOK:].rearrange("p m (b s) -> p m b s", s=NQ + 2)[:, :, :, NQ:NQ + 2])\
                .then_inc(sc_kept, 1)

        def pool_sc_in(pool, st):
            g0 = st["g0"]
            pool.wait_ge(sc_landed, 32)
            pool.memset(sc_z[:, :, 0:2], 0.0).then_inc(z_step, Z0 - 1)
            pool.tensor_copy(sc_z[:, :, 2 + NP_TOK:].rearrange("p m (b s) -> p m b s", s=NQ + 2)[:, :, :, 0:2],
                             sc_prev[:, :, :].rearrange("p m (b s) -> p m b s", s=2)).then_inc(z_step, 1)
            with pool.Fori(0, 2) as i:
                for mm in range(4):
                    j, f = mm // 2, mm % 2
                    m = bass.ds(mm + 4 * i, 1)
                    at = Z0 + 7 * mm + 28 * i
                    z = sc_z[:, m, :].rearrange("p a n -> p (a n)")
                    cv = sc_cv[:, f, :]
                    zs = sc_z[:, m, 2 + NP_TOK:].rearrange("p a (b s) -> p (a b) s", s=NQ + 2)
                    cs = sc_c[:, f, NP_TOK:].rearrange("p (b s) -> p b s", s=NQ)
                    hs = sc_h[:, f, NP_TOK:].rearrange("p (b s) -> p b s", s=NQ)
                    pool.wait_ge(evacuated, g0 + 6 * j + 5 + f + 12 * i)
                    pool.wait_ge(z_step, at)
                    pool.wait_ge(mixer_ready, st["mixer_base"] + mm + 4 * i)
                    pool.tensor_tensor(z[:, 2:2 + NP_TOK], sc_c[:, f, 0:NP_TOK], sc_h[:, f, 0:NP_TOK], ALU.mult).then_inc(z_step, 1)
                    pool.tensor_tensor(zs[:, :, 2:NQ + 2], cs, hs, ALU.mult).then_inc(z_step, 1)
                    pool.wait_ge(z_step, at + 5)
                    b = sc_b[:, m, :].rearrange("p a t -> p (a t)")
                    pool.tensor_tensor(sc_y[:, f, 0:NP_TOK], b[:, 0:NP_TOK], cv[:, 0:NP_TOK], ALU.mult).then_inc(z_step, 1)
                    pool.tensor_tensor(sc_y[:, f, NP_TOK:].rearrange("p (b s) -> p b s", s=NQ),
                                       b[:, NP_TOK:].rearrange("p (b s) -> p b s", s=NQ),
                                       cv[:, NP_TOK + 2:].rearrange("p (b s) -> p b s", s=NQ + 2)[:, :, 0:NQ],
                                       ALU.mult).then_inc(z_step, 1)
                    pool.wait_ge(sc_hi, mm + 1 + 4 * i)
                    pool.wait_ge(z_step, at + 7)
                    pool.tensor_tensor(h_lo[:, m, :], sc_y[:, f:f + 1, :], h_hi[:, m, :].bitcast(F32), ALU.subtract)\
                        .then_inc(mixer_ready, 1)
        act_primed, dve_primed, pool_primed, pe_primed = [], [], [], []

        if kinds & {"swa", "nsa"}:
            rot_turned = sem("rot_turned")
            rot_sin = sem("rot_sin")
            rot_cos = sem("rot_cos")
            rope_ready = sem("rope_ready")
            rot_s, rot_c = gate_in, up
        n_rope = 0
        for st in stages:
            st["rope"] = n_rope
            n_rope += {"swa_in": 9, "nsa_in": 10}.get(st["kind"], 0)

        def rope_tiles(engine, st, tile, src, singles):
            with engine.Fori(0, KT // 2) as j:
                for f in range(2):
                    t = bass.ds(2 * j + f, 1)
                    tile(st["rope"] + f + 2 * j, f, src[:, t, :])
            for k, one in enumerate(singles):
                tile(st["rope"] + KT + k, k % 2, one)

        def flat(a):
            return a.rearrange("p a t -> p (a t)")

        def pe_rope(pe, st, src, singles):
            def tile(r, f, s):
                pe.wait_ge(rot_sin, r + 1)
                pe.matmul(bank[5 + f][:, 0:T], cst("perm"), flat(s), start=True, stop=True).then_inc(rot_turned, 1)
            pe.wait_ge(evacuated, st["g0"] + st["groups"])
            rope_tiles(pe, st, tile, src, singles)

        def dve_rope(dve, st, src, singles):
            def tile(r, f, s):
                dve.wait_ge(rot_turned, r + 1)
                dve.wait_ge(rope_ready, r + 1)
                dve.tensor_tensor(rot_s[:, f, :], bank[5 + f][:, 0:T], cst("sin"), ALU.mult).then_inc(rot_sin, 1)
            rope_tiles(dve, st, tile, src, singles)

        def pool_rope(pool, st, src, dst, singles):
            def tile(r, f, s, t):
                pool.wait_ge(rope_ready, r + 2)
                pool.tensor_tensor(rot_c[:, f, :], flat(s), cst("cos"), ALU.mult).then_inc(rot_cos, 1)
                pool.wait_ge(rot_cos, r + 1)
                pool.wait_ge(rot_sin, r + 3)
                pool.tensor_tensor(flat(dst[:, t:t + 1, :] if t is not None else s), rot_c[:, f, :], rot_s[:, f, :], ALU.add).then_inc(rope_ready, 1)
            pool.wait_ge(evacuated, st["g0"] + st["groups"])
            for t in range(KT):
                tile(st["rope"] + t, t % 2, src[:, t:t + 1, :], t)
            for k, one in enumerate(singles):
                tile(st["rope"] + KT + k, k % 2, one, None)

        def dve_take3(dve, n, half, g, dst, i=0, step=0, gstep=0, count=1):
            dve.wait_ge(half_used, 2 * n + half + 1 + 2 * step * i)
            dve.tensor_tensor(dst, bank[g % BANKS][:, 0:T].rearrange("p (a t) -> p a t", a=1),
                              rstd[:, :].rearrange("p (a t) -> p a t", a=1), ALU.mult).then_inc(evacuated, count)

        def act_splits(act, st, loop):
            n0 = st["n0"]
            act_std(act, st["norm"])
            with act.Fori(0, loop) as i:
                for c in range(2):
                    act_split(act, n0 + RAW + c, i, 2)
            for c in range(2 * loop, st["chunks"]):
                act_split(act, n0 + RAW + c)

        def queries(q, t, rows, grp=None):
            return q[:, bass.ds(t, 1), rows].rearrange("p a t -> p (a t)")

        def sample_rows(q, grp, b):
            return q[HD * grp:HD * grp + HD, 0:KT, bass.ds(NP_TOK + NQ * b, NQ)]

        def sample_queries(q, b):
            return q[:, 0:KT, bass.ds(NP_TOK + NQ * b, NQ)].rearrange("p (g t) s -> p g t s", g=1).broadcast_to([P, 2, KT, NQ])

        if "swa" in kinds:
            area = Area()
            at_q = area("at_q", [P, KT, T])
            at_kv = area("at_kv", [P, 2, T])
            at_kbd = area("at_kbd", [P, 2, 2, P])
            at_vbd = area("at_vbd", [P, 2, 2, P])
            at_vs = area("at_vs", [NS_TOK, P])
            at_kc = area("at_kc", [P, NB, P])
            at_vc = area("at_vc", [P, NB, P])
            at_qst = area("at_qst", [P, 2, P])
            at_vst = area("at_vst", [P, 2, P])
            at_p = area("at_p", [P, 2, 512])
            at_pt = area("at_pt", [P, 2, 512])
            at_mx = area("at_mx", [P, 2, 2])
            at_neg = area("at_neg", [P, 2, 2])
            at_esk = area("at_esk", [P, 2, 2])
            at_es = area("at_es", [P, 2, 2])
            at_sum = area("at_sum", [P, 2, 2])
            at_rec = area("at_rec", [P, 2, 2])
            at_sink = area("at_sink", [P, 17])
            at_sink8 = area("at_sink8", [P, 17])
            swa_landed = sem("swa_landed")
            swa_passed = sem("swa_passed")
            kbd_ready = sem("kbd_ready")
            v_turned = sem("v_turned")
            vbd_ready = sem("vbd_ready")
            sink_ready = sem("sink_ready")
            q_staged = sem("q_staged")
            s_ready = sem("s_ready")
            masked = sem("masked")
            at_step = sem("at_step")
            neg_ready = sem("neg_ready")
            exp_ready = sem("exp_ready")
            p_ready = sem("p_ready")
            pt_turned = sem("pt_turned")
            pt_copied = sem("pt_copied")
            o_ready = sem("o_ready")
            o_hi = sem("o_hi")
            o_lo = sem("o_lo")
            pool_primed += [q_staged]
            pe_primed += [s_ready, pt_turned, o_ready]
            dve_primed += [masked, neg_ready, p_ready, o_lo]
            act_primed += [exp_ready, pt_copied, o_hi]

        def swa_units(engine, unit_lists):
            for c in (0, 1, None):
                with engine.Fori(0, 4) as i:
                    for step in unit_lists:
                        for u in range(2):
                            base = PRIME + (16 if c is None else 8 * c)
                            step(base + u + 1 + 2 * i, u, c, 2 * i + u)

        def sp_swa_load(sp):
            sp.wait_ge(evacuated, swa_st["g0"])
            for dst, name in ((at_kc, "swa_k"), (at_vc, "swa_v")):
                sp.dma_start(dst[:, :, :], A[name]).then_inc(swa_landed, 16)
            sp.dma_start(at_sink[:, :], A["sinks"]).then_inc(swa_landed, 16)
            sp.dma_start(O["swa_passed"], A["swa_old"][:, NQ:P, :]).then_inc(swa_passed, 16)

        def sp_swa_store(sp):
            sp.wait_ge(rope_ready, 2 + swa_st["rope"] + 9)
            sp.dma_start(O["swa_kv"], at_kv[:, :, :]).then_inc(mix_stored["swa"], 16)

        def pe_swa(pe, st):
            pe_in(pe, st)
            pe_rope(pe, st, at_q, [at_kv[:, 0:1, :]])
            for c in range(3):
                w = P if c < 2 else NS_TOK
                tr = pe.transpose(bank[7][0:w, P * c:P * c + P], at_kv[:, 1, P * c:P * c + w], cst("ident"))
            tr.then_inc(v_turned, 1)
            pe.wait_ge(kbd_ready, 5)
            pe.wait_ge(swa_landed, 48)

            def scores(V, u, c, t):
                pe.wait_ge(q_staged, V)
                pe.wait_ge(masked, V - 2)
                if c is not None:
                    n = 2 * P * (c + 1)
                    pe.matmul(bank[u][:, 0:n], at_qst[:, u, :], at_kbd[:, 0:c + 1, :, :], start=True, stop=True)\
                        .then_inc(s_ready, 1)
                else:
                    pe.matmul(bank[u][:, 0:P], at_qst[:, u, :], at_kc[:, bass.ds(t, 1), :].rearrange("p a t -> p (a t)"),
                              start=True, stop=True)
                    pe.matmul(bank[u][:, P:P + NS_TOK], at_qst[:, u, :], at_kv[:, 0, NP_TOK:T], start=True, stop=True)\
                        .then_inc(s_ready, 1)

            def turn(V, u, c, t):
                pe.wait_ge(p_ready, V)
                pe.wait_ge(pt_copied, V - 2)
                if c is not None:
                    for k in range(2 * (c + 1)):
                        tr = pe.transpose(bank[2 + u][:, P * k:P * k + P], at_p[:, u, P * k:P * k + P], cst("ident"))
                else:
                    pe.transpose(bank[2 + u][:, 0:P], at_p[:, u, 0:P], cst("ident"))
                    tr = pe.transpose(bank[2 + u][0:NS_TOK, P:2 * P], at_p[:, u, P:P + NS_TOK], cst("ident"))
                tr.then_inc(pt_turned, 1)

            def values(V, u, c, t):
                pe.wait_ge(pt_copied, V)
                pe.wait_ge(o_lo, V - 2)
                out = bank[4 + u][:, 0:P]
                if c is not None:
                    for k in range(2 * (c + 1)):
                        mm = pe.matmul(out, at_vbd[:, k // 2, k % 2, :], at_pt[:, u, P * k:P * k + P],
                                       start=(k == 0), stop=(k == 2 * c + 1))
                else:
                    pe.matmul(out, at_vst[:, u, :], at_pt[:, u, 0:P], start=True, stop=False)
                    mm = pe.matmul(out, at_vs[:, :], at_pt[0:NS_TOK, u, P:2 * P], start=False, stop=True)
                mm.then_inc(o_ready, 1)

            pe.wait_ge(vbd_ready, 3)
            swa_units(pe, (scores, turn, values))

        def act_swa(act, st):
            act_splits(act, st, 2)
            act.wait_ge(v_turned, 1)
            act.wait_ge(kbd_ready, 3)
            vt = bank[7][:, 0:2 * P].rearrange("p (c g d) -> p c g d", c=2, g=2)
            for grp in range(2):
                act.activation(at_vbd[:, :, grp, HD * grp:HD * grp + HD], vt[:, :, grp, :], ACT.Copy).then_inc(vbd_ready, 1)
            act.activation(at_vs[:, :], bank[7][0:NS_TOK, 2 * P:3 * P], ACT.Copy).then_inc(vbd_ready, 1)

            def exps(V, u, c, t):
                act.wait_ge(neg_ready, V)
                if c is not None:
                    n = c + 1
                    pg = at_p[:, u, 0:2 * P * n].rearrange("p (k g j) -> p k g j", g=2, j=P)
                    for grp in range(2):
                        act.activation(pg[:, :, grp, :], pg[:, :, grp, :], ACT.Exp, bias=at_neg[:, u, grp:grp + 1],
                                       scale=SCALE, accum_out=at_sum[:, u, grp:grp + 1])
                    act.activation(at_es[:, u, :], at_esk[:, u, :], ACT.Exp, scale=SCALE).then_inc(exp_ready, 1)
                else:
                    pg = at_p[:, u, 0:P + NS_TOK]
                    act.activation(pg, pg, ACT.Exp, bias=at_neg[:, u, 0:1], scale=SCALE, accum_out=at_sum[:, u, 0:1])
                    act.activation(at_es[:, u, 0:1], at_esk[:, u, 0:1], ACT.Exp, scale=SCALE).then_inc(exp_ready, 1)

            def copies(V, u, c, t):
                act.wait_ge(pt_turned, V)
                act.wait_ge(o_ready, V - 2)
                if c is not None:
                    n = 2 * P * (c + 1)
                    act.activation(at_pt[:, u, 0:n], bank[2 + u][:, 0:n], ACT.Copy).then_inc(pt_copied, 1)
                else:
                    act.activation(at_pt[:, u, 0:P], bank[2 + u][:, 0:P], ACT.Copy)
                    act.activation(at_pt[0:NS_TOK, u, P:2 * P], bank[2 + u][0:NS_TOK, P:2 * P], ACT.Copy).then_inc(pt_copied, 1)

            def outs(V, u, c, t):
                act.wait_ge(o_ready, V)
                if c is not None:
                    act.activation(queries(h_hi, t, slice(P * c, P * c + P)), bank[4 + u][:, 0:P], ACT.Copy).then_inc(o_hi, 1)
                else:
                    for grp in range(2):
                        o = act.activation(sample_rows(h_hi, grp, t),
                                           bank[4 + u][HD * grp:HD * grp + HD, HD * grp:HD * grp + HD]
                                           .rearrange("p (t s) -> p t s", s=NQ), ACT.Copy)
                    o.then_inc(o_hi, 1)

            swa_units(act, (exps, copies, outs))

        def dve_swa(dve, st):
            n0, g0 = st["n0"], st["g0"]
            dve_rstd(dve, st["norm"])
            with dve.Fori(0, 2) as i:
                for c in range(2):
                    for f in range(2):
                        dve_take3(dve, n0 + c, f, g0 + 2 * c + f, at_q[:, bass.ds(2 * c + f + 4 * i, 1), :], i, 2, 4)
                    dve_split(dve, n0 + RAW + c, i, 2)
            for f in range(2):
                dve_take3(dve, n0 + 4, f, g0 + 8 + f, at_kv[:, f:f + 1, :])
            dve_split(dve, n0 + RAW + 4)
            dve_rope(dve, st, at_q, [at_kv[:, 0:1, :]])
            dve.wait_ge(swa_landed, 48)
            dve.tensor_scalar(at_sink8[:, :], at_sink[:, :], 1.0 / SCALE, None, ALU.mult).then_inc(sink_ready, 1)
            dve.wait_ge(sink_ready, 1)

            def mask(V, u, c, t):
                dve.wait_ge(s_ready, V)
                dve.wait_ge(pt_turned, V - 2)
                if c is not None:
                    n = 2 * P * (c + 1)
                    dve.tensor_tensor(at_p[:, u, 0:n], bank[u][:, 0:n], cst("m_band")[:, 0 if c else 2 * P:4 * P], ALU.add).then_inc(masked, 1)
                else:
                    dve.tensor_tensor(at_p[:, u, 0:P], bank[u][:, 0:P], cst("m_old"), ALU.add)
                    m = cst("m_new").rearrange("p (b k) -> p b k", b=NB)[:, bass.ds(t, 1), :].rearrange("p b k -> p (b k)")
                    dve.tensor_tensor(at_p[:, u, P:P + NS_TOK], bank[u][:, P:P + NS_TOK], m, ALU.add).then_inc(masked, 1)

            def unit(V):
                return 5 * (V - PRIME - 1)

            def sink_of(c, t):
                if c is None:
                    return at_sink8[:, 16:17]
                return at_sink8[:, 0:16].rearrange("p (g t) -> p g t", g=2)[:, :, bass.ds(t, 1)].rearrange("p g t -> p (g t)")

            def maxima(V, u, c, t):
                w = 1 if c is None else 2
                at = unit(V - u) + u
                dve.wait_ge(masked, V)
                if c is None:
                    dve.tensor_reduce(at_mx[:, u, 0:1], at_p[:, u, 0:P + NS_TOK], AX.X, ALU.max).then_inc(at_step, 1)
                else:
                    pg = at_p[:, u, 0:2 * P * (c + 1)].rearrange("p (k g j) -> p g k j", g=2, j=P)
                    dve.tensor_reduce(at_mx[:, u, :], pg, AX.XY, ALU.max).then_inc(at_step, 1)

            def with_sink(V, u, c, t):
                w = 1 if c is None else 2
                dve.wait_ge(at_step, unit(V - u) + u + 1)
                dve.tensor_tensor(at_mx[:, u, 0:w], at_mx[:, u, 0:w], sink_of(c, t), ALU.max).then_inc(at_step, 1)

            def sink_left(V, u, c, t):
                w = 1 if c is None else 2
                dve.wait_ge(at_step, unit(V - u) + 2 + u + 1)
                dve.tensor_tensor(at_esk[:, u, 0:w], sink_of(c, t), at_mx[:, u, 0:w], ALU.subtract).then_inc(at_step, 1)

            def negate(V, u, c, t):
                w = 1 if c is None else 2
                dve.tensor_scalar(at_neg[:, u, 0:w], at_mx[:, u, 0:w], -SCALE, None, ALU.mult).then_inc(neg_ready, 1)

            def total(V, u, c, t):
                w = 1 if c is None else 2
                dve.wait_ge(exp_ready, V)
                dve.tensor_tensor(at_sum[:, u, 0:w], at_sum[:, u, 0:w], at_es[:, u, 0:w], ALU.add).then_inc(at_step, 1)

            def inverse(V, u, c, t):
                w = 1 if c is None else 2
                dve.wait_ge(at_step, unit(V - u) + 6 + u + 1)
                dve.reciprocal(at_rec[:, u, 0:w], at_sum[:, u, 0:w]).then_inc(at_step, 1)

            def scale(V, u, c, t):
                dve.wait_ge(at_step, unit(V - u) + 8 + u + 1)
                if c is None:
                    pg = at_p[:, u, 0:P + NS_TOK]
                    dve.tensor_scalar(pg, pg, at_rec[:, u, 0:1], None, ALU.mult).then_inc(p_ready, 1)
                else:
                    pg = at_p[:, u, 0:2 * P * (c + 1)].rearrange("p (k g j) -> p k g j", g=2, j=P)
                    for grp in range(2):
                        o = dve.tensor_scalar(pg[:, :, grp, :], pg[:, :, grp, :], at_rec[:, u, grp:grp + 1], None, ALU.mult)
                    o.then_inc(p_ready, 1)

            def remainder(V, u, c, t):
                dve.wait_ge(o_hi, V)
                if c is not None:
                    rows = slice(P * c, P * c + P)
                    dve.tensor_tensor(queries(h_lo, t, rows), bank[4 + u][:, 0:P], queries(h_hi, t, rows).bitcast(F32),
                                      ALU.subtract).then_inc(o_lo, 1)
                else:
                    for grp in range(2):
                        o = dve.tensor_tensor(sample_rows(h_lo, grp, t),
                                              bank[4 + u][HD * grp:HD * grp + HD, HD * grp:HD * grp + HD]
                                              .rearrange("p (t s) -> p t s", s=NQ),
                                              sample_rows(h_hi, grp, t).bitcast(F32), ALU.subtract)
                    o.then_inc(o_lo, 1)

            swa_units(dve, (mask, maxima, with_sink, sink_left, negate, total, inverse, scale, remainder))
            dve.wait_ge(o_lo, PRIME + 24)
            dve.nop().then_inc(mixer_ready, KT)

        def pool_swa(pool, st):
            pool.wait_ge(evacuated, st["g0"])
            pool.memset(at_kbd[:, :, :, :], 0.0).then_inc(kbd_ready, 1)
            pool.memset(at_vbd[:, :, :, :], 0.0).then_inc(kbd_ready, 2)
            pool_rope(pool, st, at_q, at_q, [at_kv[:, 0:1, :]])
            pool.wait_ge(rope_ready, 2 + st["rope"] + 9)
            pool.wait_ge(kbd_ready, 3)
            for grp in range(2):
                rows = slice(HD * grp, HD * grp + HD)
                pool.tensor_copy(at_kbd[rows, :, grp, :], at_kv[rows, 0, 0:NP_TOK].rearrange("p (c j) -> p c j", c=2))\
                    .then_inc(kbd_ready, 1)
            pool.wait_ge(swa_landed, 48)
            pool.wait_ge(kbd_ready, 5)

            def stage_queries(V, u, c, t):
                pool.wait_ge(s_ready, V - 2)
                if c is not None:
                    pool.tensor_copy(at_qst[:, u, :], queries(at_q, t, slice(P * c, P * c + P))).then_inc(q_staged, 1)
                else:
                    pool.tensor_tensor(at_qst[:, u, :].rearrange("p (g t s) -> p g t s", g=2, s=NQ), sample_queries(at_q, t),
                                       cst("bd").rearrange("p (g t s) -> p g t s", g=2, s=NQ), ALU.mult)
                    pool.wait_ge(o_ready, V - 2)
                    pool.tensor_copy(at_vst[:, u, :], at_vc[:, bass.ds(t, 1), :].rearrange("p a d -> p (a d)")).then_inc(q_staged, 1)

            for c in (0, 1, None):
                with pool.Fori(0, 4) as i:
                    for u in range(2):
                        base = PRIME + (16 if c is None else 8 * c)
                        stage_queries(base + u + 1 + 2 * i, u, c, 2 * i + u)

        N_STRIDE = 8
        n_pages = A["pool_cmp"].shape[0]
        if "nsa" in kinds:
            space = Space(H_AT, LIMIT)
            w1_past = space("w1_past", [P, 2, 16, 256])
            past_pairs = space("past_pairs", [P, 2, 4, 2 * PAST // 2])
            past_hid = space("past_hid", [P, 2, 2, 2, 2 * N_CMP_S])
            cmp_landed = sem("cmp_landed")
            pairs_landed = [sem(f"pairs_landed{s}") for s in range(2)]
            hid_ready = sem("hid_ready")
            bias_summed = sem("bias_summed")
            bias_ready = sem("bias_ready")
            hid_gelu = sem("hid_gelu")
            cmp_made = sem("cmp_made")
            cmp_kept = sem("cmp_kept")
            win_passed = sem("win_passed")

            r1, r2 = Space(H_AT + KT * T * 4, HL_AT), Space(HL_AT + KT * T * 4, END)
            xh, xl = Space(XH_AT, XL_AT), Space(XL_AT, CONST_AT)
            w1_space, r3 = Space(END, LIMIT), Space(END, LIMIT)
            n_q = r1("n_q", [P, KT, T])
            n_kv = r1("n_kv", [P, 6, T])
            n_qr = r2("n_qr", [P, KT, T])
            n_kbd = [r2(f"n_kbd{a}", [P, 2, 2, P]) for a in range(2)]
            n_gates = r2("n_gates", [P, 1, T])
            n_gt = r2("n_gt", [P, 2, 48])
            n_kcb = r2("n_kcb", [P, 64])
            n_vcb = r2("n_vcb", [64, P])
            n_sg = r2("n_sg", [P, NB, 3])
            n_vbd = [xh(f"n_vbd{a}", [P, 2, 2, P]) for a in range(2)]
            n_wk = xh("n_wk", [P, NB, P])
            n_qst = xh("n_qst", [P, 2, 2, P])
            n_wv = xl("n_wv", [P, NB, P])
            n_vst = xl("n_vst", [P, 2, P])
            n_vcst = xl("n_vcst", [64, 2, P])
            n_vs = [xl(f"n_vs{a}", [NS_TOK, P]) for a in range(2)]
            n_pairs = xl("n_pairs", [P, 2, 2, NP_TOK // 2])
            n_mx, n_neg, n_sum, n_rec, n_fac = (silu_space("n_" + s, [P, 2, 6]) for s in ("mx", "neg", "sum", "rec", "fac"))
            n_imp, n_hit, n_blk = (silu_space("n_" + s, [P, 2, 16]) for s in ("imp", "hit", "blk"))
            n_low, n_drop = (silu_space("n_" + s, [P, 2]) for s in ("low", "drop"))
            n_srow = silu_space("n_srow", [P, 3, NS_TOK])
            n_hid = h_space("n_hid", [P, 2, 2, P])
            w1_new = w1_space("w1_new", [P, 2, 16, 256])
            n_p = r3("n_p", [P, 2, 1344])
            n_pt = r3("n_pt", [P, 2304])
            n_sel = r3("n_sel", [P, 2, NPAGES, 2 * P])
            w1_landed = sem("w1_landed")
            win_landed = sem("win_landed")
            sel_landed = [sem(f"sel_landed{s}") for s in range(2)]
            pairs_ready = sem("pairs_ready")
            hid_clear = sem("hid_clear")
            lay_clear = sem("lay_clear")
            nhid_ready = sem("nhid_ready")
            nhid_gelu = sem("nhid_gelu")
            gates_ready = sem("gates_ready")
            nv_turned = sem("nv_turned")
            nv_ready = sem("nv_ready")
            n_laid = sem("n_laid")
            n_lay_step = sem("n_lay_step")
            nk_ready = sem("nk_ready")
            nq_staged = sem("nq_staged")
            ns_ready = sem("ns_ready")
            nmasked = sem("nmasked")
            n_step = sem("n_step")
            nneg_ready = sem("nneg_ready")
            nexp_ready = sem("nexp_ready")
            sel_kept = sem("sel_kept")
            pc_ready = sem("pc_ready")
            imp_ready = sem("imp_ready")
            imp_read = sem("imp_read")
            selneg_ready = sem("selneg_ready")
            selexp_ready = sem("selexp_ready")
            np_ready = sem("np_ready")
            npt_turned = sem("npt_turned")
            npt_copied = sem("npt_copied")
            no_ready = sem("no_ready")
            no_hi = sem("no_hi")
            no_lo = sem("no_lo")
            pe_primed += [ns_ready, npt_turned, no_ready, cmp_made]
            act_primed += [npt_copied, no_hi, sel_kept, hid_gelu, cmp_kept]
            dve_primed += [nmasked, no_lo, imp_read]
            pool_primed += [nq_staged]

        def sp_past_pairs(sp, j):
            if j >= 2:
                sp.wait_ge(hid_ready, 4 * (j - 1))
            with sp.Fori(0, 2 * NPAGES) as r:
                pg = sp.value_load(pages[0:1, bass.ds(r + 2 * NPAGES * j, 1)], min_val=0, max_val=n_pages - 1)
                sp.dma_start(past_pairs[:, j % 2, :, bass.ds(N_PAIR * r, N_PAIR)],
                             A["pool_cmp"][bass.ds(pg, 1)].rearrange("a p (k n) -> p (a k) n", k=4))\
                    .then_inc(pairs_landed[j % 2], 16)

        def sp_past_first(sp):
            sp.dma_start(pages[:, :], A["pages"]).then_inc(cmp_landed, 16)
            sp.dma_start(cmp_pe[:, :, :], A["cmp_pe"]).then_inc(cmp_landed, 16)
            sp.dma_start(w1_past[:, :, :, :], A["cmp_w1"]).then_inc(cmp_landed, 16)
            sp.dma_start(w2z[:, :, :, :, :], A["cmp_w2"]).then_inc(cmp_landed, 16)
            sp.wait_ge(cmp_landed, 64)
            for j in range(2):
                sp_past_pairs(sp, j)

        def sp_past_rest(sp):
            for j in range(2, NB // 2):
                sp_past_pairs(sp, j)

        def pe_hidden(pe, w1, pairs, blocks, kv, ht, out):
            for pp in range(16):
                mm = pe.matmul(out, w1[:, kv, pp, P * ht:P * ht + P],
                               pairs[..., pp:pp + N_STRIDE * (blocks - 1) + 1:N_STRIDE], start=(pp == 0), stop=(pp == 15))
            return mm

        def pe_past(pe):
            pe.wait_ge(cmp_landed, 64)
            for kv in range(2):
                for ht in range(2):
                    for pp in range(16):
                        mm = pe.matmul(bank[7][:, 2 * kv + ht:2 * kv + ht + 1], w1_past[:, kv, pp, P * ht:P * ht + P],
                                       cmp_pe[:, kv, pp:pp + 1], start=(pp == 0), stop=(pp == 15))
            mm.then_inc(bias_summed, 1)
            with pe.Fori(0, 2) as i:
                for q in range(2):
                    pe.wait_ge(pairs_landed[q], 32 * NPAGES * (i + 1))
                    for kv in range(2):
                        for ht in range(2):
                            pe.wait_ge(hid_gelu, PRIME + 4 * q + 2 * kv + ht + 1 - 4 + 8 * i)
                            pairs = past_pairs[:, q, 2 * kv:2 * kv + 2, :].rearrange("p g (b n) -> p g b n", b=2)
                            out = bank[2 * kv + ht][:, 0:4 * N_CMP_S].rearrange("p (g b n) -> p g b n", g=2, b=2)
                            pe_hidden(pe, w1_past, pairs, N_CMP_S, kv, ht, out).then_inc(hid_ready, 1)
                    pe.wait_ge(hid_gelu, 4 + 4 * q + 2 + 8 * i)
                    pe.wait_ge(cmp_kept, PRIME + 2 * q - 1 + 4 * i)
                    for k in range(4):
                        mm = pe.matmul(bank[5][:, 0:2 * N_CMP_S], w2z[:, 0, k // 2, k % 2, :], past_hid[:, 0, k // 2, k % 2, :],
                                       start=(k == 0), stop=(k == 3))
                    mm.then_inc(cmp_made, 1)
                    pe.wait_ge(hid_gelu, 4 + 4 * q + 4 + 8 * i)
                    pe.wait_ge(cmp_kept, PRIME + 2 * q + 4 * i)
                    for b in range(2):
                        for k in range(4):
                            mm = pe.matmul(bank[6][0:N_CMP_S, P * b:P * b + P],
                                           past_hid[:, 1, k // 2, k % 2, N_CMP_S * b:N_CMP_S * b + N_CMP_S],
                                           w2z[:, 1, k // 2, k % 2, :], start=(k == 0), stop=(k == 3))
                    mm.then_inc(cmp_made, 1)

        def act_past(act):
            act.wait_ge(bias_summed, 1)
            act.activation(cmp_bias[:, :, :].rearrange("p k h -> p (k h)"), bank[7][:, 0:4], ACT.Copy).then_inc(bias_ready, 1)
            act.wait_ge(bias_ready, 1)
            with act.Fori(0, 2) as i:
                for q in range(2):
                    for kv in range(2):
                        act.wait_ge(cmp_made, PRIME + 2 * q + kv - 1 + 4 * i)
                        for ht in range(2):
                            act.wait_ge(hid_ready, 4 * q + 2 * kv + ht + 1 + 8 * i)
                            act.activation(past_hid[:, kv, ht, :, :],
                                           bank[2 * kv + ht][:, 0:4 * N_CMP_S].rearrange("p (g n) -> p g n", g=2),
                                           ACT.Gelu_apprx_tanh, bias=cmp_bias[:, kv, ht:ht + 1]).then_inc(hid_gelu, 1)
                    act.wait_ge(cmp_made, PRIME + 2 * q + 1 + 4 * i)
                    act.activation(kcmp_s[:, bass.ds(4 * i + 2 * q, 2), 0:N_CMP_S],
                                   bank[5][:, 0:2 * N_CMP_S].rearrange("p (b n) -> p b n", b=2), ACT.Copy).then_inc(cmp_kept, 1)
                    act.wait_ge(cmp_made, PRIME + 2 * q + 2 + 4 * i)
                    act.activation(vcmp_s[0:N_CMP_S, bass.ds(4 * i + 2 * q, 2), :],
                                   bank[6][0:N_CMP_S, 0:2 * P].rearrange("p (b d) -> p b d", b=2), ACT.Copy).then_inc(cmp_kept, 1)

        def sp_nsa_load(sp):
            sp.dma_start(O["win_passed"], A["win_old"][:, NQ:P, :]).then_inc(win_passed, 16)

        def sp_nsa_store(sp):
            sp.wait_ge(evacuated, nsa_st["g0"] + nsa_st["groups"])
            sp.dma_start(n_wk[:, :, :], A["win_k"]).then_inc(win_landed, 16)
            sp.dma_start(n_wv[:, :, :], A["win_v"]).then_inc(win_landed, 16)
            sp.wait_ge(nhid_ready, 4)
            with sp.Fori(0, NB // 2) as i:
                for u in range(2):
                    with sp.Fori(0, NPAGES) as r:
                        pg = sp.value_load(pages[0:1, bass.ds(r + 2 * NPAGES * i + NPAGES * u, 1)], min_val=0, max_val=n_pages - 1)
                        sp.wait_ge(no_ready, PRIME + 16 + u - 1 + 2 * i)
                        sp.dma_start(n_sel[:, u, bass.ds(r, 1), :], A["pool_sel"][bass.ds(pg, 1)].rearrange("a p n -> p a n"))\
                            .then_inc(sel_landed[u], 16)
            sp.wait_ge(rope_ready, 2 + nsa_st["rope"] + 10)
            sp.dma_start(O["nsa_kv"], n_kv[:, :, :]).then_inc(mix_stored["nsa"], 16)

        def nsa_units(engine, prompt_lists, sample_lists):
            for c in (0, 1, None):
                with engine.Fori(0, 4) as i:
                    for step in (sample_lists if c is None else prompt_lists):
                        for u in range(2):
                            base = PRIME + (16 if c is None else 8 * c)
                            step(base + u + 1 + 2 * i, u, c, 2 * i + u)

        def pe_nsa(pe, st):
            pe_in(pe, st)
            pe_rope(pe, st, n_q, [n_kv[:, 2:3, :], n_kv[:, 4:5, :]])
            pe.wait_ge(w1_landed, 16)
            pe.wait_ge(pairs_ready, 4)
            for kv in range(2):
                for ht in range(2):
                    out = bank[2 * kv + ht][:, 0:2 * N_CMP_P].rearrange("p (g n) -> p g n", g=2)
                    pe_hidden(pe, w1_new, n_pairs[:, kv, :, :], N_CMP_P, kv, ht, out).then_inc(nhid_ready, 1)
            pe.wait_ge(rot_sin, 2 + st["rope"] + 10)
            for a in range(2):
                for c in range(3):
                    w = P if c < 2 else NS_TOK
                    tr = pe.transpose(bank[5 + a][0:w, P * c:P * c + P], n_kv[:, 3 + 2 * a, P * c:P * c + w], cst("ident"))
            tr.then_inc(nv_turned, 1)
            pe.wait_ge(gates_ready, 1)
            for c in range(2):
                pe.transpose(bank[7][:, P * c:P * c + P], n_gates[:, 0, P * c:P * c + P], cst("ident"))
            for k in range(3):
                pe.matmul(bank[7][:, 320 + NS_TOK * k:320 + NS_TOK * (k + 1)], cst("row_of")[:, P * k:P * k + P],
                          n_gates[:, 0, NP_TOK:T], start=True, stop=True)
            pe.wait_ge(nhid_gelu, 4)
            for k in range(4):
                pe.matmul(bank[7][:, 256:320], w2z[:, 0, k // 2, k % 2, :], n_hid_of(0, k), start=(k == 0), stop=(k == 3))
            for k in range(4):
                mm = pe.matmul(bank[4][0:64, 0:P], n_hid_of(1, k), w2z[:, 1, k // 2, k % 2, :], start=(k == 0), stop=(k == 3))
            mm.then_inc(n_laid, 1)
            pe.wait_ge(nk_ready, 4)
            pe.wait_ge(win_landed, 32)
            pe.wait_ge(n_lay_step, 5)
            pe.wait_ge(nv_ready, 6)

            def scores(V, u, c, t):
                pe.wait_ge(nq_staged, V)
                pe.wait_ge(nmasked, V - 1)
                plain, turned = n_qst[:, u, 0, :], n_qst[:, u, 1, :]
                if c is not None:
                    n = 2 * P * (c + 1)
                    for a in range(2):
                        pe.matmul(bank[a][:, 0:n], turned, n_kbd[a][:, 0:c + 1, :, :], start=True, stop=True)
                    pe.matmul(bank[2][:, 0:64], plain, n_kcb[:, :], start=True, stop=True).then_inc(ns_ready, 1)
                    return
                pe.wait_ge(sel_kept, V - 16 - 1)
                pe.matmul(bank[2][:, 0:64], turned, n_kv[:, 2, NP_TOK:T], start=True, stop=True)
                pe.matmul(bank[2][:, 64:128], turned, n_kv[:, 4, NP_TOK:T], start=True, stop=True)
                pe.matmul(bank[2][:, 128:256], turned, one(n_wk, t), start=True, stop=True)
                pe.matmul(bank[2][:, 256:256 + N_CMP_S], plain,
                          kcmp_s[:, bass.ds(t, 1), 0:N_CMP_S].rearrange("p a n -> p (a n)"), start=True, stop=True)
                pe.wait_ge(sel_landed[u], 8 * NPAGES * (t - u + 2))
                for a in range(2):
                    mm = pe.matmul(bank[a][:, :], turned, n_sel[:, u, 4 * a:4 * a + 4, 0:P], start=True, stop=True)
                mm.then_inc(ns_ready, 1)

            def importance(V, u, c, t):
                pe.wait_ge(pc_ready, V - PRIME - 16)
                pe.wait_ge(imp_read, V - 16 - 1)
                pe.matmul(bank[4][:, 0:N_CMP_S], cst("sum_r"), n_p[:, u, 1280:1280 + N_CMP_S], start=True, stop=True)\
                    .then_inc(imp_ready, 1)

            def turn(V, u, c, t):
                pe.wait_ge(np_ready, V - PRIME)
                pe.wait_ge(npt_copied, V - 1)
                ident = cst("ident")
                if c is not None:
                    for a in range(2):
                        for k in range(2 * (c + 1)):
                            pe.transpose(bank[(3, 5)[a]][:, P * k:P * k + P], n_p[:, u, 512 * a + P * k:512 * a + P * k + P], ident)
                    pe.transpose(bank[6][0:64, 0:P], n_p[:, u, 1024:1088], ident).then_inc(npt_turned, 1)
                    return
                for k in range(NPAGES):
                    pe.transpose(bank[(3, 5)[k // 4]][:, P * (k % 4):P * (k % 4) + P], n_p[:, u, P * k:P * k + P], ident)
                for k, (at, n) in enumerate(((1152, P), (1088, 64), (1024, 64), (1280, N_CMP_S))):
                    tr = pe.transpose(bank[6][0:n, P * k:P * k + P], n_p[:, u, at:at + n], ident)
                tr.then_inc(npt_turned, 1)

            def values(V, u, c, t):
                pe.wait_ge(npt_copied, V)
                pe.wait_ge(no_lo, V - 1)
                if c is not None:
                    at = 1152 * u
                    terms = [(n_vbd[a][:, k // 2, k % 2, :], n_pt[:, at + 512 * a + P * k:at + 512 * a + P * k + P])
                             for a in range(2) for k in range(2 * (c + 1))]
                    terms.append((n_vcb[:, :], n_pt[0:64, at + 1024:at + 1152]))
                else:
                    terms = [(n_sel[:, u, k, P:2 * P], n_pt[:, P * k:P * k + P]) for k in range(NPAGES)]
                    terms += [(n_vst[:, u, :], n_pt[:, 1024:1152]), (n_vs[1][:, :], n_pt[0:64, 1152:1280]),
                              (n_vs[0][:, :], n_pt[0:64, 1280:1408]), (n_vcst[0:N_CMP_S, u, :], n_pt[0:N_CMP_S, 1408:1536])]
                for k, (v, p) in enumerate(terms):
                    mm = pe.matmul(bank[7][:, 0:P], v, p, start=(k == 0), stop=(k == len(terms) - 1))
                mm.then_inc(no_ready, 1)

            nsa_units(pe, (scores, turn, values), (scores, importance, turn, values))

        def n_hid_of(kv, k):
            return n_hid[:, kv, k // 2, 64 * (k % 2):64 * (k % 2) + 64]

        def one(a, t):
            return a[:, bass.ds(t, 1), :].rearrange("p a n -> p (a n)")

        def act_nsa(act, st):
            act.wait_ge(evacuated, st["g0"])
            act.dma_start(w1_new[:, :, :, :], A["cmp_w1"]).then_inc(w1_landed, 16)
            act_splits(act, st, 2)
            act.wait_ge(evacuated, st["g0"] + st["groups"])
            act.activation(n_gates[:, :, :], n_gates[:, :, :], ACT.Sigmoid).then_inc(gates_ready, 1)
            act.wait_ge(hid_clear, 1)
            for kv in range(2):
                for ht in range(2):
                    act.wait_ge(nhid_ready, 2 * kv + ht + 1)
                    for grp in range(2):
                        g_op = act.activation(n_hid_of(kv, 2 * ht + grp)[:, 32 * grp:32 * grp + N_CMP_P],
                                              bank[2 * kv + ht][:, N_CMP_P * grp:N_CMP_P * grp + N_CMP_P],
                                              ACT.Gelu_apprx_tanh, bias=cmp_bias[:, kv, ht:ht + 1])
                    g_op.then_inc(nhid_gelu, 1)
            act.wait_ge(nv_turned, 1)
            act.wait_ge(lay_clear, 4)
            for a in range(2):
                vt = bank[5 + a][:, 0:2 * P].rearrange("p (c g d) -> p c g d", c=2, g=2)
                for grp in range(2):
                    act.activation(n_vbd[a][:, :, grp, HD * grp:HD * grp + HD], vt[:, :, grp, :], ACT.Copy).then_inc(nv_ready, 1)
                act.activation(n_vs[a][:, :], bank[5 + a][0:NS_TOK, 2 * P:3 * P], ACT.Copy).then_inc(nv_ready, 1)

            def exp_of(u, at, n, col, **kw):
                p = n_p[:, u, at:at + n]
                return act.activation(p, p, ACT.Exp, bias=n_neg[:, u, col:col + 1], scale=SCALE, accum_out=n_sum[:, u, col:col + 1])

            def exps(V, u, c, t):
                act.wait_ge(nneg_ready, V - PRIME)
                if c is not None:
                    for a in range(2):
                        pg = n_p[:, u, 512 * a:512 * a + 2 * P * (c + 1)].rearrange("p (k g j) -> p k g j", g=2, j=P)
                        for grp in range(2):
                            col = 2 * (a + 1) + grp
                            act.activation(pg[:, :, grp, :], pg[:, :, grp, :], ACT.Exp, bias=n_neg[:, u, col:col + 1],
                                           scale=SCALE, accum_out=n_sum[:, u, col:col + 1])
                    exp_of(u, 1024, 32, 0)
                    exp_of(u, 1056, 32, 1).then_inc(nexp_ready, 1)
                else:
                    exp_of(u, 1088, 192, 2)
                    exp_of(u, 1280, N_CMP_S, 0).then_inc(nexp_ready, 1)

            def keep(V, u, c, t):
                act.wait_ge(ns_ready, V)
                act.wait_ge(npt_turned, V - 2)
                act.activation(n_p[:, u, 0:512], bank[0][:, :], ACT.Copy)
                act.activation(n_p[:, u, 512:1024], bank[1][:, :], ACT.Copy).then_inc(sel_kept, 1)

            def sel_exps(V, u, c, t):
                act.wait_ge(selneg_ready, V - PRIME - 16)
                exp_of(u, 0, 1088, 1).then_inc(selexp_ready, 1)

            def copies(V, u, c, t):
                act.wait_ge(npt_turned, V)
                if c is not None:
                    act.wait_ge(no_ready, V - 2)
                    n, at = 2 * P * (c + 1), 1152 * u
                    act.activation(n_pt[:, at:at + n], bank[3][:, 0:n], ACT.Copy)
                    act.activation(n_pt[:, at + 512:at + 512 + n], bank[5][:, 0:n], ACT.Copy)
                    act.activation(n_pt[0:64, at + 1024:at + 1152], bank[6][0:64, 0:P], ACT.Copy).then_inc(npt_copied, 1)
                    return
                act.wait_ge(no_ready, V - 1)
                act.activation(n_pt[:, 0:512], bank[3][:, :], ACT.Copy)
                act.activation(n_pt[:, 512:1024], bank[5][:, :], ACT.Copy)
                act.activation(n_pt[:, 1024:1152], bank[6][:, 0:P], ACT.Copy)
                act.activation(n_pt[0:64, 1152:1408], bank[6][0:64, P:3 * P], ACT.Copy)
                act.activation(n_pt[0:N_CMP_S, 1408:1536], bank[6][0:N_CMP_S, 3 * P:4 * P], ACT.Copy).then_inc(npt_copied, 1)

            def outs(V, u, c, t):
                act.wait_ge(no_ready, V)
                if c is not None:
                    act.activation(queries(h_hi, t, slice(P * c, P * c + P)), bank[7][:, 0:P], ACT.Copy).then_inc(no_hi, 1)
                else:
                    for grp in range(2):
                        o = act.activation(sample_rows(h_hi, grp, t), out_block(bank[7], grp), ACT.Copy)
                    o.then_inc(no_hi, 1)

            nsa_units(act, (exps, copies, outs), (keep, exps, sel_exps, copies, outs))

        def out_block(b, grp):
            return b[HD * grp:HD * grp + HD, HD * grp:HD * grp + HD].rearrange("p (t s) -> p t s", s=NQ)

        def dve_nsa(dve, st):
            n0, g0 = st["n0"], st["g0"]
            dve_rstd(dve, st["norm"])
            with dve.Fori(0, 2) as i:
                for c in range(2):
                    for f in range(2):
                        dve_take3(dve, n0 + c, f, g0 + 2 * c + f, n_q[:, bass.ds(2 * c + f + 4 * i, 1), :], i, 2, 4)
                    dve_split(dve, n0 + RAW + c, i, 2)
            for c in range(4, 7):
                for f in range(2):
                    dve_take3(dve, n0 + c, f, g0 + 2 * c + f, n_kv[:, 2 * (c - 4) + f:2 * (c - 4) + f + 1, :])
                dve_split(dve, n0 + RAW + c)
            dve_take3(dve, n0 + 7, 0, g0 + 14, n_gates[:, :, :], count=2)
            dve_split(dve, n0 + RAW + 7)
            dve.wait_ge(evacuated, g0 + st["groups"])
            for e in range(2):
                for grp in range(2):
                    dve.tensor_copy(n_pairs[HD * e:HD * e + HD, :, grp, :], n_kv[HD * grp:HD * grp + HD, 0:2, e:NP_TOK:2])\
                        .then_inc(pairs_ready, 1)
            dve_rope(dve, st, n_q, [n_kv[:, 2:3, :], n_kv[:, 4:5, :]])
            dve.wait_ge(n_laid, 1)
            dve.tensor_copy(n_gt[:, :, :], bank[7][:, 0:2 * P].rearrange("p (c n) -> p c n", c=2)[:, :, 0:48]).then_inc(n_lay_step, 1)
            dve.tensor_copy(n_kcb[:, :], bank[7][:, 256:320]).then_inc(n_lay_step, 1)
            dve.tensor_copy(n_vcb[:, :], bank[4][0:64, 0:P]).then_inc(n_lay_step, 1)
            dve.tensor_tensor(n_srow[:, :, :], bank[7][:, 320:512].rearrange("p (k t) -> p k t", k=3),
                              cst("tok_of").rearrange("p (k t) -> p k t", k=1).broadcast_to([P, 3, NS_TOK]), ALU.mult)\
                .then_inc(n_lay_step, 1)
            dve.wait_ge(n_lay_step, 4)
            dve.tensor_reduce(n_sg[:, :, :], n_srow[:, :, :].rearrange("p k (b s) -> p b k s", s=NQ), AX.X, ALU.add)\
                .then_inc(n_lay_step, 1)
            dve.wait_ge(n_lay_step, 5)

            causal = cst("m_band")[:, 2 * P:4 * P]

            def mask(V, u, c, t):
                dve.wait_ge(ns_ready, V)
                dve.wait_ge(npt_turned, V - 2)
                if c is None:
                    dve.wait_ge(no_ready, V - 2)
                    dve.tensor_copy(n_vcst[0:N_CMP_S, u, :], one(vcmp_s[0:N_CMP_S], t))
                    m = cst("m_new").rearrange("p (b k) -> p b k", b=NB)[:, bass.ds(t, 1), :].broadcast_to([P, 2, NS_TOK])
                    dve.tensor_tensor(n_p[:, u, 1024:1152].rearrange("p (a k) -> p a k", a=2),
                                      bank[2][:, 0:128].rearrange("p (a k) -> p a k", a=2), m, ALU.add)
                    dve.tensor_tensor(n_p[:, u, 1152:1280], bank[2][:, 128:256], cst("m_old"), ALU.add)
                    dve.tensor_copy(n_p[:, u, 1280:1280 + N_CMP_S], bank[2][:, 256:256 + N_CMP_S]).then_inc(nmasked, 1)
                    return
                if c:
                    dve.tensor_copy(n_p[:, u, 0:256], bank[0][:, 0:256])
                    dve.tensor_tensor(n_p[:, u, 256:512], bank[0][:, 256:512], causal, ALU.add)
                    dve.tensor_tensor(n_p[:, u, 512:1024], bank[1][:, :], cst("m_band"), ALU.add)
                else:
                    for a in range(2):
                        dve.tensor_tensor(n_p[:, u, 512 * a:512 * a + 256], bank[a][:, 0:256], causal, ALU.add)
                seen = cst("m_cmp")[:, 8 - 8 * c:40 - 8 * c].rearrange("p (g n) -> p g n", g=1).broadcast_to([P, 2, 32])
                dve.tensor_tensor(n_p[:, u, 1024:1088].rearrange("p (g n) -> p g n", g=2),
                                  bank[2][:, 0:64].rearrange("p (g n) -> p g n", g=2), seen, ALU.add).then_inc(nmasked, 1)

            N_PROMPT_STEPS, N_SAMPLE_STEPS = 3, 12

            def done(V, u, c, k):
                if c is None:
                    return N_PROMPT_STEPS * 16 + N_SAMPLE_STEPS * (V - u - PRIME - 17) + 2 * k + u + 1
                return N_PROMPT_STEPS * (V - u - PRIME - 1) + 2 * k + u + 1

            def maxima(V, u, c, t):
                dve.wait_ge(nmasked, V)
                if c is None:
                    dve.tensor_reduce(n_mx[:, u, 0:1], n_p[:, u, 1280:1280 + N_CMP_S], AX.X, ALU.max)
                    dve.tensor_reduce(n_mx[:, u, 2:3], n_p[:, u, 1088:1280], AX.X, ALU.max).then_inc(n_step, 1)
                    return
                for a in range(2):
                    pg = n_p[:, u, 512 * a:512 * a + 2 * P * (c + 1)].rearrange("p (k g j) -> p g k j", g=2, j=P)
                    dve.tensor_reduce(n_mx[:, u, 2 * a + 2:2 * a + 4], pg, AX.XY, ALU.max)
                dve.tensor_reduce(n_mx[:, u, 0:2], n_p[:, u, 1024:1088].rearrange("p (g n) -> p g n", g=2), AX.X, ALU.max)\
                    .then_inc(n_step, 1)

            def negate(V, u, c, t):
                dve.wait_ge(n_step, done(V, u, c, 0))
                cols = slice(0, 6) if c is not None else slice(0, 3, 2)
                dve.tensor_scalar(n_neg[:, u, cols], n_mx[:, u, cols], -SCALE, None, ALU.mult).then_inc(nneg_ready, 1)

            def inverse(V, u, c, t):
                dve.wait_ge(nexp_ready, V - PRIME)
                n = 6 if c is not None else 1
                dve.reciprocal(n_rec[:, u, 0:n], n_sum[:, u, 0:n]).then_inc(n_step, 1)

            def gate(V, u, c, t):
                dve.wait_ge(n_step, done(V, u, c, 1))
                g = n_gt[:, c, :].rearrange("p (k g t) -> p k g t", k=3, g=2)[:, :, :, bass.ds(t, 1)].rearrange("p k g t -> p k (g t)")
                dve.tensor_tensor(n_fac[:, u, :].rearrange("p (k g) -> p k g", k=3), n_rec[:, u, :].rearrange("p (k g) -> p k g", k=3),
                                  g, ALU.mult).then_inc(n_step, 1)

            def scale(V, u, c, t):
                dve.wait_ge(n_step, done(V, u, c, 2))
                for a in range(2):
                    pg = n_p[:, u, 512 * a:512 * a + 2 * P * (c + 1)].rearrange("p (k g j) -> p k g j", g=2, j=P)
                    for grp in range(2):
                        col = 2 * (a + 1) + grp
                        dve.tensor_scalar(pg[:, :, grp, :], pg[:, :, grp, :], n_fac[:, u, col:col + 1], None, ALU.mult)
                for grp in range(2):
                    pc = n_p[:, u, 1024 + 32 * grp:1056 + 32 * grp]
                    o = dve.scalar_tensor_tensor(out=pc, in0=pc, scalar=n_fac[:, u, grp:grp + 1],
                                                 in1=cst("ok_cmp")[:, 8 - 8 * c:40 - 8 * c], op0=ALU.mult, op1=ALU.mult)
                o.then_inc(np_ready, 1)

            def remainder(V, u, c, t):
                dve.wait_ge(no_hi, V)
                if c is not None:
                    rows = slice(P * c, P * c + P)
                    dve.tensor_tensor(queries(h_lo, t, rows), bank[7][:, 0:P], queries(h_hi, t, rows).bitcast(F32),
                                      ALU.subtract).then_inc(no_lo, 1)
                    return
                for grp in range(2):
                    o = dve.tensor_tensor(sample_rows(h_lo, grp, t), out_block(bank[7], grp),
                                          sample_rows(h_hi, grp, t).bitcast(F32), ALU.subtract)
                o.then_inc(no_lo, 1)

            def block_probs(V, u, c, t):
                dve.wait_ge(n_step, done(V, u, c, 1))
                p = n_p[:, u, 1280:1280 + N_CMP_S]
                dve.tensor_scalar(p, p, n_rec[:, u, 0:1], None, ALU.mult).then_inc(pc_ready, 1)

            def block_scores(V, u, c, t):
                dve.wait_ge(imp_ready, V - PRIME - 16)
                dve.tensor_reduce(n_imp[:, u, 0:14], bank[4][:, 3:59].rearrange("p (k f) -> p k f", f=4), AX.X, ALU.add)\
                    .then_inc(n_step, 1)
                dve.wait_ge(n_step, done(V, u, c, 2))
                dve.tensor_tensor(n_imp[:, u, 0:14], n_imp[:, u, 0:14], bank[4][:, 7:60:4], ALU.add).then_inc(imp_read, 1)

            def least(V, u, c, t):
                dve.wait_ge(imp_read, V - 16)
                dve.tensor_reduce(n_low[:, u:u + 1], n_imp[:, u, 0:14], AX.X, ALU.min).then_inc(n_step, 1)

            def numbers_of_least(V, u, c, t):
                dve.wait_ge(n_step, done(V, u, c, 3))
                dve.scalar_tensor_tensor(out=n_hit[:, u, 0:14], in0=n_imp[:, u, 0:14], scalar=n_low[:, u:u + 1],
                                         in1=cst("blk_no")[:, 1:15], op0=ALU.is_equal, op1=ALU.mult).then_inc(n_step, 1)

            def dropped(V, u, c, t):
                dve.wait_ge(n_step, done(V, u, c, 4))
                dve.tensor_reduce(n_drop[:, u:u + 1], n_hit[:, u, 0:14], AX.X, ALU.max).then_inc(n_step, 1)

            def block_mask(V, u, c, t):
                dve.wait_ge(n_step, done(V, u, c, 5))
                dve.tensor_scalar(n_blk[:, u, :], cst("blk_no"), n_drop[:, u:u + 1], NEG, ALU.is_equal, ALU.mult).then_inc(n_step, 1)

            def select(V, u, c, t):
                dve.wait_ge(n_step, done(V, u, c, 6))
                dve.wait_ge(sel_kept, V - 16)
                p = n_p[:, u, 0:1024].rearrange("p (k j) -> p k j", k=16)
                dve.tensor_tensor(p, p, n_blk[:, u, :].rearrange("p (k j) -> p k j", j=1).broadcast_to([P, 16, 64]), ALU.add)\
                    .then_inc(n_step, 1)

            def sel_maximum(V, u, c, t):
                dve.wait_ge(n_step, done(V, u, c, 7))
                dve.tensor_reduce(n_mx[:, u, 1:2], n_p[:, u, 0:1088], AX.X, ALU.max).then_inc(n_step, 1)

            def sel_negate(V, u, c, t):
                dve.wait_ge(n_step, done(V, u, c, 8))
                dve.tensor_scalar(n_neg[:, u, 1:2], n_mx[:, u, 1:2], -SCALE, None, ALU.mult).then_inc(selneg_ready, 1)

            def sel_inverse(V, u, c, t):
                dve.wait_ge(selexp_ready, V - PRIME - 16)
                dve.reciprocal(n_rec[:, u, 1:3], n_sum[:, u, 1:3]).then_inc(n_step, 1)

            def sel_gate(V, u, c, t):
                dve.wait_ge(n_step, done(V, u, c, 9))
                dve.tensor_tensor(n_fac[:, u, 1:3], n_rec[:, u, 1:3],
                                  n_sg[:, bass.ds(t, 1), 1:3].rearrange("p a k -> p (a k)"), ALU.mult).then_inc(n_step, 1)

            def cmp_gate(V, u, c, t):
                dve.tensor_copy(n_fac[:, u, 0:1], n_sg[:, bass.ds(t, 1), 0:1].rearrange("p a k -> p (a k)")).then_inc(n_step, 1)

            def sample_scale(V, u, c, t):
                dve.wait_ge(n_step, done(V, u, c, 11))
                dve.wait_ge(imp_ready, V - PRIME - 16)
                for col, at, n in ((0, 1280, N_CMP_S), (2, 1088, 192), (1, 0, 1088)):
                    p = n_p[:, u, at:at + n]
                    o = dve.tensor_scalar(p, p, n_fac[:, u, col:col + 1], None, ALU.mult)
                o.then_inc(np_ready, 1)

            nsa_units(dve, (mask, maxima, negate, inverse, gate, scale, remainder),
                      (mask, maxima, negate, inverse, block_probs, block_scores, least, numbers_of_least,
                       dropped, block_mask, select, sel_maximum, sel_negate, sel_inverse, sel_gate, cmp_gate, sample_scale,
                       remainder))
            dve.wait_ge(no_lo, PRIME + 24)
            dve.nop().then_inc(mixer_ready, KT)

        def pool_nsa(pool, st):
            pool.wait_ge(evacuated, st["g0"])
            pool.memset(n_hid[:, :, :, :], 0.0).then_inc(hid_clear, 1)
            for a in range(2):
                pool.memset(n_kbd[a][:, :, :, :], 0.0).then_inc(lay_clear, 1)
            pool.wait_ge(evacuated, st["g0"] + st["groups"])
            for a in range(2):
                pool.memset(n_vbd[a][:, :, :, :], 0.0).then_inc(lay_clear, 1)
            pool_rope(pool, st, n_q, n_qr, [n_kv[:, 2:3, :], n_kv[:, 4:5, :]])
            pool.wait_ge(rope_ready, 2 + st["rope"] + 10)
            pool.wait_ge(lay_clear, 4)
            for a in range(2):
                for grp in range(2):
                    rows = slice(HD * grp, HD * grp + HD)
                    pool.tensor_copy(n_kbd[a][rows, :, grp, :], n_kv[rows, 2 + 2 * a, 0:NP_TOK].rearrange("p (c j) -> p c j", c=2))\
                        .then_inc(nk_ready, 1)
                pool.wait_ge(nk_ready, 2 * a + 2)
            pool.wait_ge(win_landed, 32)

            def stage_queries(V, u, c, t):
                pool.wait_ge(ns_ready, V - 2)
                if c is not None:
                    rows = slice(P * c, P * c + P)
                    pool.tensor_copy(n_qst[:, u, 0, :], queries(n_q, t, rows))
                    pool.tensor_copy(n_qst[:, u, 1, :], queries(n_qr, t, rows)).then_inc(nq_staged, 1)
                    return
                for a, q in enumerate((n_q, n_qr)):
                    pool.tensor_tensor(n_qst[:, u, a, :].rearrange("p (g t s) -> p g t s", g=2, s=NQ), sample_queries(q, t),
                                       cst("bd").rearrange("p (g t s) -> p g t s", g=2, s=NQ), ALU.mult)
                pool.wait_ge(no_ready, V - 2)
                pool.tensor_copy(n_vst[:, u, :], one(n_wv, t)).then_inc(nq_staged, 1)

            for c in (0, 1, None):
                with pool.Fori(0, 4) as i:
                    for u in range(2):
                        base = PRIME + (16 if c is None else 8 * c)
                        stage_queries(base + u + 1 + 2 * i, u, c, 2 * i + u)

        mix_stored = {k: sem(k + "_stored") for k in ("cm", "swa", "sc", "nsa") if k in kinds}
        sp_after, sp_store = {}, {}
        pe_stage = {"ffn_in": pe_in, "ffn_out": pe_ffn_out, "mix_out": pe_mix_out}
        act_stage = {"ffn_in": act_ffn_in, "ffn_out": act_ffn_out, "mix_out": act_mix_out}
        dve_stage = {"ffn_in": dve_ffn_in, "ffn_out": dve_ffn_out, "mix_out": dve_mix_out}
        pool_stage = {"ffn_in": pool_ffn_in, "ffn_out": pool_out, "mix_out": pool_out}
        if "cm" in kinds:
            sp_after["cm_in"], sp_store["cm"] = sp_cm_load, sp_cm_store
            pe_stage["cm_in"], act_stage["cm_in"], dve_stage["cm_in"], pool_stage["cm_in"] = pe_cm, act_cm_in, dve_cm_in, pool_cm_in
        if "swa" in kinds:
            sp_after["swa_in"], sp_store["swa"] = sp_swa_load, sp_swa_store
            pe_stage["swa_in"], act_stage["swa_in"], dve_stage["swa_in"], pool_stage["swa_in"] = pe_swa, act_swa, dve_swa, pool_swa
        if "sc" in kinds:
            sp_store["sc"] = sp_sc_store
            pe_stage["sc_in"], act_stage["sc_in"], dve_stage["sc_in"], pool_stage["sc_in"] = pe_in, act_sc_in, dve_sc_in, pool_sc_in
        if "nsa" in kinds:
            sp_after["nsa_in"], sp_store["nsa"] = sp_nsa_load, sp_nsa_store
            pe_stage["nsa_in"], act_stage["nsa_in"], dve_stage["nsa_in"], pool_stage["nsa_in"] = pe_nsa, act_nsa, dve_nsa, pool_nsa


        def kind_of(name):
            return next((st for st in stages if st["kind"] == name), None)

        cm_st, sc_st, swa_st, nsa_st = (kind_of(k + "_in") for k in ("cm", "sc", "swa", "nsa"))
        block = ctx.enter_context(nc.Block())

        def guard(engine, st):
            at = stages.index(st)
            if at and stages[at - 1]["kind"] == "mix_out":
                engine.wait_ge(mix_stored[stages[at - 1]["mixer"]], 16)

        @block.sync
        def _(sp):
            sp.dma_start(const[:, :], A["const"]).then_inc(const_landed, 16)
            sp.dma_start(gains[:, :, :], A["gains"]).then_inc(const_landed, 16)
            sp.dma_start(x[:, :, :], A["x_t"]).then_inc(x_landed, 16)
            if "sc" in kinds:
                sp_sc_load(sp)
            if "nsa" in kinds:
                sp_past_first(sp)
            for n in range(RAW):
                sp_chunk(sp, n)
            if "nsa" in kinds:
                sp_past_rest(sp)
            for st in stages:
                sp_stream(sp, st)
                if st["kind"] in sp_after:
                    sp_after[st["kind"]](sp)
                if st["kind"] == "mix_out":
                    sp_store[st["mixer"]](sp)
            sp.wait_ge(y_ready, KT)
            sp.dma_start(O["y_t"], x[:, :, :]).then_inc(stored, 16)
            sp.wait_ge(stored, 16)
            for s in mix_stored.values():
                sp.wait_ge(s, 16)
            if "swa" in kinds:
                sp.wait_ge(swa_passed, 16)
            if "nsa" in kinds:
                sp.wait_ge(win_passed, 16)

        @block.tensor
        def _(pe):
            for name in pe_primed:
                pe.nop().then_inc(name, PRIME)
            pe.wait_ge(const_landed, 32)
            if "nsa" in kinds:
                pe_past(pe)
            for st in stages:
                pe_stage[st["kind"]](pe, st)
            pe_final(pe)

        @block.scalar
        def _(act):
            act.nop().then_inc(silu_ready, 2)
            act.nop().then_inc(hhi_ready, 2)
            if "cm" in kinds:
                act.nop().then_inc(gelu_ready, 2)
            for name in act_primed:
                act.nop().then_inc(name, PRIME)
            act_x_in(act)
            for n in range(RAW):
                act_split(act, n)
            if "nsa" in kinds:
                act_past(act)
            for st in stages:
                if st["kind"] == "ffn_in":
                    guard(act, st)
                act_stage[st["kind"]](act, st)
            act_std(act, final_norm)

        @block.vector
        def _(dve):
            if kinds & {"swa", "nsa"}:
                dve.nop().then_inc(rot_sin, 2)
            for name in dve_primed:
                dve.nop().then_inc(name, PRIME)
            dve_x_in(dve)
            for n in range(RAW):
                dve_split(dve, n)
            for st in stages:
                dve_stage[st["kind"]](dve, st)
            dve_final(dve)

        @block.gpsimd
        def _(pool):
            pool.nop().then_inc(prod_ready, 2)
            pool.nop().then_inc(hlo_ready, 2)
            if kinds & {"swa", "nsa"}:
                pool.nop().then_inc(rope_ready, 2)
            for name in pool_primed:
                pool.nop().then_inc(name, PRIME)
            pool_x_in(pool)
            for st in stages:
                if st["kind"] == "ffn_in":
                    guard(pool, st)
                pool_stage[st["kind"]](pool, st)


def feature_major(a):
    return np.ascontiguousarray(a.reshape(a.shape[0], -1, P).transpose(2, 1, 0))


def chunks_of(w, k0=0, k=KT):
    c = w[P * k0:P * (k0 + k)].reshape(k, P, -1, CW).transpose(2, 1, 0, 3)
    out = np.zeros((c.shape[0], P, KT, CW), w.dtype)
    out[:, :, 0:k] = c
    return out.reshape(c.shape[0], P, KT * CW)


def lay_out(inputs, schedule):
    v = {k: np.asarray(a) for k, a in inputs.items()}
    ins = {"const": CONST}
    heads = np.concatenate([np.arange(HD * q, HD * q + HD) for q in HEAD_ORDER])
    mixers = {"cm": 0, "swa": 1, "sc": 2, "nsa": 3}
    stream, norms = [], []
    for s in schedule:
        if s[0] == "ffn":
            w_in, w_out = v["ffn_in"][s[1], s[2]], v["ffn_out"][s[1], s[2]]
            gate, up = chunks_of(w_in[:, :FF]), chunks_of(w_in[:, FF:])
            stream.append(np.stack([gate, up], 1).reshape(-1, P, KT * CW))
            stream.append(np.stack([chunks_of(w_out, 0), chunks_of(w_out, 8), chunks_of(w_out, 16, 6)], 1)
                          .reshape(-1, P, KT * CW))
            norms.append(v["norm_g"][s[1], 2 * s[2]])
            continue
        norms.append(v["norm_g"][mixers[s[0]], 1])
        if s[0] == "cm":
            stream += [chunks_of(v["cm_w_in"]), chunks_of(v["cm_w_out"])]
        elif s[0] == "swa":
            w = v["swa_w_qkv"]
            stream += [chunks_of(w[:, heads]), chunks_of(w[:, D:]), chunks_of(v["swa_w_o"][heads])]
        elif s[0] == "sc":
            w = chunks_of(v["sc_w_in"]).reshape(3, 4, P, KT * CW).transpose(1, 0, 2, 3).reshape(12, P, KT * CW)
            stream += [w, chunks_of(v["sc_w_out"])]
        else:
            w = v["nsa_w_in"]
            gates = np.concatenate([w[:, D + 768:], np.zeros((D, CW - 48), w.dtype)], 1)
            stream += [chunks_of(w[:, heads]), chunks_of(w[:, D:D + 768]), chunks_of(gates), chunks_of(v["nsa_w_o"][heads])]
    norms.append(v["final_norm_g"])
    ins["stream"] = np.concatenate(stream, 0)
    gains = np.zeros((P, 14, KT), np.float32)
    for n, a in enumerate(norms):
        gains[:, n] = a.reshape(KT, P).T
    gains[:, 13] = v["cm_norm_g"].reshape(KT, P).T
    ins["gains"] = gains
    ins["x_t"] = feature_major(np.concatenate([v["x_prompt"][0], v["x_sample"].reshape(NS_TOK, D)], 0))
    ins["ws_t"] = np.ascontiguousarray(v["cm_w_s"].transpose(2, 0, 1))
    ws_s = np.zeros((NS_TOK, 4, NS_TOK), np.float32)
    for b in range(NB):
        ws_s[NQ * b:NQ * b + NQ, :, NQ * b:NQ * b + NQ] = v["cm_w_s"][:, :NQ, :NQ].transpose(2, 0, 1)
    ins["ws_s_t"] = ws_s
    ins["bs"] = np.concatenate([v["cm_b_s"], v["cm_b_s"]] + [v["cm_b_s"][:, :NQ]] * NB, 1)[None]
    ins["conv_w"] = np.ascontiguousarray(v["sc_conv_w"].reshape(3, KT, P).transpose(2, 0, 1))
    ins["conv_prev"] = feature_major(v["state_conv"].reshape(2 * NB, D))
    for name, cache in (("swa", v["cache_swa_kv"]), ("win", v["cache_nsa_win_kv"])):
        kv = cache.reshape(NB, P, 2, P)
        ins[name + "_k"] = np.ascontiguousarray(kv[:, :, 0].transpose(2, 0, 1))
        ins[name + "_v"] = np.ascontiguousarray(kv[:, :, 1].transpose(1, 0, 2))
        ins[name + "_old"] = np.ascontiguousarray(cache.reshape(NB, P, 2 * P))
    sinks = v["swa_sinks"]
    ins["sinks"] = np.concatenate([np.tile(sinks[None], (P, 1)), np.repeat(sinks, NQ)[:, None]], 1)
    pool = v["cache_nsa_kv"]
    n_pool = pool.shape[0]
    pairs = pool[:, :, 0:2].reshape(n_pool, N_PAIR, 2, 2, 2, HD).transpose(0, 2, 5, 3, 4, 1)
    ins["pool_cmp"] = np.ascontiguousarray(pairs.reshape(n_pool, P, 2 * P))
    k_t = pool[:, :, 2].reshape(n_pool, P, P).transpose(0, 2, 1)
    ins["pool_sel"] = np.concatenate([k_t, pool[:, :, 3].reshape(n_pool, P, P)], 2)
    ins["pages"] = np.ascontiguousarray(v["page_table"].reshape(1, -1))
    ins["cmp_w1"] = np.ascontiguousarray(v["nsa_cmp_w1"].reshape(2, 16, P, 256).transpose(2, 0, 1, 3))
    ins["cmp_pe"] = np.ascontiguousarray(v["nsa_cmp_pe"].reshape(2, 16, P).transpose(2, 0, 1))
    w2 = np.zeros((P, 2, 2, 2, P), np.float32)
    for grp in range(2):
        w2[:, :, :, grp, HD * grp:HD * grp + HD] = v["nsa_cmp_w2"].reshape(2, 2, P, HD).transpose(2, 0, 1, 3)
    ins["cmp_w2"] = w2
    return ins


OUTS = {
    "y_t": (P, KT, T), "cm_v": (P, KT, NS_TOK), "conv_end": (P, KT, 2 + 2 * NB), "swa_kv": (P, 2, T),
    "swa_passed": (NB, P - NQ, 2 * P), "nsa_kv": (P, 6, T), "win_passed": (NB, P - NQ, 2 * P),
}


def assemble(got):
    def rows(a):
        return a.transpose(2, 1, 0).reshape(a.shape[2], -1)

    y = rows(got["y_t"])
    out = [y[:NP_TOK].reshape(1, NP_TOK, D), y[NP_TOK:].reshape(NB, NQ, D),
           rows(got["cm_v"]).reshape(NB, NQ, D)]
    swa = rows(got["swa_kv"])
    out.append(swa[NP_TOK - P:NP_TOK].reshape(1, P, 2, 2, HD))
    out.append(np.concatenate([got["swa_passed"], swa[NP_TOK:].reshape(NB, NQ, 2 * P)], 1).reshape(NB, P, 2, 2, HD))
    end = rows(got["conv_end"])
    out += [end[0:2].reshape(1, 2, D), end[2:].reshape(NB, 2, D)]
    nsa = rows(got["nsa_kv"])
    out += [nsa[:NP_TOK, :4 * P].reshape(1, NP_TOK, 4, 2, HD), nsa[NP_TOK:, :4 * P].reshape(NB, NQ, 4, 2, HD)]
    win = nsa[:, 4 * P:]
    out.append(win[NP_TOK - P:NP_TOK].reshape(1, P, 2, 2, HD))
    out.append(np.concatenate([got["win_passed"], win[NP_TOK:].reshape(NB, NQ, 2 * P)], 1).reshape(NB, P, 2, 2, HD))
    return tuple(np.ascontiguousarray(a) for a in out)


def kernel(**inputs):
    import concourse.bacc as bacc
    from concourse.bass_utils import run_bass_kernel_spmd

    nc = bacc.Bacc("TRN2", target_bir_lowering=False, num_devices=1)
    arrays = lay_out(inputs, SCHEDULE)
    A = {n: nc.dram_tensor(n, a.shape, mybir.dt.from_np(a.dtype), kind="ExternalInput").ap() for n, a in arrays.items()}
    O = {n: nc.dram_tensor("out_" + n, s, F32, kind="ExternalOutput").ap() for n, s in OUTS.items()}
    program(nc, A, O, SCHEDULE)
    results = run_bass_kernel_spmd(nc, [arrays], core_ids=[0]).results[0]
    return assemble({n: results["out_" + n] for n in OUTS})
```

```python
from contextlib import ExitStack

import numpy as np

import concourse.bass as bass
from concourse import mybir

F32 = mybir.dt.float32
F32R = mybir.dt.float32r
I32 = mybir.dt.int32
ACT = mybir.ActivationFunctionType
ALU = mybir.AluOpType
AX = mybir.AxisListType

P = 128
D = 1024
KT = D // P
NP_TOK = 256
NS_TOK = 64
T = NP_TOK + NS_TOK
NB, NQ = 8, 8
FF = 2816
FT = FF // P
CW = 256
EPS = 1e-6
HD = 64
SCALE = HD ** -0.5
PAST = 1024
PAGE = 128
NPAGES = PAST // PAGE
NEG = -1e30
RAW = 2
HALVES = 2 * RAW
BANKS = 4
N_CMP_P = 15
N_CMP_S = 63
PRIME = 4


def const_tables():
    c = {}
    eye = np.eye(P, dtype=np.float32)
    c["ident"] = eye
    c["ones"] = np.ones((P, P), np.float32)
    perm = np.zeros((P, P), np.float32)
    for blk in range(2):
        for d in range(32):
            perm[64 * blk + 32 + d, 64 * blk + d] = -1.0
            perm[64 * blk + d, 64 * blk + 32 + d] = 1.0
    c["perm"] = perm
    half = 32
    inv = np.power(np.float32(10000.0), -np.arange(half, dtype=np.float32) / np.float32(half)).astype(np.float32)
    pos = np.concatenate([np.arange(NP_TOK), np.tile(PAST + np.arange(NQ), NB)]).astype(np.float32)
    ang = (pos[None, :] * inv[:, None]).astype(np.float32)
    c["cos"] = np.tile(np.cos(ang), (4, 1)).astype(np.float32)
    c["sin"] = np.tile(np.sin(ang), (4, 1)).astype(np.float32)
    i = np.arange(P)[:, None]
    j = np.arange(P)[None, :]
    causal = np.where(j <= i, 0.0, NEG)
    prev = np.where(j >= i, 0.0, NEG)
    c["m_band"] = np.concatenate([prev, prev, causal, causal], 1)
    s = np.arange(P)[:, None] % NQ
    c["m_old"] = np.where(j >= s, 0.0, NEG)
    k = np.arange(NS_TOK)[None, :]
    c["m_new"] = np.concatenate([np.where((k // NQ == b) & (k % NQ <= s), 0.0, NEG) for b in range(NB)], 1)
    ok = 16 * (np.arange(40)[None, :] - 8) + 31 <= i
    c["m_cmp"] = np.where(ok, 0.0, NEG)
    c["ok_cmp"] = np.where(ok, 1.0, 0.0)
    c["sum_r"] = ((i // 64 == j // 64) & (i % NQ == j % NQ)).astype(np.float32)
    c["bd"] = (i // 64 == j // 64).astype(np.float32)
    c["blk_no"] = np.tile(np.arange(16, dtype=np.float32)[None, :], (P, 1))
    c["tri"] = (i <= j).astype(np.float32)
    r = np.arange(P)
    head_of = 8 * (r // 64) + (r % 64) // NQ
    c["row_of"] = np.concatenate([np.where(np.arange(P)[:, None] == 16 * k + head_of[None, :], 1.0, 0.0) for k in range(3)], 1)
    c["tok_of"] = (np.arange(NS_TOK)[None, :] % NQ == (r % NQ)[:, None]).astype(np.float32)
    c["eps"] = np.full((P, 1), EPS, np.float32)
    at, cols, parts = 0, {}, []
    for name, a in c.items():
        cols[name] = (at, a.shape[1])
        at += a.shape[1]
        parts.append(a.astype(np.float32))
    return np.concatenate(parts, 1), cols


CONST, COLS = const_tables()


HEAD_ORDER = [h * 8 + t for t in range(8) for h in range(2)]
SCHEDULE = [("ffn", 0, 0), ("cm",), ("ffn", 0, 1), ("ffn", 1, 0), ("swa",), ("ffn", 1, 1),
            ("ffn", 2, 0), ("sc",), ("ffn", 2, 1), ("ffn", 3, 0), ("nsa",), ("ffn", 3, 1)]
N_PAIR = PAGE // 2


def program(nc, A, O, schedule):
    ctx = ExitStack()
    with ctx:
        def sem(name):
            return ctx.enter_context(nc.semaphore(name))

        kinds = {s[0] for s in schedule}
        BASE = (nc.sbuf_base + 63) // 64 * 64
        top = [0]

        def sb(name, shape, dt=F32):
            at = top[0]
            top[0] = (at + int(np.prod(shape[1:])) * 4 + 63) // 64 * 64
            assert BASE + top[0] <= nc.sbuf_usable_end, (name, top[0])
            return nc.alloc_sbuf_tensor_at(name, list(shape), dt, offset=BASE + at)

        raw = sb("w_raw", [P, RAW, KT, CW])
        w_hi = sb("w_hi", [P, HALVES, KT, P], F32R)
        w_lo = sb("w_lo", [P, HALVES, KT, P], F32R)
        x = sb("x", [P, KT, T])
        XH_AT = top[0]
        x_hi = sb("x_hi", [P, KT, T], F32R)
        XL_AT = top[0]
        x_lo = sb("x_lo", [P, KT, T], F32R)
        CONST_AT = top[0]
        const = sb("const", [P, CONST.shape[1]])
        gains = sb("gains", [P, 14, KT])
        ssum = sb("ssum", [P, T])
        sq = sb("sq", [P, T])
        std = sb("std", [P, T])
        rstd = sb("rstd", [P, T])
        GATE_AT = top[0]
        gate_in = sb("gate_in", [P, 2, T])
        SILU_AT = top[0]
        silu = sb("silu", [P, 2, T])
        UP_AT = top[0]
        up = sb("up", [P, 2, T])
        HIN_AT = top[0]
        h = sb("h", [P, 2, T])
        kcmp_s = sb("kcmp_s", [P, NB, 64])
        pages = sb("page_table", [1, NB * NPAGES], I32)
        vcmp_s = sb("vcmp_s", [64, NB, P])
        cmp_bias = sb("cmp_bias", [P, 2, 2])
        w2z = sb("w2z", [P, 2, 2, 2, P])
        cmp_pe = sb("cmp_pe", [P, 2, 16])
        sc_w = sb("sc_w", [P, 3, KT])
        sc_prev = sb("sc_prev", [P, KT, 2 * NB])
        H_AT = top[0]
        h_hi = sb("h_hi", [P, FT, T], F32R)
        HL_AT = top[0]
        h_lo = sb("h_lo", [P, FT, T], F32R)
        END = top[0]
        bank = [ctx.enter_context(nc.psum_tensor(f"bank{i}", [P, 512], F32)) for i in range(8)]

        class Area:

            def __init__(self):
                kept = KT * T * 4
                self.free = [[END, nc.sbuf_usable_end - BASE], [H_AT + kept, HL_AT], [HL_AT + kept, END]]

            def __call__(self, name, shape, dt=F32):
                size = (int(np.prod(shape[1:])) * 4 + 63) // 64 * 64
                fit = [r for r in self.free if r[1] - r[0] >= size]
                assert fit, (name, size, self.free)
                r = min(fit, key=lambda r: r[1] - r[0])
                at = r[0]
                r[0] += size
                return nc.alloc_sbuf_tensor_at(name, list(shape), dt, offset=BASE + at)

        LIMIT = nc.sbuf_usable_end - BASE

        class Space:

            def __init__(self, at, end):
                self.at, self.end = at, end

            def __call__(self, name, shape, dt=F32):
                at = self.at
                self.at = (at + int(np.prod(shape[1:])) * 4 + 63) // 64 * 64
                assert self.at <= self.end, (name, self.at - self.end)
                return nc.alloc_sbuf_tensor_at(name, list(shape), dt, offset=BASE + at)

        gate_silu_space, up_space, h_space = Space(GATE_AT, UP_AT), Space(UP_AT, HIN_AT), Space(HIN_AT, HIN_AT + 2 * T * 4)

        def cst(name):
            a, n = COLS[name]
            return const[:, a:a + n]

        const_landed = sem("const_landed")
        x_landed = sem("x_landed")
        raw_landed = [sem(f"raw_landed{s}") for s in range(RAW)]
        hi_ready = sem("hi_ready")
        lo_ready = sem("lo_ready")
        half_used = sem("half_used")
        evacuated = sem("evacuated")
        xhi_ready = sem("xhi_ready")
        xlo_ready = sem("xlo_ready")
        ssum_step = sem("ssum_step")
        stat_ready = sem("stat_ready")
        std_ready = sem("std_ready")
        rstd_ready = sem("rstd_ready")
        silu_ready = sem("silu_ready")
        prod_ready = sem("prod_ready")
        hhi_ready = sem("hhi_ready")
        hlo_ready = sem("hlo_ready")
        y_ready = sem("y_ready")
        stored = sem("stored")

        stages = []
        n_norm = n_ffn = g = n_chunks = 0

        def stage(kind, chunks, groups, **more):
            nonlocal g, n_chunks
            stages.append(dict(kind=kind, n0=n_chunks, g0=g, chunks=chunks, groups=groups, norm=n_norm, **more))
            n_chunks += chunks
            g += groups

        IN_CHUNKS = {"cm": 8, "swa": 5, "sc": 12, "nsa": 8}
        for s in schedule:
            if s[0] == "ffn":
                stage("ffn_in", FT, 2 * FT, ffn=n_ffn)
                n_norm += 1
                stage("ffn_out", 3 * KT // 2, KT, ffn=n_ffn)
                n_ffn += 1
            else:
                n_in = IN_CHUNKS[s[0]]
                stage(s[0] + "_in", n_in, 2 * n_in)
                n_norm += 1
                stage("mix_out", KT // 2, KT, mixer=s[0])
        final_norm = n_norm
        narrow = {st["n0"] + 3 for st in stages if st["kind"] == "nsa_in"}

        def landed(n):
            return 16 * (n // RAW + 1)

        def sp_chunk(sp, n, i=0, step=0, k=KT):
            if n >= RAW:
                sp.wait_ge(lo_ready, 2 * n - 2 * RAW + 2 + 2 * step * i)
            src = A["stream"][bass.ds(n + step * i, 1)] if step else A["stream"][n:n + 1]
            sp.dma_start(raw[:, n % RAW, 0:k, :].rearrange("p k n -> p (k n)"),
                         src.rearrange("a p n -> p (a n)")[:, 0:k * CW]).then_inc(raw_landed[n % RAW], 16)

        def sp_stream(sp, st):
            n0, chunks = st["n0"], st["chunks"]
            if st["kind"] == "ffn_out":
                with sp.Fori(0, 2) as i:
                    for c in range(6):
                        sp_chunk(sp, n0 + c, i, 6, k=(8, 8, 6)[c % 3])
                return
            peel = RAW if n0 == 0 else 0
            with sp.Fori(0, (chunks - peel) // 2) as i:
                for c in range(2):
                    sp_chunk(sp, n0 + peel + c, i, 2)
            if chunks % 2:
                sp_chunk(sp, n0 + chunks - 1)

        def act_split(act, n, i=0, step=0, k=KT):
            act.wait_ge(raw_landed[n % RAW], landed(n) + 16 * (step // RAW) * i)
            one = n in narrow and not step
            for half in range(1 if one else 2):
                if n >= RAW:
                    act.wait_ge(half_used, 2 * n + half + 1 - HALVES + 2 * step * i)
                act.activation(w_hi[:, (2 * n + half) % HALVES, 0:k, :],
                               raw[:, n % RAW, 0:k, P * half:P * half + P], ACT.Copy).then_inc(hi_ready, 2 if one else 1)

        def dve_split(dve, n, i=0, step=0, k=KT):
            one = n in narrow and not step
            for half in range(1 if one else 2):
                s = (2 * n + half) % HALVES
                dve.wait_ge(hi_ready, 2 * n + half + 1 + 2 * step * i)
                dve.tensor_tensor(w_lo[:, s, 0:k, :], raw[:, n % RAW, 0:k, P * half:P * half + P],
                                  w_hi[:, s, 0:k, :].bitcast(F32), ALU.subtract).then_inc(lo_ready, 2 if one else 1)

        def pe_half(pe, n, half, g, act_hi, act_lo, k0=0, k=KT, i=0, step=0, gstep=0, first=True, last=True,
                    operand=None):
            s = (2 * n + half) % HALVES
            acc = bank[g % BANKS][:, 0:T]
            pe.wait_ge(lo_ready, 2 * n + half + 1 + 2 * step * i)
            if first and g >= BANKS:
                pe.wait_ge(evacuated, g + 1 - BANKS + gstep * i)
            for kk in range(k):
                if operand:
                    operand(kk)
                for w, a in ((w_hi, act_hi), (w_lo, act_hi), (w_hi, act_lo)):
                    mm = pe.matmul(acc, w[:, s, kk, :], a[:, k0 + kk, :],
                                   start=(first and kk == 0 and w is w_hi and a is act_hi),
                                   stop=(last and kk == k - 1 and a is act_lo))
            return mm

        def pe_norm(pe, norm):
            pe.wait_ge(ssum_step, 17 * norm + 17)
            if norm:
                pe.wait_ge(std_ready, norm)
            pe.matmul(bank[4][:, 0:T], cst("ones"), ssum[:, :], start=True, stop=True).then_inc(stat_ready, 1)

        def pe_in(pe, st):
            n0, g0, norm = st["n0"], st["g0"], st["norm"]

            def chunk(c, i=0, operand=None):
                one = n0 + c in narrow
                for half in range(1 if one else 2):
                    n, g = n0 + c, g0 + 2 * c + half
                    mm = pe_half(pe, n, half, g, x_hi, x_lo, i=i, step=2, gstep=4, operand=operand if half == 0 else None)
                    mm.then_inc(half_used, 2 if one else 1)

            chunk(0, operand=lambda k: pe.wait_ge(xlo_ready, KT * norm + k + 1))
            pe_norm(pe, norm)
            chunk(1)
            full = (st["chunks"] - (n0 + st["chunks"] - 1 in narrow)) // 2
            with pe.Fori(1, full) as i:
                chunk(0, i)
                chunk(1, i)
            for c in range(2 * full, st["chunks"]):
                chunk(c)

        def pe_ffn_out(pe, st):
            n0, g0 = st["n0"], st["g0"]
            base = 2 + FT * st["ffn"]

            def body(i):
                for c in range(6):
                    k0, k = 8 * (c % 3), (8, 8, 6)[c % 3]
                    for half in range(2):
                        pe_half(pe, n0 + c, half, g0 + 2 * (c // 3) + half, h_hi, h_lo, k0, k, i=i, step=6, gstep=4,
                                first=c % 3 == 0, last=c % 3 == 2,
                                operand=(lambda kk, k0=k0: pe.wait_ge(hlo_ready, base + k0 + kk + 1)) if half == 0 else None)\
                            .then_inc(half_used, 1)

            with pe.Fori(0, 2) as i:
                body(i)

        def act_std(act, norm):
            act.wait_ge(stat_ready, norm + 1)
            if norm:
                act.wait_ge(rstd_ready, norm)
            act.activation(std[:, :], bank[4][:, 0:T], ACT.Sqrt, bias=cst("eps"), scale=1.0 / D).then_inc(std_ready, 1)

        def act_x_hi(act, norm, m):
            act.activation(x_hi[:, bass.ds(m, 1), :], x[:, bass.ds(m, 1), :], ACT.Copy,
                           scale=gains[:, norm, bass.ds(m, 1)]).then_inc(xhi_ready, 1)

        def act_ffn_in(act, st):
            n0, g0 = st["n0"], st["g0"]
            base = FT * st["ffn"]
            act_std(act, st["norm"])
            with act.Fori(0, FT // 2) as i:
                act_split(act, n0 + 2, i, 2)
                for f in range(2):
                    act.wait_ge(evacuated, g0 + f + 1 + 4 * i)
                    act.wait_ge(prod_ready, base + f + 1 + 2 * i)
                    act.activation(silu[:, f, :], gate_in[:, f, :], ACT.Silu).then_inc(silu_ready, 1)
                act_split(act, n0 + 3, i, 2)
                for f in range(2):
                    act.wait_ge(prod_ready, base + f + 3 + 2 * i)
                    act.activation(h_hi[:, bass.ds(2 * i + f, 1), :], h[:, f:f + 1, :], ACT.Copy).then_inc(hhi_ready, 1)

        def act_ffn_out(act, st):
            n0, g0, norm = st["n0"], st["g0"], st["norm"]
            final = norm == final_norm

            def body(i, c):
                if c % 3 == 2 and not final:
                    for f in range(2):
                        m = 2 * (c // 3) + f
                        act.wait_ge(evacuated, g0 + m + 1 + 4 * i)
                        act_x_hi(act, norm, m + 4 * i)
                if not final or n0 + c + RAW + 6 * i < n_chunks:
                    act_split(act, n0 + c + 2, i, 6, k=(8, 8, 6)[(c + 2) % 3])

            if final:
                for i in range(2):
                    for c in range(6):
                        body(i, c)
            else:
                with act.Fori(0, 2) as i:
                    for c in range(6):
                        body(i, c)

        def dve_rstd(dve, norm):
            dve.wait_ge(std_ready, norm + 1)
            dve.reciprocal(rstd[:, :], std[:, :]).then_inc(rstd_ready, 1)
            dve.wait_ge(rstd_ready, norm + 1)

        def dve_x_lo(dve, norm, m):
            dve.scalar_tensor_tensor(out=x_lo[:, bass.ds(m, 1), :], in0=x[:, bass.ds(m, 1), :],
                                     scalar=gains[:, norm, bass.ds(m, 1)], in1=x_hi[:, bass.ds(m, 1), :].bitcast(F32),
                                     op0=ALU.mult, op1=ALU.subtract).then_inc(xlo_ready, 1)

        def dve_take(dve, n, g, dst, i=0, step=0, gstep=0):
            dve.wait_ge(half_used, 2 * n + g % 2 + 1 + 2 * step * i)
            dve.tensor_tensor(dst, bank[g % BANKS][:, 0:T], rstd[:, :], ALU.mult).then_inc(evacuated, 1)

        def dve_ffn_in(dve, st):
            n0, g0 = st["n0"], st["g0"]
            base = FT * st["ffn"]
            dve_rstd(dve, st["norm"])
            with dve.Fori(0, FT // 2) as i:
                for f in range(2):
                    dve.wait_ge(silu_ready, base + f + 1 + 2 * i)
                    dve_take(dve, n0, g0 + f, gate_in[:, f, :], i, 2, 4)
                dve_split(dve, n0 + 2, i, 2)
                for f in range(2):
                    dve.wait_ge(prod_ready, base + f + 1 + 2 * i)
                    dve_take(dve, n0 + 1, g0 + 2 + f, up[:, f, :], i, 2, 4)
                dve_split(dve, n0 + 3, i, 2)

        def dve_add_x(dve, n, g, m, scale, i=0, step=0):
            dve.wait_ge(half_used, 2 * n + g % 2 + 1 + 2 * step * i)
            xm = x[:, bass.ds(m, 1), :]
            dve.scalar_tensor_tensor(out=xm, in0=bank[g % BANKS][:, 0:T].rearrange("p (a t) -> p a t", a=1),
                                     scalar=scale, in1=xm, op0=ALU.mult, op1=ALU.add).then_inc(evacuated, 1)

        def dve_ffn_out(dve, st):
            n0, g0, norm = st["n0"], st["g0"], st["norm"]
            final = norm == final_norm

            def body(i, c):
                if c % 3 == 2:
                    for f in range(2):
                        m = 2 * (c // 3) + f
                        dve_add_x(dve, n0 + c, g0 + m, m + 4 * i, 0.5, i, 6)
                    for f in range(2 * (not final)):
                        m = 2 * (c // 3) + f
                        dve.wait_ge(evacuated, g0 + m + 1 + 4 * i)
                        dve.wait_ge(xhi_ready, KT * norm + m + 1 + 4 * i)
                        dve_x_lo(dve, norm, m + 4 * i)
                if not final or n0 + c + RAW + 6 * i < n_chunks:
                    dve_split(dve, n0 + c + 2, i, 6, k=(8, 8, 6)[(c + 2) % 3])

            if final:
                for i in range(2):
                    for c in range(6):
                        body(i, c)
            else:
                with dve.Fori(0, 2) as i:
                    for c in range(6):
                        body(i, c)

        def pool_clear_ssum(pool, norm):
            if norm:
                pool.wait_ge(stat_ready, norm)
            pool.memset(ssum[:, :], 0.0).then_inc(ssum_step, 1)

        def pool_square(pool, norm, m):
            pool.wait_ge(ssum_step, 17 * norm + 1 + 2 * m)
            pool.tensor_tensor(sq[:, :].rearrange("p (a t) -> p a t", a=1), x[:, bass.ds(m, 1), :], x[:, bass.ds(m, 1), :],
                               ALU.mult).then_inc(ssum_step, 1)
            pool.wait_ge(ssum_step, 17 * norm + 2 + 2 * m)
            pool.tensor_tensor(ssum[:, :], ssum[:, :], sq[:, :], ALU.add).then_inc(ssum_step, 1)

        def pool_ffn_in(pool, st):
            g0 = st["g0"]
            base = FT * st["ffn"]
            with pool.Fori(0, FT // 2) as i:
                for f in range(2):
                    pool.wait_ge(evacuated, g0 + 2 + f + 1 + 4 * i)
                    pool.wait_ge(silu_ready, base + f + 3 + 2 * i)
                    pool.wait_ge(hlo_ready, base + f + 1 + 2 * i)
                    pool.tensor_tensor(h[:, f, :], silu[:, f, :], up[:, f, :], ALU.mult).then_inc(prod_ready, 1)
                for f in range(2):
                    pool.wait_ge(hhi_ready, base + f + 3 + 2 * i)
                    pool.wait_ge(prod_ready, base + f + 3 + 2 * i)
                    t = bass.ds(2 * i + f, 1)
                    pool.tensor_tensor(h_lo[:, t, :], h[:, f:f + 1, :], h_hi[:, t, :].bitcast(F32),
                                       ALU.subtract).then_inc(hlo_ready, 1)

        def pool_out(pool, st):
            g0, norm = st["g0"], st["norm"]
            pool_clear_ssum(pool, norm)
            with pool.Fori(0, KT) as m:
                pool.wait_ge(evacuated, g0 + 1 + m)
                pool_square(pool, norm, m)

        def act_x_in(act):
            act.wait_ge(const_landed, 32)
            act.wait_ge(x_landed, 16)
            for m in range(KT):
                act_x_hi(act, 0, m)

        def dve_x_in(dve):
            dve.wait_ge(const_landed, 32)
            dve.wait_ge(x_landed, 16)
            for m in range(KT):
                dve.wait_ge(xhi_ready, m + 1)
                dve_x_lo(dve, 0, m)

        def pool_x_in(pool):
            pool_clear_ssum(pool, 0)
            pool.wait_ge(x_landed, 16)
            for m in range(KT):
                pool_square(pool, 0, m)

        def pe_final(pe):
            pe.wait_ge(ssum_step, 17 * final_norm + 17)
            pe.wait_ge(std_ready, final_norm)
            pe.matmul(bank[4][:, 0:T], cst("ones"), ssum[:, :], start=True, stop=True).then_inc(stat_ready, 1)

        def dve_final(dve):
            dve_rstd(dve, final_norm)
            for m in range(KT):
                xm = x[:, m, :]
                dve.scalar_tensor_tensor(out=xm, in0=xm, scalar=gains[:, final_norm, m:m + 1], in1=rstd[:, :],
                                         op0=ALU.mult, op1=ALU.mult).then_inc(y_ready, 1)

        mixer_ready = sem("mixer_ready")
        n_mixer = 0
        for st in stages:
            st["mixer_base"] = KT * n_mixer
            n_mixer += st["kind"] == "mix_out"

        def pe_mix_out(pe, st):
            n0, g0 = st["n0"], st["g0"]

            def chunk(c, i=0, operand=None):
                for half in range(2):
                    pe_half(pe, n0 + c, half, g0 + 2 * c + half, h_hi, h_lo, i=i, step=2, gstep=4,
                            operand=operand if half == 0 else None).then_inc(half_used, 1)

            chunk(0, operand=lambda k: pe.wait_ge(mixer_ready, st["mixer_base"] + k + 1))
            chunk(1)
            with pe.Fori(1, 2) as i:
                chunk(0, i)
                chunk(1, i)

        def act_mix_out(act, st):
            n0, g0, norm = st["n0"], st["g0"], st["norm"]
            for c in range(KT // 2):
                for f in range(2):
                    m = 2 * c + f
                    act.wait_ge(evacuated, g0 + m + 1)
                    act_x_hi(act, norm, m)
                if n0 + c + RAW < n_chunks:
                    act_split(act, n0 + c + RAW)

        def dve_mix_out(dve, st):
            n0, g0, norm = st["n0"], st["g0"], st["norm"]
            for c in range(KT // 2):
                for f in range(2):
                    m = 2 * c + f
                    dve_add_x(dve, n0 + c, g0 + m, m, 1.0)
                for f in range(2):
                    m = 2 * c + f
                    dve.wait_ge(evacuated, g0 + m + 1)
                    dve.wait_ge(xhi_ready, KT * norm + m + 1)
                    dve_x_lo(dve, norm, m)
                if n0 + c + RAW < n_chunks:
                    dve_split(dve, n0 + c + RAW)


        if "cm" in kinds:
            area = Area()
            cm_u = area("cm_u", [P, KT, T])
            cm_v = area("cm_v", [P, KT, T])
            cm_vt = area("cm_vt", [P, 3, D])
            cm_ws = area("cm_ws", [P, 4, P])
            cm_ws_s = area("cm_ws_s", [NS_TOK, 4, NS_TOK])
            cm_bs = area("cm_bs", [P, 4, T])
            vsum = area("vsum", [P, T])
            vsq = area("vsq", [P, T])
            vstd = area("vstd", [P, T])
            vrstd = area("vrstd", [P, T])
            cm_landed = sem("cm_landed")
            gelu_ready = sem("gelu_ready")
            vsum_step = sem("vsum_step")
            vstat_ready = sem("vstat_ready")
            vstd_ready = sem("vstd_ready")
            vrstd_ready = sem("vrstd_ready")
            ws_ready = sem("ws_ready")
            vn_ready = sem("vn_ready")
            vt_turned = sem("vt_turned")
            vt_copied = sem("vt_copied")
            mixed_ready = sem("mixed_ready")
            cy_biased = sem("cy_biased")
            cy_ready = sem("cy_ready")
            cy_hi = sem("cy_hi")
            cm_banks = [7, 4]

        def sp_cm_load(sp):
            sp.wait_ge(evacuated, cm_st["g0"])
            for dst, name in ((cm_ws, "ws_t"), (cm_ws_s, "ws_s_t"), (cm_bs, "bs")):
                sp.dma_start(dst[:, :, :], A[name]).then_inc(cm_landed, 16)

        def sp_cm_store(sp):
            sp.wait_ge(vn_ready, KT)
            sp.dma_start(O["cm_v"], cm_v[:, :, NP_TOK:T]).then_inc(mix_stored["cm"], 16)

        def act_cm_in(act, st):
            n0, g0 = st["n0"], st["g0"]
            act_std(act, st["norm"])
            for part, dst in enumerate((cm_u, cm_v)):
                with act.Fori(0, 2) as i:
                    for c in range(2):
                        act_split(act, n0 + RAW + 4 * part + c, i, 2)
                        for f in range(2):
                            q = 8 * part + 2 * c + f
                            act.wait_ge(evacuated, g0 + q + 1 + 4 * i)
                            act.activation(dst[:, bass.ds(2 * c + f + 4 * i, 1), :], gate_in[:, f:f + 1, :],
                                           ACT.Gelu_apprx_tanh).then_inc(gelu_ready, 1)
            act.wait_ge(vstat_ready, 1)
            act.activation(vstd[:, :], bank[4][:, 0:T], ACT.Sqrt, bias=cst("eps"), scale=1.0 / D).then_inc(vstd_ready, 1)
            for m in range(KT):
                act.wait_ge(vt_turned, m + 1)
                src = bank[5 + m % 2]
                act.activation(cm_vt[:, 0:2, P * m:P * m + P], src[:, 0:2 * P].rearrange("p (c f) -> p c f", c=2), ACT.Copy)
                act.activation(cm_vt[0:NS_TOK, 2, P * m:P * m + P], src[0:NS_TOK, 2 * P:3 * P], ACT.Copy)\
                    .then_inc(vt_copied, 1)
            for m in range(KT):
                act.wait_ge(cy_ready, m + 1)
                act.activation(h_hi[:, m, :], up[:, m % 2, :], ACT.Copy).then_inc(cy_hi, 1)

        def dve_cm_in(dve, st):
            n0, g0 = st["n0"], st["g0"]
            dve_rstd(dve, st["norm"])
            for part in range(2):
                with dve.Fori(0, 2) as i:
                    for c in range(2):
                        for f in range(2):
                            q = 8 * part + 2 * c + f
                            dve.wait_ge(gelu_ready, q + 1 + 4 * i)
                            dve_take(dve, n0 + 4 * part + c, g0 + q, gate_in[:, f, :], i, 2, 4)
                        dve_split(dve, n0 + RAW + 4 * part + c, i, 2)
            dve.wait_ge(cm_landed, 48)
            dve.tensor_tensor(cm_ws[:, :, :], cm_ws[:, :, :],
                              cst("tri").rearrange("p (a j) -> p a j", a=1).broadcast_to([P, 4, P]), ALU.mult)\
                .then_inc(ws_ready, 1)
            dve.tensor_tensor(cm_ws_s[:, :, :], cm_ws_s[:, :, :],
                              cst("tri")[0:NS_TOK, 0:NS_TOK].rearrange("p (a j) -> p a j", a=1).broadcast_to([NS_TOK, 4, NS_TOK]),
                              ALU.mult).then_inc(ws_ready, 1)
            dve.wait_ge(vstd_ready, 1)
            dve.reciprocal(vrstd[:, :], vstd[:, :]).then_inc(vrstd_ready, 1)
            dve.wait_ge(vrstd_ready, 1)
            for m in range(KT):
                vm = cm_v[:, m, :]
                dve.scalar_tensor_tensor(out=vm, in0=vm, scalar=gains[:, 13, m:m + 1], in1=vrstd[:, :],
                                         op0=ALU.mult, op1=ALU.mult).then_inc(vn_ready, 1)
            for m in range(KT + 1):
                if m < KT:
                    y = up[:, m % 2, :]
                    dve.wait_ge(mixed_ready, m + 1)
                    if m >= 2:
                        dve.wait_ge(cy_hi, m - 1)
                        dve.wait_ge(mixer_ready, st["mixer_base"] + m - 1)
                    dve.tensor_tensor(y, bank[cm_banks[m % 2]][:, 0:T], cm_bs[:, m // 2, :], ALU.add).then_inc(cy_biased, 1)
                    dve.wait_ge(cy_biased, m + 1)
                    dve.tensor_tensor(y, y, cm_u[:, m, :], ALU.mult).then_inc(cy_ready, 1)
                if m:
                    dve.wait_ge(cy_ready, m)
                    dve.wait_ge(cy_hi, m)
                    dve.tensor_tensor(h_lo[:, m - 1, :], up[:, (m - 1) % 2, :], h_hi[:, m - 1, :].bitcast(F32), ALU.subtract)\
                        .then_inc(mixer_ready, 1)

        def pool_cm_in(pool, st):
            pool.wait_ge(evacuated, st["g0"])
            pool.memset(vsum[:, :], 0.0).then_inc(vsum_step, 1)
            with pool.Fori(0, KT) as m:
                pool.wait_ge(gelu_ready, 2 + 8 + 1 + m)
                pool.wait_ge(vsum_step, 1 + 2 * m)
                vm = cm_v[:, bass.ds(m, 1), :]
                pool.tensor_tensor(vsq[:, :].rearrange("p (a t) -> p a t", a=1), vm, vm, ALU.mult).then_inc(vsum_step, 1)
                pool.wait_ge(vsum_step, 2 + 2 * m)
                pool.tensor_tensor(vsum[:, :], vsum[:, :], vsq[:, :], ALU.add).then_inc(vsum_step, 1)

        def pe_cm(pe, st):
            pe_in(pe, st)
            pe.wait_ge(vsum_step, 17)
            pe.matmul(bank[4][:, 0:T], cst("ones"), vsum[:, :], start=True, stop=True).then_inc(vstat_ready, 1)
            for m in range(KT):
                pe.wait_ge(vn_ready, m + 1)
                if m >= 2:
                    pe.wait_ge(vt_copied, m - 1)
                for c in range(3):
                    w = P if c < 2 else NS_TOK
                    t = pe.transpose(bank[5 + m % 2][0:w, P * c:P * c + P], cm_v[:, m, P * c:P * c + w], cst("ident"))
                t.then_inc(vt_turned, 1)
            pe.wait_ge(ws_ready, 2)
            pe.wait_ge(evacuated, st["g0"] + st["groups"])
            for m in range(KT):
                pe.wait_ge(vt_copied, m + 1)
                if m >= 2:
                    pe.wait_ge(cy_biased, m - 1)
                grp, out = m // 2, bank[cm_banks[m % 2]]
                for c in range(2):
                    pe.matmul(out[:, P * c:P * c + P], cm_vt[:, c, P * m:P * m + P], cm_ws[:, grp, :], start=True, stop=True)
                pe.matmul(out[:, 2 * P:T], cm_vt[0:NS_TOK, 2, P * m:P * m + P], cm_ws_s[:, grp, :],
                          start=True, stop=True).then_inc(mixed_ready, 1)

        Z_COLS = 2 + NP_TOK + NB * (NQ + 2)
        if "sc" in kinds:
            area = Area()
            sc_b = area("sc_b", [P, KT, T])
            sc_z = area("sc_z", [P, KT, Z_COLS])
            sc_c = area("sc_c", [P, 2, T])
            sc_h = area("sc_h", [P, 2, T])
            sc_cv = area("sc_cv", [P, 2, Z_COLS])
            sc_y = area("sc_y", [P, 2, T])
            sc_end = area("sc_end", [P, KT, 2 + 2 * NB])
            sc_landed = sem("sc_landed")
            z_clear = sem("z_clear")
            z_ready = sem("z_ready")
            cv_step = sem("cv_step")
            sc_y_ready = sem("sc_y_ready")
            sc_hi = sem("sc_hi")
            sc_kept = sem("sc_kept")

        def sp_sc_load(sp):
            sp.dma_start(sc_w[:, :, :], A["conv_w"]).then_inc(sc_landed, 16)
            sp.dma_start(sc_prev[:, :, :], A["conv_prev"]).then_inc(sc_landed, 16)

        def sp_sc_store(sp):
            sp.wait_ge(sc_kept, 2)
            sp.dma_start(O["conv_end"], sc_end[:, :, :]).then_inc(mix_stored["sc"], 16)

        def act_sc_in(act, st):
            act_std(act, st["norm"])
            for c in range(st["chunks"] + 3):
                if c < st["chunks"]:
                    act_split(act, st["n0"] + RAW + c)
                if c >= 4 and c % 3 == 1:
                    for m in range(2 * (c // 3) - 2, 2 * (c // 3)):
                        act.wait_ge(sc_y_ready, m + 1)
                        act.activation(h_hi[:, m, :], sc_y[:, m % 2, :], ACT.Copy).then_inc(sc_hi, 1)

        def dve_sc_in(dve, st):
            n0, g0 = st["n0"], st["g0"]

            def convolve(m):
                cv = sc_cv[:, m % 2, 0:Z_COLS - 2]
                dve.wait_ge(z_ready, m + 1)
                if m >= 2:
                    dve.wait_ge(sc_y_ready, m - 1)
                for k in range(3):
                    zk = sc_z[:, m, k:k + Z_COLS - 2]
                    if k:
                        dve.wait_ge(cv_step, 3 * m + k)
                        op = dve.scalar_tensor_tensor(out=cv, in0=zk, scalar=sc_w[:, k, m:m + 1], in1=cv, op0=ALU.mult, op1=ALU.add)
                    else:
                        op = dve.tensor_scalar(cv, zk, sc_w[:, 0, m:m + 1], None, ALU.mult)
                    op.then_inc(cv_step, 1)

            dve_rstd(dve, st["norm"])
            for c in range(st["chunks"]):
                for f in range(2):
                    m, g = 2 * (c // 3) + f, g0 + 2 * c + f
                    if c % 3 and m >= 2:
                        dve.wait_ge(z_ready, m - 1)
                    dst = (sc_b[:, m:m + 1, :], sc_c[:, f:f + 1, :], sc_h[:, f:f + 1, :])[c % 3]
                    dve_take3(dve, n0 + c, f, g, dst)
                dve_split(dve, n0 + RAW + c)
                if c % 3 == 0 and c:
                    convolve(2 * (c // 3) - 2)
                    convolve(2 * (c // 3) - 1)
            convolve(KT - 2)
            convolve(KT - 1)
            dve.tensor_copy(sc_end[:, :, 0:2], sc_z[:, :, NP_TOK:NP_TOK + 2]).then_inc(sc_kept, 1)
            dve.tensor_copy(sc_end[:, :, 2:].rearrange("p m (b s) -> p m b s", s=2),
                            sc_z[:, :, 2 + NP_TOK:].rearrange("p m (b s) -> p m b s", s=NQ + 2)[:, :, :, NQ:NQ + 2])\
                .then_inc(sc_kept, 1)

        def pool_sc_in(pool, st):
            pool.wait_ge(sc_landed, 32)
            pool.memset(sc_z[:, :, 0:2], 0.0)
            pool.tensor_copy(sc_z[:, :, 2 + NP_TOK:].rearrange("p m (b s) -> p m b s", s=NQ + 2)[:, :, :, 0:2],
                             sc_prev[:, :, :].rearrange("p m (b s) -> p m b s", s=2)).then_inc(z_clear, 1)
            pool.wait_ge(z_clear, 1)

            def by_sequence(a, s=NQ):
                return a.rearrange("p (b s) -> p b s", s=s)

            def product(m):
                f = m % 2
                pool.wait_ge(evacuated, st["g0"] + 6 * (m // 2) + 5 + f)
                pool.tensor_tensor(sc_z[:, m, 2:2 + NP_TOK], sc_c[:, f, 0:NP_TOK], sc_h[:, f, 0:NP_TOK], ALU.mult)
                pool.tensor_tensor(by_sequence(sc_z[:, m, 2 + NP_TOK:], NQ + 2)[:, :, 2:NQ + 2], by_sequence(sc_c[:, f, NP_TOK:]),
                                   by_sequence(sc_h[:, f, NP_TOK:]), ALU.mult).then_inc(z_ready, 1)

            def gated(m):
                f = m % 2
                cv = sc_cv[:, f, :]
                pool.wait_ge(cv_step, 3 * m + 3)
                if m >= 2:
                    pool.wait_ge(mixer_ready, st["mixer_base"] + m - 1)
                pool.tensor_tensor(sc_y[:, f, 0:NP_TOK], sc_b[:, m, 0:NP_TOK], cv[:, 0:NP_TOK], ALU.mult)
                pool.tensor_tensor(by_sequence(sc_y[:, f, NP_TOK:]), by_sequence(sc_b[:, m, NP_TOK:]),
                                   by_sequence(cv[:, NP_TOK + 2:], NQ + 2)[:, :, 0:NQ], ALU.mult).then_inc(sc_y_ready, 1)

            def remainder(m):
                pool.wait_ge(sc_hi, m + 1)
                pool.tensor_tensor(h_lo[:, m, :], sc_y[:, m % 2, :], h_hi[:, m, :].bitcast(F32), ALU.subtract)\
                    .then_inc(mixer_ready, 1)

            for m in range(0, KT + 2, 2):
                for step, at in ((product, m), (remainder, m - 2), (gated, m)):
                    for f in range(2):
                        if 0 <= at < KT:
                            step(at + f)
        act_primed, dve_primed, pool_primed, pe_primed = [], [], [], []

        if kinds & {"swa", "nsa"}:
            rot_turned = sem("rot_turned")
            rot_sin = sem("rot_sin")
            rot_cos = sem("rot_cos")
            rope_ready = sem("rope_ready")
            rot_s, rot_c = gate_in, up
        n_rope = 0
        for st in stages:
            st["rope"] = n_rope
            n_rope += {"swa_in": 9, "nsa_in": 10}.get(st["kind"], 0)

        def flat1(a):
            return a.rearrange("p a n -> p (a n)")

        def turns_of(turns, c):
            return [(r, src, dst) for r, (tile, src, dst) in enumerate(turns) if tile // 2 == c]

        def pe_in_turning(pe, st, turns, between=None):
            n0, g0, norm = st["n0"], st["g0"], st["norm"]

            def turn(c):
                for r, src, _ in turns_of(turns, c):
                    pe.wait_ge(evacuated, g0 + turns[r][0] + 1)
                    pe.wait_ge(rot_sin, st["rope"] + r + 1)
                    pe.matmul(bank[5 + r % 2][:, 0:T], cst("perm"), flat1(src), start=True, stop=True).then_inc(rot_turned, 1)

            for c in range(st["chunks"]):
                one = n0 + c in narrow
                for half in range(1 if one else 2):
                    operand = (lambda k: pe.wait_ge(xlo_ready, KT * norm + k + 1)) if c == half == 0 else None
                    pe_half(pe, n0 + c, half, g0 + 2 * c + half, x_hi, x_lo, operand=operand).then_inc(half_used, 2 if one else 1)
                if c == 0:
                    pe_norm(pe, norm)
                turn(c - 1)
                if between and c in between:
                    between[c]()
            turn(st["chunks"] - 1)

        def dve_in_turning(dve, st, outs, turns, between=None):
            n0, g0 = st["n0"], st["g0"]

            def turned(c):
                for r, _, dst in turns_of(turns, c):
                    at = st["rope"] + r
                    dve.wait_ge(rot_turned, at + 1)
                    dve.wait_ge(rope_ready, at + 1)
                    dve.tensor_tensor(rot_s[:, r % 2, :], bank[5 + r % 2][:, 0:T], cst("sin"), ALU.mult).then_inc(rot_sin, 1)
                    dve.wait_ge(rot_sin, at + 3)
                    dve.wait_ge(rot_cos, at + 1)
                    dve.tensor_tensor(flat1(dst), rot_c[:, r % 2, :], rot_s[:, r % 2, :], ALU.add).then_inc(rope_ready, 1)

            dve_rstd(dve, st["norm"])
            for c in range(st["chunks"]):
                one = n0 + c in narrow
                for half in range(1 if one else 2):
                    dve_take3(dve, n0 + c, half, g0 + 2 * c + half, outs[2 * c + half], count=2 if one else 1)
                dve_split(dve, n0 + RAW + c)
                turned(c - 1)
                if between and c in between:
                    between[c]()
            turned(st["chunks"] - 1)

        def pool_turns(pool, st, turns):
            for r, (tile, src, _) in enumerate(turns):
                at = st["rope"] + r
                pool.wait_ge(evacuated, st["g0"] + tile + 1)
                pool.wait_ge(rope_ready, at + 1)
                pool.tensor_tensor(rot_c[:, r % 2, :], flat1(src), cst("cos"), ALU.mult).then_inc(rot_cos, 1)

        def dve_take3(dve, n, half, g, dst, i=0, step=0, gstep=0, count=1):
            dve.wait_ge(half_used, 2 * n + half + 1 + 2 * step * i)
            dve.tensor_tensor(dst, bank[g % BANKS][:, 0:T].rearrange("p (a t) -> p a t", a=1),
                              rstd[:, :].rearrange("p (a t) -> p a t", a=1), ALU.mult).then_inc(evacuated, count)

        def queries(q, t, rows, grp=None):
            return q[:, bass.ds(t, 1), rows].rearrange("p a t -> p (a t)")

        def sample_rows(q, grp, b):
            return q[HD * grp:HD * grp + HD, 0:KT, bass.ds(NP_TOK + NQ * b, NQ)]

        def sample_queries(q, b):
            return q[:, 0:KT, bass.ds(NP_TOK + NQ * b, NQ)].rearrange("p (g t) s -> p g t s", g=1).broadcast_to([P, 2, KT, NQ])

        def rounds(engine, order, steps):
            def run(r, k, now=True, ahead=True):
                for *when, u, names in order:
                    if ahead if when else now:
                        for name in names.split():
                            if name in steps:
                                at = r + 1 if when else r
                                steps[name](PRIME + 3 * at + u + 1, u, at, (k + 1) % 2 if when else k)
            run(-1, 1, now=False)
            with engine.Fori(0, 3) as j:
                for k in range(2):
                    run(2 * j + k, k)
            run(6, 0)
            run(7, 1, ahead=False)

        SWA_ROUND = (
            ("next", 0, "scores mask"), ("next", 1, "scores"), (0, "turn copies"), (1, "turn"), (2, "turn"),
            (0, "values"), ("next", 2, "scores"), (1, "copies"), ("next", 0, "maxima"), ("next", 1, "mask"),
            ("next", 0, "negate"), (1, "values"), (2, "copies"), ("next", 1, "maxima"), ("next", 2, "mask"),
            (0, "outs"), ("next", 0, "exps"), ("next", 1, "negate"), (0, "remainder"), (1, "outs"),
            ("next", 2, "maxima negate"), ("next", 0, "total"), ("next", 1, "exps"), ("next", 2, "exps"),
            (2, "values"), ("next", 0, "scale"), ("next", 1, "total"), ("next", 2, "total"), (2, "outs"),
            ("next", 1, "scale"), ("next", 2, "scale"), (1, "remainder"), (2, "remainder"))
        KEYS = (2 * P, 4 * P, P + NS_TOK)

        if "swa" in kinds:
            area = Area()
            at_q = area("at_q", [P, KT, T])
            at_kv = area("at_kv", [P, 2, T])
            swa_turns = [(0, at_kv[:, 0:1, :], at_kv[:, 0:1, :])]
            swa_turns += [(2 + t, at_q[:, t:t + 1, :], at_q[:, t:t + 1, :]) for t in range(KT)]
            at_kbd = area("at_kbd", [P, 2, 2, P])
            at_vbd = area("at_vbd", [P, 2, 2, P])
            at_vs = area("at_vs", [NS_TOK, P])
            at_kc = area("at_kc", [P, NB, P])
            at_vc = area("at_vc", [P, NB, P])
            at_qst = area("at_qst", [P, 3, P])
            at_vst = area("at_vst", [P, P])
            at_p = area("at_p", [P, 3, 512])
            at_pt = area("at_pt", [P, 3, 512])
            at_mx, at_neg, at_esk, at_es, at_sum, at_rec = (area("at_" + n, [P, 3, 2])
                                                            for n in ("mx", "neg", "esk", "es", "sum", "rec"))
            at_sink = area("at_sink", [P, 17])
            at_sink8 = area("at_sink8", [P, 17])
            score_bank, turned_bank, out_bank = (bank[0:3], [bank[3], bank[5], bank[6]], [bank[7], bank[4], bank[7]])
            swa_landed = sem("swa_landed")
            swa_passed = sem("swa_passed")
            kbd_ready = sem("kbd_ready")
            v_turned = sem("v_turned")
            vbd_ready = sem("vbd_ready")
            sink_ready = sem("sink_ready")
            q_staged = sem("q_staged")
            s_ready = sem("s_ready")
            masked = sem("masked")
            at_step = [sem(f"at_step{u}") for u in range(3)]
            vst_staged = sem("vst_staged")
            neg_ready = sem("neg_ready")
            exp_ready = sem("exp_ready")
            p_ready = sem("p_ready")
            p1_ready = [sem(f"p1_ready{u}") for u in range(2)]
            pt_turned = sem("pt_turned")
            pt_copied = sem("pt_copied")
            o_ready = sem("o_ready")
            o_hi = sem("o_hi")
            o_lo = sem("o_lo")
            pool_primed += [q_staged]
            pe_primed += [s_ready, pt_turned, o_ready]
            dve_primed += [masked, neg_ready, p_ready, o_lo]
            act_primed += [exp_ready, pt_copied, o_hi]

        def groups(u):
            return at_p[:, u, 0:KEYS[u]].rearrange("p (k g j) -> p g k j", g=2, j=P)

        def sp_swa_load(sp):
            sp.wait_ge(evacuated, swa_st["g0"])
            for dst, name in ((at_kc, "swa_k"), (at_vc, "swa_v")):
                sp.dma_start(dst[:, :, :], A[name]).then_inc(swa_landed, 16)
            sp.dma_start(at_sink[:, :], A["sinks"]).then_inc(swa_landed, 16)
            sp.dma_start(O["swa_passed"], A["swa_old"][:, NQ:P, :]).then_inc(swa_passed, 16)

        def sp_swa_store(sp):
            sp.wait_ge(rope_ready, 2 + swa_st["rope"] + 9)
            sp.dma_start(O["swa_kv"], at_kv[:, :, :]).then_inc(mix_stored["swa"], 16)

        def pe_swa(pe, st):
            def turn_values():
                pe.wait_ge(evacuated, st["g0"] + 2)
                for c in range(3):
                    w = P if c < 2 else NS_TOK
                    tr = pe.transpose(bank[7][0:w, P * c:P * c + P], at_kv[:, 1, P * c:P * c + w], cst("ident"))
                tr.then_inc(v_turned, 1)

            pe_in_turning(pe, st, swa_turns, between={1: turn_values})
            pe.wait_ge(kbd_ready, 5)
            pe.wait_ge(swa_landed, 48)

            pe.wait_ge(vbd_ready, 3)

            def scores(V, u, r, k):
                pe.wait_ge(q_staged, V)
                pe.wait_ge(masked, V - 3)
                out, q = score_bank[u], at_qst[:, u, :]
                if u < 2:
                    mm = pe.matmul(out[:, 0:KEYS[u]], q, at_kbd[:, 0:u + 1, :, :], start=True, stop=True)
                else:
                    pe.matmul(out[:, 0:P], q, flat1(at_kc[:, bass.ds(r, 1), :]), start=True, stop=True)
                    mm = pe.matmul(out[:, P:P + NS_TOK], q, at_kv[:, 0, NP_TOK:T], start=True, stop=True)
                mm.then_inc(s_ready, 1)

            def turn(V, u, r, k):
                pe.wait_ge(p_ready, V)
                if u < 2:
                    pe.wait_ge(p1_ready[u], r + 1)
                pe.wait_ge(pt_copied, V - 3)
                out = turned_bank[u]
                if u < 2:
                    for m in range(2 * (u + 1)):
                        tr = pe.transpose(out[:, P * m:P * m + P], at_p[:, u, P * m:P * m + P], cst("ident"))
                else:
                    pe.transpose(out[:, 0:P], at_p[:, u, 0:P], cst("ident"))
                    tr = pe.transpose(out[0:NS_TOK, P:2 * P], at_p[:, u, P:P + NS_TOK], cst("ident"))
                tr.then_inc(pt_turned, 1)

            def values(V, u, r, k):
                pe.wait_ge(pt_copied, V)
                pe.wait_ge(o_lo, V - (1, 2, 2)[u])
                out = out_bank[u][:, 0:P]
                if u < 2:
                    n = 2 * (u + 1)
                    for m in range(n):
                        mm = pe.matmul(out, at_vbd[:, m // 2, m % 2, :], at_pt[:, u, P * m:P * m + P],
                                       start=(m == 0), stop=(m == n - 1))
                else:
                    pe.wait_ge(vst_staged, r + 1)
                    pe.matmul(out, at_vst[:, :], at_pt[:, u, 0:P], start=True, stop=False)
                    mm = pe.matmul(out, at_vs[:, :], at_pt[0:NS_TOK, u, P:2 * P], start=False, stop=True)
                mm.then_inc(o_ready, 1)

            rounds(pe, SWA_ROUND, dict(scores=scores, turn=turn, values=values))

        def act_swa(act, st):
            act_std(act, st["norm"])
            for c in range(3):
                act_split(act, st["n0"] + RAW + c)
            act.wait_ge(v_turned, 1)
            act.wait_ge(kbd_ready, 3)
            vt = bank[7][:, 0:2 * P].rearrange("p (c g d) -> p c g d", c=2, g=2)
            for grp in range(2):
                act.activation(at_vbd[:, :, grp, HD * grp:HD * grp + HD], vt[:, :, grp, :], ACT.Copy).then_inc(vbd_ready, 1)
            act.activation(at_vs[:, :], bank[7][0:NS_TOK, 2 * P:3 * P], ACT.Copy).then_inc(vbd_ready, 1)
            for c in range(3, st["chunks"]):
                act_split(act, st["n0"] + RAW + c)

            def exps(V, u, r, k):
                act.wait_ge(neg_ready, V)
                if u < 2:
                    pg = at_p[:, u, 0:KEYS[u]].rearrange("p (k g j) -> p k g j", g=2, j=P)
                    parts = [pg[:, :, grp, :] for grp in range(2)]
                else:
                    parts = [at_p[:, u, 0:KEYS[u]]]
                for c, p in enumerate(parts):
                    act.activation(p, p, ACT.Exp, bias=at_neg[:, u, c:c + 1], scale=SCALE, accum_out=at_sum[:, u, c:c + 1])
                w = len(parts)
                act.activation(at_es[:, u, 0:w], at_esk[:, u, 0:w], ACT.Exp, scale=SCALE).then_inc(exp_ready, 1)

            def copies(V, u, r, k):
                act.wait_ge(pt_turned, V)
                act.wait_ge(o_ready, V - 3)
                if u < 2:
                    o = act.activation(at_pt[:, u, 0:KEYS[u]], turned_bank[u][:, 0:KEYS[u]], ACT.Copy)
                else:
                    act.activation(at_pt[:, u, 0:P], turned_bank[u][:, 0:P], ACT.Copy)
                    o = act.activation(at_pt[0:NS_TOK, u, P:2 * P], turned_bank[u][0:NS_TOK, P:2 * P], ACT.Copy)
                o.then_inc(pt_copied, 1)

            def outs(V, u, r, k):
                act.wait_ge(o_ready, V)
                if u < 2:
                    o = act.activation(queries(h_hi, r, slice(P * u, P * u + P)), out_bank[u][:, 0:P], ACT.Copy)
                else:
                    for grp in range(2):
                        o = act.activation(sample_rows(h_hi, grp, r), out_block(out_bank[u], grp), ACT.Copy)
                o.then_inc(o_hi, 1)

            def scale(V, u, r, k):
                if u < 2:
                    act.wait_ge(at_step[u], 5 * r + 5)
                    p = groups(u)[:, 1, :, :]
                    act.activation(p, p, ACT.Copy, scale=at_rec[:, u, 1:2]).then_inc(p1_ready[u], 1)

            rounds(act, SWA_ROUND, dict(exps=exps, copies=copies, outs=outs, scale=scale))

        def out_block(b, grp):
            return b[HD * grp:HD * grp + HD, HD * grp:HD * grp + HD].rearrange("p (t s) -> p t s", s=NQ)

        def dve_swa(dve, st):
            def lay_keys():
                dve.wait_ge(rope_ready, 2 + st["rope"] + 1)
                dve.wait_ge(kbd_ready, 3)
                for grp in range(2):
                    rows = slice(HD * grp, HD * grp + HD)
                    dve.tensor_copy(at_kbd[rows, :, grp, :], at_kv[rows, 0, 0:NP_TOK].rearrange("p (c j) -> p c j", c=2))\
                        .then_inc(kbd_ready, 1)

            dve_in_turning(dve, st, [at_kv[:, t:t + 1, :] for t in range(2)] + [at_q[:, t:t + 1, :] for t in range(KT)], swa_turns,
                           between={2: lay_keys})
            dve.wait_ge(swa_landed, 48)
            dve.tensor_scalar(at_sink8[:, :], at_sink[:, :], 1.0 / SCALE, None, ALU.mult).then_inc(sink_ready, 1)
            dve.wait_ge(sink_ready, 1)

            def stepped(u, r, m):
                dve.wait_ge(at_step[u], 5 * r + m)

            def sinks(u, r):
                if u == 2:
                    return at_sink8[:, 16:17]
                return at_sink8[:, 0:16].rearrange("p (g t) -> p g t", g=2)[:, :, bass.ds(r, 1)].rearrange("p g t -> p (g t)")

            def mask(V, u, r, k):
                dve.wait_ge(s_ready, V)
                dve.wait_ge(pt_turned, V - 3)
                if u < 2:
                    m = dve.tensor_tensor(at_p[:, u, 0:KEYS[u]], score_bank[u][:, 0:KEYS[u]],
                                          cst("m_band")[:, 4 * P - KEYS[u]:4 * P], ALU.add)
                else:
                    dve.tensor_tensor(at_p[:, u, 0:P], score_bank[u][:, 0:P], cst("m_old"), ALU.add)
                    new = cst("m_new").rearrange("p (b k) -> p b k", b=NB)[:, bass.ds(r, 1), :]
                    m = dve.tensor_tensor(at_p[:, u, P:P + NS_TOK], score_bank[u][:, P:P + NS_TOK], flat1(new), ALU.add)
                m.then_inc(masked, 1)

            def maxima(V, u, r, k):
                w = 1 + (u < 2)
                dve.wait_ge(masked, V)
                if u < 2:
                    dve.tensor_reduce(at_mx[:, u, :], groups(u), AX.XY, ALU.max).then_inc(at_step[u], 1)
                else:
                    dve.tensor_reduce(at_mx[:, u, 0:1], at_p[:, u, 0:KEYS[u]], AX.X, ALU.max).then_inc(at_step[u], 1)
                stepped(u, r, 1)
                dve.tensor_tensor(at_mx[:, u, 0:w], at_mx[:, u, 0:w], sinks(u, r), ALU.max).then_inc(at_step[u], 1)

            def negate(V, u, r, k):
                w = 1 + (u < 2)
                stepped(u, r, 2)
                dve.tensor_tensor(at_esk[:, u, 0:w], sinks(u, r), at_mx[:, u, 0:w], ALU.subtract).then_inc(at_step[u], 1)
                dve.tensor_scalar(at_neg[:, u, 0:w], at_mx[:, u, 0:w], -SCALE, None, ALU.mult).then_inc(neg_ready, 1)

            def total(V, u, r, k):
                w = 1 + (u < 2)
                dve.wait_ge(exp_ready, V)
                dve.tensor_tensor(at_sum[:, u, 0:w], at_sum[:, u, 0:w], at_es[:, u, 0:w], ALU.add).then_inc(at_step[u], 1)
                stepped(u, r, 4)
                dve.reciprocal(at_rec[:, u, 0:w], at_sum[:, u, 0:w]).then_inc(at_step[u], 1)

            def scale(V, u, r, k):
                stepped(u, r, 5)
                if u < 2:
                    p = groups(u)[:, 0, :, :]
                    o = dve.tensor_scalar(p, p, at_rec[:, u, 0:1], None, ALU.mult)
                else:
                    p = at_p[:, u, 0:KEYS[u]]
                    o = dve.tensor_scalar(p, p, at_rec[:, u, 0:1], None, ALU.mult)
                o.then_inc(p_ready, 1)

            def remainder(V, u, r, k):
                dve.wait_ge(o_hi, V)
                if u < 2:
                    rows = slice(P * u, P * u + P)
                    o = dve.tensor_tensor(queries(h_lo, r, rows), out_bank[u][:, 0:P], queries(h_hi, r, rows).bitcast(F32),
                                          ALU.subtract)
                else:
                    for grp in range(2):
                        o = dve.tensor_tensor(sample_rows(h_lo, grp, r), out_block(out_bank[u], grp),
                                              sample_rows(h_hi, grp, r).bitcast(F32), ALU.subtract)
                o.then_inc(o_lo, 1)

            rounds(dve, SWA_ROUND, dict(mask=mask, maxima=maxima, negate=negate, total=total, scale=scale, remainder=remainder))
            dve.wait_ge(o_lo, PRIME + 24)
            dve.nop().then_inc(mixer_ready, KT)

        def pool_swa(pool, st):
            pool.wait_ge(evacuated, st["g0"])
            pool.memset(at_kbd[:, :, :, :], 0.0).then_inc(kbd_ready, 1)
            pool.memset(at_vbd[:, :, :, :], 0.0).then_inc(kbd_ready, 2)
            pool_turns(pool, st, swa_turns)
            pool.wait_ge(rope_ready, 2 + st["rope"] + 9)

            def stage_queries(V, u, r, k):
                pool.wait_ge(s_ready, V - 3)
                if u < 2:
                    pool.tensor_copy(at_qst[:, u, :], queries(at_q, r, slice(P * u, P * u + P))).then_inc(q_staged, 1)
                else:
                    pool.tensor_tensor(at_qst[:, u, :].rearrange("p (g t s) -> p g t s", g=2, s=NQ), sample_queries(at_q, r),
                                       cst("bd").rearrange("p (g t s) -> p g t s", g=2, s=NQ), ALU.mult).then_inc(q_staged, 1)

            def stage_values(V, u, r, k):
                if u == 2:
                    pool.wait_ge(swa_landed, 48)
                    pool.wait_ge(o_ready, V - 3)
                    pool.tensor_copy(at_vst[:, :], flat1(at_vc[:, bass.ds(r, 1), :])).then_inc(vst_staged, 1)

            rounds(pool, SWA_ROUND, dict(scores=stage_queries, turn=stage_values))

        N_STRIDE = 8
        HROWS = 2 * N_CMP_P + 1
        n_pages = A["pool_cmp"].shape[0]
        if "nsa" in kinds:
            space = Space(H_AT, LIMIT)
            w1_past = space("w1_past", [P, 2, 16, 256])
            past_pairs = space("past_pairs", [P, 2, 4, 2 * PAST // 2])
            past_hid = space("past_hid", [P, 2, 2, 2, 2 * N_CMP_S])
            cmp_landed = sem("cmp_landed")
            w2_landed = sem("w2_landed")
            pages_landed = sem("pages_landed")
            bias_part = space("bias_part", [P, 2, 256])
            one_col = space("one_col", [P, 1])
            bias_step = sem("bias_step")
            pairs_landed = [[sem(f"pairs_landed{s}_{b}") for b in range(2)] for s in range(2)]
            hid_ready = sem("hid_ready")
            bias_summed = sem("bias_summed")
            bias_ready = sem("bias_ready")
            hid_gelu = sem("hid_gelu")
            cmp_made = sem("cmp_made")
            cmp_kept = sem("cmp_kept")
            win_passed = sem("win_passed")

            r1, r2 = Space(H_AT + KT * T * 4, HL_AT), Space(HL_AT + KT * T * 4, END)
            xh, xl = Space(XH_AT, XL_AT), Space(XL_AT, CONST_AT)
            w1_space, r3 = Space(END, LIMIT), Space(END, LIMIT)
            n_q = r1("n_q", [P, KT, T])
            n_kv = r1("n_kv", [P, 6, T])
            n_qr = r2("n_qr", [P, KT, T])
            nsa_turns = [(t, n_kv[:, t:t + 1, :], n_kv[:, t:t + 1, :]) for t in (2, 4)]
            nsa_turns += [(KT + t, n_q[:, t:t + 1, :], n_qr[:, t:t + 1, :]) for t in range(KT)]
            n_kbd = [r2(f"n_kbd{a}", [P, 2, 2, P]) for a in range(2)]
            n_gates = r2("n_gates", [P, 1, T])
            n_gt = r2("n_gt", [P, 2, 48])
            n_kcb = r2("n_kcb", [P, 64])
            n_vcb = r2("n_vcb", [64, P])
            n_sg = r2("n_sg", [P, NB, 3])
            n_vbd = [xh(f"n_vbd{a}", [P, 2, 2, P]) for a in range(2)]
            n_wk = xh("n_wk", [P, NB, P])
            n_qst = xh("n_qst", [P, 2, 2, P])
            n_wv = xl("n_wv", [P, NB, P])
            n_vst = xl("n_vst", [P, P])
            n_vcst = xl("n_vcst", [64, P])
            n_qss = xl("n_qss", [P, 2, P])
            n_vs = [xl(f"n_vs{a}", [NS_TOK, P]) for a in range(2)]
            n_mx, n_neg, n_sum, n_rec, n_fac = (up_space("n_" + s, [P, 3, 6]) for s in ("mx", "neg", "sum", "rec", "fac"))
            n_imp, n_hit, n_blk = (up_space("n_" + s, [P, 16]) for s in ("imp", "hit", "blk"))
            n_low, n_drop = (up_space("n_" + s, [P, 1]) for s in ("low", "drop"))
            n_srow = Space(SILU_AT, UP_AT)("n_srow", [P, 3, NS_TOK])
            n_hid = h_space("n_hid", [P, 2, 2, P])
            w1_new = w1_space("w1_new", [P, 2, 16, 256])
            n_pairs = w1_space("n_pairs", [P, 2, 2, NP_TOK // 2])
            n_hrow = w1_space("n_hrow", [HROWS, 2, 256])
            n_p = r3("n_p", [P, 2, 1088])
            n_ps = r3("n_ps", [P, 1344])
            n_pts = r3("n_pts", [P, 1536])
            n_pt = gate_silu_space("n_pt", [P, 1152])
            n_sel = r3("n_sel", [P, 2, NPAGES, 2 * P])
            w1_landed = sem("w1_landed")
            win_landed = sem("win_landed")
            sel_landed = [sem(f"sel_landed{s}") for s in range(2)]
            pairs_ready = sem("pairs_ready")
            hid_clear = sem("hid_clear")
            lay_clear = sem("lay_clear")
            nhid_ready = sem("nhid_ready")
            nhid_copied = sem("nhid_copied")
            nhid_turned = sem("nhid_turned")
            nhid_gelu = sem("nhid_gelu")
            gates_ready = sem("gates_ready")
            nv_turned = sem("nv_turned")
            nv_ready = sem("nv_ready")
            n_laid = sem("n_laid")
            n_lay_step = sem("n_lay_step")
            nk_ready = sem("nk_ready")
            nq_staged = sem("nq_staged")
            nv_staged = sem("nv_staged")
            ns_ready = sem("ns_ready")
            nmasked = sem("nmasked")
            n_step = [sem(f"n_step{a}") for a in range(3)]
            nneg_ready = sem("nneg_ready")
            nexp_ready = sem("nexp_ready")
            sel_kept = sem("sel_kept")
            pc_ready = sem("pc_ready")
            imp_ready = sem("imp_ready")
            rec_ready = sem("rec_ready")
            selneg_ready = sem("selneg_ready")
            selexp_ready = sem("selexp_ready")
            np_ready = [sem(f"np_ready{a}") for a in range(3)]
            npt_turned = sem("npt_turned")
            npt_copied = sem("npt_copied")
            no_ready = sem("no_ready")
            no_hi = sem("no_hi")
            no_lo = sem("no_lo")
            pe_primed += [ns_ready, npt_turned, no_ready, cmp_made]
            act_primed += [npt_copied, no_hi, sel_kept, hid_gelu, cmp_kept]
            dve_primed += [nmasked, no_lo]
            pool_primed += [nq_staged]

        def past_pairs_of(engine, b):
            if b >= 4:
                engine.wait_ge(hid_ready, 4 * (b // 2 - 1))
            elif b >= 2:
                engine.wait_ge(bias_summed, 1)
            with engine.Fori(0, NPAGES) as r:
                pg = engine.value_load(pages[0:1, bass.ds(r + NPAGES * b, 1)], min_val=0, max_val=n_pages - 1)
                engine.dma_start(past_pairs[:, b // 2 % 2, :, bass.ds(N_PAIR * (r + NPAGES * (b % 2)), N_PAIR)],
                                 A["pool_cmp"][bass.ds(pg, 1)].rearrange("a p (k n) -> p (a k) n", k=4))\
                    .then_inc(pairs_landed[b // 2 % 2][b % 2], 16)

        def sp_past_first(sp):
            sp.dma_start(pages[:, :], A["pages"]).then_inc(pages_landed, 16)
            sp.dma_start(cmp_pe[:, :, :], A["cmp_pe"]).then_inc(cmp_landed, 16)
            sp.dma_start(w1_past[:, :, :, :], A["cmp_w1"]).then_inc(cmp_landed, 16)
            sp.wait_ge(pages_landed, 16)
            past_pairs_of(sp, 0)
            sp.dma_start(w2z[:, :, :, :, :], A["cmp_w2"]).then_inc(w2_landed, 16)

        def sp_past_rest(sp):
            for b in range(2, NB, 2):
                past_pairs_of(sp, b)

        def pool_past(pool):
            pool.wait_ge(pages_landed, 16)
            for b in range(1, NB, 2):
                past_pairs_of(pool, b)

        def pe_hidden(pe, w1, pairs, blocks, kv, ht, out):
            for pp in range(16):
                mm = pe.matmul(out, w1[:, kv, pp, P * ht:P * ht + P],
                               pairs[..., pp:pp + N_STRIDE * (blocks - 1) + 1:N_STRIDE], start=(pp == 0), stop=(pp == 15))
            return mm

        def pe_past(pe):
            pe.wait_ge(cmp_landed, 32)
            pe.wait_ge(w2_landed, 16)
            pe.wait_ge(bias_step, 32)
            for k in range(4):
                mm = pe.matmul(bank[7][:, k:k + 1], bias_part[:, k // 2, P * (k % 2):P * (k % 2) + P], one_col[:, :],
                               start=True, stop=True)
            mm.then_inc(bias_summed, 1)
            with pe.Fori(0, 2) as i:
                for q in range(2):
                    for b in range(2):
                        pe.wait_ge(pairs_landed[q][b], 16 * NPAGES * (i + 1))
                    for kv in range(2):
                        for ht in range(2):
                            pe.wait_ge(hid_gelu, PRIME + 4 * q + 2 * kv + ht + 1 - 4 + 8 * i)
                            pairs = past_pairs[:, q, 2 * kv:2 * kv + 2, :].rearrange("p g (b n) -> p g b n", b=2)
                            out = bank[2 * kv + ht][:, 0:4 * N_CMP_S].rearrange("p (g b n) -> p g b n", g=2, b=2)
                            pe_hidden(pe, w1_past, pairs, N_CMP_S, kv, ht, out).then_inc(hid_ready, 1)
                    pe.wait_ge(hid_gelu, 4 + 4 * q + 2 + 8 * i)
                    pe.wait_ge(cmp_kept, PRIME + 2 * q - 1 + 4 * i)
                    for k in range(4):
                        mm = pe.matmul(bank[5][:, 0:2 * N_CMP_S], w2z[:, 0, k // 2, k % 2, :], past_hid[:, 0, k // 2, k % 2, :],
                                       start=(k == 0), stop=(k == 3))
                    mm.then_inc(cmp_made, 1)
                    pe.wait_ge(hid_gelu, 4 + 4 * q + 4 + 8 * i)
                    pe.wait_ge(cmp_kept, PRIME + 2 * q + 4 * i)
                    for b in range(2):
                        for k in range(4):
                            mm = pe.matmul(bank[6][0:N_CMP_S, P * b:P * b + P],
                                           past_hid[:, 1, k // 2, k % 2, N_CMP_S * b:N_CMP_S * b + N_CMP_S],
                                           w2z[:, 1, k // 2, k % 2, :], start=(k == 0), stop=(k == 3))
                    mm.then_inc(cmp_made, 1)

        def dve_past(dve):
            dve.memset(one_col[:, :], 1.0)
            dve.wait_ge(cmp_landed, 32)
            for kv in range(2):
                dve.tensor_scalar(bias_part[:, kv, :], w1_past[:, kv, 0, :], cmp_pe[:, kv, 0:1], None, ALU.mult).then_inc(bias_step, 1)
            with dve.Fori(1, 16) as pp:
                for kv in range(2):
                    dve.wait_ge(bias_step, 2 * pp - 1 + kv)
                    dve.scalar_tensor_tensor(out=bias_part[:, kv, :], in0=flat1(w1_past[:, kv, bass.ds(pp, 1), :]),
                                             scalar=cmp_pe[:, kv, bass.ds(pp, 1)], in1=bias_part[:, kv, :],
                                             op0=ALU.mult, op1=ALU.add).then_inc(bias_step, 1)

        def act_past(act, i):
            if i == 0:
                act.wait_ge(bias_summed, 1)
                act.activation(cmp_bias[:, :, :].rearrange("p k h -> p (k h)"), bank[7][:, 0:4], ACT.Copy).then_inc(bias_ready, 1)
                act.wait_ge(bias_ready, 1)
            for q in range(2):
                for kv in range(2):
                    act.wait_ge(cmp_made, PRIME + 2 * q + kv - 1 + 4 * i)
                    for ht in range(2):
                        act.wait_ge(hid_ready, 4 * q + 2 * kv + ht + 1 + 8 * i)
                        act.activation(past_hid[:, kv, ht, :, :],
                                       bank[2 * kv + ht][:, 0:4 * N_CMP_S].rearrange("p (g n) -> p g n", g=2),
                                       ACT.Gelu_apprx_tanh, bias=cmp_bias[:, kv, ht:ht + 1]).then_inc(hid_gelu, 1)
                act.wait_ge(cmp_made, PRIME + 2 * q + 1 + 4 * i)
                act.activation(kcmp_s[:, bass.ds(4 * i + 2 * q, 2), 0:N_CMP_S],
                               bank[5][:, 0:2 * N_CMP_S].rearrange("p (b n) -> p b n", b=2), ACT.Copy).then_inc(cmp_kept, 1)
                act.wait_ge(cmp_made, PRIME + 2 * q + 2 + 4 * i)
                act.activation(vcmp_s[0:N_CMP_S, bass.ds(4 * i + 2 * q, 2), :],
                               bank[6][0:N_CMP_S, 0:2 * P].rearrange("p (b d) -> p b d", b=2), ACT.Copy).then_inc(cmp_kept, 1)

        def sp_nsa_load(sp):
            sp.dma_start(O["win_passed"], A["win_old"][:, NQ:P, :]).then_inc(win_passed, 16)

        def sp_nsa_store(sp):
            sp.wait_ge(evacuated, nsa_st["g0"] + nsa_st["groups"])
            sp.dma_start(n_wk[:, :, :], A["win_k"]).then_inc(win_landed, 16)
            sp.dma_start(n_wv[:, :, :], A["win_v"]).then_inc(win_landed, 16)
            sp.wait_ge(nhid_turned, 2)
            with sp.Fori(0, NB // 2) as i:
                for u in range(2):
                    with sp.Fori(0, NPAGES) as r:
                        pg = sp.value_load(pages[0:1, bass.ds(r + 2 * NPAGES * i + NPAGES * u, 1)], min_val=0, max_val=n_pages - 1)
                        sp.wait_ge(no_ready, PRIME + 3 * (u - 1) + 6 * i)
                        sp.dma_start(n_sel[:, u, bass.ds(r, 1), :], A["pool_sel"][bass.ds(pg, 1)].rearrange("a p n -> p a n"))\
                            .then_inc(sel_landed[u], 16)
            sp.wait_ge(rope_ready, 2 + nsa_st["rope"] + 10)
            sp.dma_start(O["nsa_kv"], n_kv[:, :, :]).then_inc(mix_stored["nsa"], 16)

        NSA_ROUND = (
            (2, "exps inverse block_probs importance"), (0, "values outs"), (2, "block_scores block_mask"),
            (1, "turn copies"), (2, "select"), ("next", 0, "scores"), (0, "remainder"), (2, "sel_exps"),
            ("next", 0, "mask"), (1, "values outs"), (2, "sel_inverse"), ("next", 0, "maxima negate"),
            ("next", 1, "scores"), ("next", 0, "exps"), (2, "scale"), ("next", 1, "mask"), (2, "turn"),
            ("next", 1, "maxima"), (1, "remainder"), ("next", 1, "negate"), (2, "copies"), ("next", 0, "inverse"),
            ("next", 1, "exps"), ("next", 0, "gate scale"), ("next", 2, "scores"), ("next", 1, "inverse"),
            ("next", 2, "keep"), ("next", 1, "gate"), ("next", 2, "mask maxima negate"), (2, "values"),
            ("next", 1, "scale"), ("next", 0, "turn"), (2, "outs"), ("next", 0, "copies"), (2, "remainder"))

        def pe_nsa(pe, st):
            hid_bank = (bank[7], bank[4])

            def hidden():
                pe.wait_ge(w1_landed, 16)
                pe.wait_ge(pairs_ready, 4)
                pe.wait_ge(std_ready, st["norm"] + 1)
                for kv in range(2):
                    for pp in range(16):
                        pairs = n_pairs[:, kv, :, :].rearrange("p g n -> p (g n)")[:, pp:pp + N_STRIDE * (HROWS - 1) + 1:N_STRIDE]
                        mm = pe.matmul(hid_bank[kv][0:HROWS, 0:256], pairs, w1_new[:, kv, pp, :], start=(pp == 0), stop=(pp == 15))
                    mm.then_inc(nhid_ready, 1)

            def turn_hidden():
                for kv in range(2):
                    pe.wait_ge(nhid_copied, kv + 1)
                    for ht in range(2):
                        tr = pe.transpose(hid_bank[kv][:, 256 + 32 * ht:256 + 32 * ht + HROWS], n_hrow[:, kv, P * ht:P * ht + P],
                                          cst("ident")[0:HROWS, 0:HROWS])
                    tr.then_inc(nhid_turned, 1)

            def lay():
                pe.wait_ge(gates_ready, 1)
                pe.wait_ge(nhid_gelu, 4)
                for c in range(2):
                    pe.transpose(bank[7][:, P * c:P * c + P], n_gates[:, 0, P * c:P * c + P], cst("ident"))
                for k in range(3):
                    pe.matmul(bank[7][:, 320 + NS_TOK * k:320 + NS_TOK * (k + 1)], cst("row_of")[:, P * k:P * k + P],
                              n_gates[:, 0, NP_TOK:T], start=True, stop=True)
                for k in range(4):
                    pe.matmul(bank[7][:, 256:320], w2z[:, 0, k // 2, k % 2, :], n_hid_of(0, k), start=(k == 0), stop=(k == 3))
                for k in range(4):
                    mm = pe.matmul(bank[4][0:64, 0:P], n_hid_of(1, k), w2z[:, 1, k // 2, k % 2, :], start=(k == 0), stop=(k == 3))
                mm.then_inc(n_laid, 1)

            pe_in_turning(pe, st, nsa_turns, between={3: hidden, 4: turn_hidden, 5: lay})
            pe.wait_ge(rot_sin, 2 + st["rope"] + 10)
            for a in range(2):
                for c in range(3):
                    w = P if c < 2 else NS_TOK
                    tr = pe.transpose(bank[5 + a][0:w, P * c:P * c + P], n_kv[:, 3 + 2 * a, P * c:P * c + w], cst("ident"))
            tr.then_inc(nv_turned, 1)
            pe.wait_ge(nk_ready, 4)
            pe.wait_ge(n_lay_step, 5)
            pe.wait_ge(nv_ready, 6)

            def scores(V, u, r, k):
                pe.wait_ge(nq_staged, V)
                pe.wait_ge(nmasked, V - 1)
                if u < 2:
                    if u == 0:
                        pe.wait_ge(sel_kept, PRIME + r)
                    plain, turned, n = n_qst[:, u, 0, :], n_qst[:, u, 1, :], 2 * P * (u + 1)
                    for a in range(2):
                        pe.matmul(bank[a][:, 0:n], turned, n_kbd[a][:, 0:u + 1, :, :], start=True, stop=True)
                    pe.matmul(bank[2][:, 0:64], plain, n_kcb[:, :], start=True, stop=True).then_inc(ns_ready, 1)
                    return
                plain, turned = n_qss[:, 0, :], n_qss[:, 1, :]
                pe.wait_ge(win_landed, 32)
                pe.matmul(bank[2][:, 0:64], turned, n_kv[:, 2, NP_TOK:T], start=True, stop=True)
                pe.matmul(bank[2][:, 64:128], turned, n_kv[:, 4, NP_TOK:T], start=True, stop=True)
                pe.matmul(bank[2][:, 128:256], turned, one(n_wk, r), start=True, stop=True)
                pe.matmul(bank[2][:, 256:256 + N_CMP_S], plain,
                          kcmp_s[:, bass.ds(r, 1), 0:N_CMP_S].rearrange("p a n -> p (a n)"), start=True, stop=True)
                pe.wait_ge(sel_landed[k], 8 * NPAGES * (r - k + 2))
                for a in range(2):
                    mm = pe.matmul(bank[a][:, :], turned, n_sel[:, k, 4 * a:4 * a + 4, 0:P], start=True, stop=True)
                mm.then_inc(ns_ready, 1)

            def importance(V, u, r, k):
                pe.wait_ge(pc_ready, r + 1)
                pe.matmul(bank[4][:, 0:N_CMP_S], cst("sum_r"), n_ps[:, 1280:1280 + N_CMP_S], start=True, stop=True)\
                    .then_inc(imp_ready, 1)

            def turn(V, u, r, k):
                pe.wait_ge(np_ready[u], r + 1)
                pe.wait_ge(npt_copied, V - 1)
                ident = cst("ident")
                if u < 2:
                    for a in range(2):
                        for m in range(2 * (u + 1)):
                            pe.transpose(bank[(3, 5)[a]][:, P * m:P * m + P], n_p[:, u, 512 * a + P * m:512 * a + P * m + P], ident)
                    pe.transpose(bank[6][0:64, 0:P], n_p[:, u, 1024:1088], ident).then_inc(npt_turned, 1)
                    return
                for m in range(NPAGES):
                    pe.transpose(bank[(3, 5)[m // 4]][:, P * (m % 4):P * (m % 4) + P], n_ps[:, P * m:P * m + P], ident)
                for m, (at, n) in enumerate(((1152, P), (1088, 64), (1024, 64), (1280, N_CMP_S))):
                    tr = pe.transpose(bank[6][0:n, P * m:P * m + P], n_ps[:, at:at + n], ident)
                tr.then_inc(npt_turned, 1)

            def values(V, u, r, k):
                pe.wait_ge(npt_copied, V)
                pe.wait_ge(no_lo, V - 1)
                if u < 2:
                    terms = [(n_vbd[a][:, m // 2, m % 2, :], n_pt[:, 512 * a + P * m:512 * a + P * m + P])
                             for a in range(2) for m in range(2 * (u + 1))]
                    terms.append((n_vcb[:, :], n_pt[0:64, 1024:1152]))
                else:
                    pe.wait_ge(nv_staged, r + 1)
                    terms = [(n_sel[:, k, m, P:2 * P], n_pts[:, P * m:P * m + P]) for m in range(NPAGES)]
                    terms += [(n_vst[:, :], n_pts[:, 1024:1152]), (n_vs[1][:, :], n_pts[0:64, 1152:1280]),
                              (n_vs[0][:, :], n_pts[0:64, 1280:1408]), (n_vcst[0:N_CMP_S, :], n_pts[0:N_CMP_S, 1408:1536])]
                for m, (v, p) in enumerate(terms):
                    mm = pe.matmul(bank[7][:, 0:P], v, p, start=(m == 0), stop=(m == len(terms) - 1))
                mm.then_inc(no_ready, 1)

            rounds(pe, NSA_ROUND, dict(scores=scores, importance=importance, turn=turn, values=values))

        def n_hid_of(kv, k):
            return n_hid[:, kv, k // 2, 64 * (k % 2):64 * (k % 2) + 64]

        def one(a, t):
            return a[:, bass.ds(t, 1), :].rearrange("p a n -> p (a n)")

        def act_nsa(act, st):
            act.wait_ge(evacuated, st["g0"])
            act.dma_start(w1_new[:, :, :, :], A["cmp_w1"]).then_inc(w1_landed, 16)
            act_std(act, st["norm"])
            for c in range(4):
                act_split(act, st["n0"] + RAW + c)
            act.wait_ge(evacuated, st["g0"] + KT)
            act.activation(n_gates[:, :, :], n_gates[:, :, :], ACT.Sigmoid).then_inc(gates_ready, 1)
            hid_bank = (bank[7], bank[4])
            for kv in range(2):
                act.wait_ge(nhid_ready, kv + 1)
                act.activation(n_hrow[:, kv, :], hid_bank[kv][0:HROWS, 0:256], ACT.Copy).then_inc(nhid_copied, 1)
            act_split(act, st["n0"] + RAW + 4)
            act.wait_ge(hid_clear, 1)
            for kv in range(2):
                for ht in range(2):
                    act.wait_ge(nhid_turned, kv + 1)
                    for grp in range(2):
                        g_op = act.activation(n_hid_of(kv, 2 * ht + grp)[:, 32 * grp:32 * grp + N_CMP_P],
                                              hid_bank[kv][:, 256 + 32 * ht + 16 * grp:256 + 32 * ht + 16 * grp + N_CMP_P],
                                              ACT.Gelu_apprx_tanh, bias=cmp_bias[:, kv, ht:ht + 1])
                    g_op.then_inc(nhid_gelu, 1)
            for c in range(5, 8):
                act_split(act, st["n0"] + RAW + c)
            act.wait_ge(nv_turned, 1)
            act.wait_ge(lay_clear, 4)
            act.wait_ge(evacuated, st["g0"] + st["groups"])
            for a in range(2):
                vt = bank[5 + a][:, 0:2 * P].rearrange("p (c g d) -> p c g d", c=2, g=2)
                for grp in range(2):
                    act.activation(n_vbd[a][:, :, grp, HD * grp:HD * grp + HD], vt[:, :, grp, :], ACT.Copy).then_inc(nv_ready, 1)
                act.activation(n_vs[a][:, :], bank[5 + a][0:NS_TOK, 2 * P:3 * P], ACT.Copy).then_inc(nv_ready, 1)

            def exp_of(p, u, col):
                return act.activation(p, p, ACT.Exp, bias=n_neg[:, u, col:col + 1], scale=SCALE, accum_out=n_sum[:, u, col:col + 1])

            def exps(V, u, r, k):
                act.wait_ge(nneg_ready, V - PRIME)
                if u < 2:
                    for a in range(2):
                        pg = n_p[:, u, 512 * a:512 * a + 2 * P * (u + 1)].rearrange("p (k g j) -> p k g j", g=2, j=P)
                        for grp in range(2):
                            exp_of(pg[:, :, grp, :], u, 2 * (a + 1) + grp)
                    for grp in range(2):
                        e = exp_of(n_p[:, u, 1024 + 32 * grp:1056 + 32 * grp], u, grp)
                else:
                    exp_of(n_ps[:, 1088:1280], u, 2)
                    e = exp_of(n_ps[:, 1280:1280 + N_CMP_S], u, 0)
                e.then_inc(nexp_ready, 1)

            def keep(V, u, r, k):
                act.wait_ge(ns_ready, V)
                act.wait_ge(npt_turned, V - 3)
                act.activation(n_ps[:, 0:512], bank[0][:, :], ACT.Copy)
                act.activation(n_ps[:, 512:1024], bank[1][:, :], ACT.Copy).then_inc(sel_kept, 1)

            def sel_exps(V, u, r, k):
                act.wait_ge(selneg_ready, r + 1)
                exp_of(n_ps[:, 0:1088], u, 1).then_inc(selexp_ready, 1)

            def copies(V, u, r, k):
                act.wait_ge(npt_turned, V)
                if u < 2:
                    act.wait_ge(no_ready, V - 1 - (u == 0))
                    n = 2 * P * (u + 1)
                    act.activation(n_pt[:, 0:n], bank[3][:, 0:n], ACT.Copy)
                    act.activation(n_pt[:, 512:512 + n], bank[5][:, 0:n], ACT.Copy)
                    act.activation(n_pt[0:64, 1024:1152], bank[6][0:64, 0:P], ACT.Copy).then_inc(npt_copied, 1)
                    return
                act.wait_ge(no_ready, V - 3)
                act.activation(n_pts[:, 0:512], bank[3][:, :], ACT.Copy)
                act.activation(n_pts[:, 512:1024], bank[5][:, :], ACT.Copy)
                act.activation(n_pts[:, 1024:1152], bank[6][:, 0:P], ACT.Copy)
                act.activation(n_pts[0:64, 1152:1408], bank[6][0:64, P:3 * P], ACT.Copy)
                act.activation(n_pts[0:N_CMP_S, 1408:1536], bank[6][0:N_CMP_S, 3 * P:4 * P], ACT.Copy).then_inc(npt_copied, 1)

            def outs(V, u, r, k):
                act.wait_ge(no_ready, V)
                if u < 2:
                    o = act.activation(queries(h_hi, r, slice(P * u, P * u + P)), bank[7][:, 0:P], ACT.Copy)
                else:
                    for grp in range(2):
                        o = act.activation(sample_rows(h_hi, grp, r), out_block(bank[7], grp), ACT.Copy)
                o.then_inc(no_hi, 1)

            rounds(act, NSA_ROUND, dict(exps=exps, keep=keep, sel_exps=sel_exps, copies=copies, outs=outs))

        def dve_nsa(dve, st):
            def pair_up():
                dve.wait_ge(evacuated, st["g0"] + 2)
                for e in range(2):
                    for grp in range(2):
                        dve.tensor_copy(n_pairs[HD * e:HD * e + HD, :, grp, :], n_kv[HD * grp:HD * grp + HD, 0:2, e:NP_TOK:2])\
                            .then_inc(pairs_ready, 1)

            def lay_keys():
                dve.wait_ge(rope_ready, 2 + st["rope"] + 2)
                dve.wait_ge(lay_clear, 2)
                for a in range(2):
                    for grp in range(2):
                        rows = slice(HD * grp, HD * grp + HD)
                        dve.tensor_copy(n_kbd[a][rows, :, grp, :], n_kv[rows, 2 + 2 * a, 0:NP_TOK].rearrange("p (c j) -> p c j", c=2))\
                            .then_inc(nk_ready, 1)

            def lay():
                dve.wait_ge(n_laid, 1)
                dve.tensor_copy(n_gt[:, :, :], bank[7][:, 0:2 * P].rearrange("p (c n) -> p c n", c=2)[:, :, 0:48]).then_inc(n_lay_step, 1)
                dve.tensor_copy(n_kcb[:, :], bank[7][:, 256:320]).then_inc(n_lay_step, 1)
                dve.tensor_copy(n_vcb[:, :], bank[4][0:64, 0:P]).then_inc(n_lay_step, 1)
                dve.tensor_tensor(n_srow[:, :, :], bank[7][:, 320:512].rearrange("p (k t) -> p k t", k=3),
                                  cst("tok_of").rearrange("p (k t) -> p k t", k=1).broadcast_to([P, 3, NS_TOK]), ALU.mult)\
                    .then_inc(n_lay_step, 1)
                dve.wait_ge(n_lay_step, 4)
                dve.tensor_reduce(n_sg[:, :, :], n_srow[:, :, :].rearrange("p k (b s) -> p b k s", s=NQ), AX.X, ALU.add)\
                    .then_inc(n_lay_step, 1)

            dve_in_turning(dve, st, [n_kv[:, t:t + 1, :] for t in range(6)] + [n_gates[:, :, :], None]
                           + [n_q[:, t:t + 1, :] for t in range(KT)], nsa_turns, between={1: pair_up, 4: lay_keys, 6: lay})
            dve.wait_ge(evacuated, st["g0"] + st["groups"])
            for a in range(2):
                dve.memset(n_vbd[a][:, :, :, :], 0.0).then_inc(lay_clear, 1)
            dve.wait_ge(n_lay_step, 5)
            dve.wait_ge(rope_ready, 2 + st["rope"] + 10)

            causal = cst("m_band")[:, 2 * P:4 * P]

            def stepped(u, r, m):
                dve.wait_ge(n_step[u], (3, 3, 11)[u] * r + m)

            def mask(V, u, r, k):
                dve.wait_ge(ns_ready, V)
                dve.wait_ge(npt_turned, V - 3)
                if u == 2:
                    m = cst("m_new").rearrange("p (b k) -> p b k", b=NB)[:, bass.ds(r, 1), :].broadcast_to([P, 2, NS_TOK])
                    dve.tensor_tensor(n_ps[:, 1024:1152].rearrange("p (a k) -> p a k", a=2),
                                      bank[2][:, 0:128].rearrange("p (a k) -> p a k", a=2), m, ALU.add)
                    dve.tensor_tensor(n_ps[:, 1152:1280], bank[2][:, 128:256], cst("m_old"), ALU.add)
                    dve.tensor_copy(n_ps[:, 1280:1280 + N_CMP_S], bank[2][:, 256:256 + N_CMP_S]).then_inc(nmasked, 1)
                    return
                if u:
                    dve.tensor_copy(n_p[:, u, 0:256], bank[0][:, 0:256])
                    dve.tensor_tensor(n_p[:, u, 256:512], bank[0][:, 256:512], causal, ALU.add)
                    dve.tensor_tensor(n_p[:, u, 512:1024], bank[1][:, :], cst("m_band"), ALU.add)
                else:
                    for a in range(2):
                        dve.tensor_tensor(n_p[:, u, 512 * a:512 * a + 256], bank[a][:, 0:256], causal, ALU.add)
                seen = cst("m_cmp")[:, 8 - 8 * u:40 - 8 * u].rearrange("p (g n) -> p g n", g=1).broadcast_to([P, 2, 32])
                dve.tensor_tensor(n_p[:, u, 1024:1088].rearrange("p (g n) -> p g n", g=2),
                                  bank[2][:, 0:64].rearrange("p (g n) -> p g n", g=2), seen, ALU.add).then_inc(nmasked, 1)

            def maxima(V, u, r, k):
                dve.wait_ge(nmasked, V)
                if u == 2:
                    dve.tensor_reduce(n_mx[:, u, 0:1], n_ps[:, 1280:1280 + N_CMP_S], AX.X, ALU.max)
                    dve.tensor_reduce(n_mx[:, u, 2:3], n_ps[:, 1088:1280], AX.X, ALU.max).then_inc(n_step[u], 1)
                    return
                for a in range(2):
                    pg = n_p[:, u, 512 * a:512 * a + 2 * P * (u + 1)].rearrange("p (k g j) -> p g k j", g=2, j=P)
                    dve.tensor_reduce(n_mx[:, u, 2 * a + 2:2 * a + 4], pg, AX.XY, ALU.max)
                dve.tensor_reduce(n_mx[:, u, 0:2], n_p[:, u, 1024:1088].rearrange("p (g n) -> p g n", g=2), AX.X, ALU.max)\
                    .then_inc(n_step[u], 1)

            def negate(V, u, r, k):
                stepped(u, r, 1)
                cols = slice(0, 6) if u < 2 else slice(0, 3, 2)
                dve.tensor_scalar(n_neg[:, u, cols], n_mx[:, u, cols], -SCALE, None, ALU.mult).then_inc(nneg_ready, 1)

            def inverse(V, u, r, k):
                dve.wait_ge(nexp_ready, V - PRIME)
                n = 6 if u < 2 else 1
                dve.reciprocal(n_rec[:, u, 0:n], n_sum[:, u, 0:n]).then_inc(n_step[u], 1)

            def gate(V, u, r, k):
                stepped(u, r, 2)
                g = n_gt[:, u, :].rearrange("p (k g t) -> p k g t", k=3, g=2)[:, :, :, bass.ds(r, 1)].rearrange("p k g t -> p k (g t)")
                dve.tensor_tensor(n_fac[:, u, :].rearrange("p (k g) -> p k g", k=3), n_rec[:, u, :].rearrange("p (k g) -> p k g", k=3),
                                  g, ALU.mult).then_inc(n_step[u], 1)

            def scale(V, u, r, k):
                if u == 2:
                    stepped(u, r, 11)
                    dve.wait_ge(imp_ready, r + 1)
                    for col, at, n in ((0, 1280, N_CMP_S), (2, 1088, 192), (1, 0, 1088)):
                        p = n_ps[:, at:at + n]
                        o = dve.tensor_scalar(p, p, n_fac[:, u, col:col + 1], None, ALU.mult)
                    o.then_inc(np_ready[u], 1)
                    return
                stepped(u, r, 3)
                for a in range(2):
                    pg = n_p[:, u, 512 * a:512 * a + 2 * P * (u + 1)].rearrange("p (k g j) -> p k g j", g=2, j=P)
                    for grp in range(2):
                        col = 2 * (a + 1) + grp
                        dve.tensor_scalar(pg[:, :, grp, :], pg[:, :, grp, :], n_fac[:, u, col:col + 1], None, ALU.mult)
                for grp in range(2):
                    pc = n_p[:, u, 1024 + 32 * grp:1056 + 32 * grp]
                    o = dve.scalar_tensor_tensor(out=pc, in0=pc, scalar=n_fac[:, u, grp:grp + 1],
                                                 in1=cst("ok_cmp")[:, 8 - 8 * u:40 - 8 * u], op0=ALU.mult, op1=ALU.mult)
                o.then_inc(np_ready[u], 1)

            def remainder(V, u, r, k):
                dve.wait_ge(no_hi, V)
                if u < 2:
                    rows = slice(P * u, P * u + P)
                    o = dve.tensor_tensor(queries(h_lo, r, rows), bank[7][:, 0:P], queries(h_hi, r, rows).bitcast(F32), ALU.subtract)
                else:
                    for grp in range(2):
                        o = dve.tensor_tensor(sample_rows(h_lo, grp, r), out_block(bank[7], grp),
                                              sample_rows(h_hi, grp, r).bitcast(F32), ALU.subtract)
                o.then_inc(no_lo, 1)

            def block_probs(V, u, r, k):
                stepped(u, r, 2)
                p = n_ps[:, 1280:1280 + N_CMP_S]
                dve.tensor_scalar(p, p, n_rec[:, u, 0:1], None, ALU.mult).then_inc(pc_ready, 1)

            def block_scores(V, u, r, k):
                dve.wait_ge(imp_ready, r + 1)
                dve.tensor_reduce(n_imp[:, 0:14], bank[4][:, 3:59].rearrange("p (b f) -> p b f", f=4), AX.X, ALU.add)\
                    .then_inc(n_step[u], 1)
                stepped(u, r, 3)
                dve.tensor_tensor(n_imp[:, 0:14], n_imp[:, 0:14], bank[4][:, 7:60:4], ALU.add).then_inc(n_step[u], 1)

            def block_mask(V, u, r, k):
                stepped(u, r, 4)
                dve.tensor_reduce(n_low[:, :], n_imp[:, 0:14], AX.X, ALU.min).then_inc(n_step[u], 1)
                stepped(u, r, 5)
                dve.scalar_tensor_tensor(out=n_hit[:, 0:14], in0=n_imp[:, 0:14], scalar=n_low[:, :], in1=cst("blk_no")[:, 1:15],
                                         op0=ALU.is_equal, op1=ALU.mult).then_inc(n_step[u], 1)
                stepped(u, r, 6)
                dve.tensor_reduce(n_drop[:, :], n_hit[:, 0:14], AX.X, ALU.max).then_inc(n_step[u], 1)
                stepped(u, r, 7)
                dve.tensor_scalar(n_blk[:, :], cst("blk_no"), n_drop[:, :], NEG, ALU.is_equal, ALU.mult).then_inc(n_step[u], 1)

            def select(V, u, r, k):
                stepped(u, r, 8)
                dve.wait_ge(sel_kept, PRIME + r + 1)
                p = n_ps[:, 0:1024].rearrange("p (b j) -> p b j", b=16)
                dve.tensor_tensor(p, p, n_blk[:, :].rearrange("p (b j) -> p b j", j=1).broadcast_to([P, 16, 64]), ALU.add)\
                    .then_inc(n_step[u], 1)
                stepped(u, r, 9)
                dve.tensor_reduce(n_mx[:, u, 1:2], n_ps[:, 0:1088], AX.X, ALU.max).then_inc(n_step[u], 1)
                stepped(u, r, 10)
                dve.tensor_scalar(n_neg[:, u, 1:2], n_mx[:, u, 1:2], -SCALE, None, ALU.mult).then_inc(selneg_ready, 1)

            def sel_inverse(V, u, r, k):
                dve.wait_ge(no_ready, V - 3)
                dve.tensor_copy(n_vcst[0:N_CMP_S, :], one(vcmp_s[0:N_CMP_S], r))
                dve.tensor_copy(n_fac[:, u, 0:1], n_sg[:, bass.ds(r, 1), 0:1].rearrange("p a k -> p (a k)"))
                dve.wait_ge(selexp_ready, r + 1)
                dve.reciprocal(n_rec[:, u, 1:3], n_sum[:, u, 1:3]).then_inc(rec_ready, 1)
                dve.wait_ge(rec_ready, r + 1)
                dve.tensor_tensor(n_fac[:, u, 1:3], n_rec[:, u, 1:3],
                                  n_sg[:, bass.ds(r, 1), 1:3].rearrange("p a k -> p (a k)"), ALU.mult).then_inc(n_step[u], 1)

            rounds(dve, NSA_ROUND, dict(mask=mask, maxima=maxima, negate=negate, inverse=inverse, gate=gate, scale=scale,
                                        remainder=remainder, block_probs=block_probs, block_scores=block_scores,
                                        block_mask=block_mask, select=select, sel_inverse=sel_inverse))
            dve.wait_ge(no_lo, PRIME + 24)
            dve.nop().then_inc(mixer_ready, KT)

        def pool_nsa(pool, st):
            pool.wait_ge(evacuated, st["g0"])
            pool.memset(n_hid[:, :, :, :], 0.0).then_inc(hid_clear, 1)
            for a in range(2):
                pool.memset(n_kbd[a][:, :, :, :], 0.0).then_inc(lay_clear, 1)
            pool_turns(pool, st, nsa_turns)
            pool.wait_ge(evacuated, st["g0"] + st["groups"])
            pool.wait_ge(rope_ready, 2 + st["rope"] + 10)

            def stage_queries(V, u, r, k):
                pool.wait_ge(ns_ready, V - 3)
                if u < 2:
                    rows = slice(P * u, P * u + P)
                    pool.tensor_copy(n_qst[:, u, 0, :], queries(n_q, r, rows))
                    pool.tensor_copy(n_qst[:, u, 1, :], queries(n_qr, r, rows)).then_inc(nq_staged, 1)
                    return
                for a, q in enumerate((n_q, n_qr)):
                    staged = pool.tensor_tensor(
                        n_qss[:, a, :].rearrange("p (g t s) -> p g t s", g=2, s=NQ), sample_queries(q, r),
                        cst("bd").rearrange("p (g t s) -> p g t s", g=2, s=NQ), ALU.mult)
                staged.then_inc(nq_staged, 1)

            def stage_values(V, u, r, k):
                if u == 2:
                    pool.wait_ge(win_landed, 32)
                    pool.wait_ge(no_ready, V - 3)
                    pool.tensor_copy(n_vst[:, :], one(n_wv, r)).then_inc(nv_staged, 1)

            rounds(pool, NSA_ROUND, dict(scores=stage_queries, exps=stage_values))

        mix_stored = {k: sem(k + "_stored") for k in ("cm", "swa", "sc", "nsa") if k in kinds}
        sp_after, sp_store = {}, {}
        pe_stage = {"ffn_in": pe_in, "ffn_out": pe_ffn_out, "mix_out": pe_mix_out}
        act_stage = {"ffn_in": act_ffn_in, "ffn_out": act_ffn_out, "mix_out": act_mix_out}
        dve_stage = {"ffn_in": dve_ffn_in, "ffn_out": dve_ffn_out, "mix_out": dve_mix_out}
        pool_stage = {"ffn_in": pool_ffn_in, "ffn_out": pool_out, "mix_out": pool_out}
        if "cm" in kinds:
            sp_after["cm_in"], sp_store["cm"] = sp_cm_load, sp_cm_store
            pe_stage["cm_in"], act_stage["cm_in"], dve_stage["cm_in"], pool_stage["cm_in"] = pe_cm, act_cm_in, dve_cm_in, pool_cm_in
        if "swa" in kinds:
            sp_after["swa_in"], sp_store["swa"] = sp_swa_load, sp_swa_store
            pe_stage["swa_in"], act_stage["swa_in"], dve_stage["swa_in"], pool_stage["swa_in"] = pe_swa, act_swa, dve_swa, pool_swa
        if "sc" in kinds:
            sp_store["sc"] = sp_sc_store
            pe_stage["sc_in"], act_stage["sc_in"], dve_stage["sc_in"], pool_stage["sc_in"] = pe_in, act_sc_in, dve_sc_in, pool_sc_in
        if "nsa" in kinds:
            sp_after["nsa_in"], sp_store["nsa"] = sp_nsa_load, sp_nsa_store
            pe_stage["nsa_in"], act_stage["nsa_in"], dve_stage["nsa_in"], pool_stage["nsa_in"] = pe_nsa, act_nsa, dve_nsa, pool_nsa


        def kind_of(name):
            return next((st for st in stages if st["kind"] == name), None)

        cm_st, swa_st, nsa_st = (kind_of(k + "_in") for k in ("cm", "swa", "nsa"))
        block = ctx.enter_context(nc.Block())

        def guard(engine, st):
            at = stages.index(st)
            if at and stages[at - 1]["kind"] == "mix_out":
                engine.wait_ge(mix_stored[stages[at - 1]["mixer"]], 16)

        @block.sync
        def _(sp):
            if "nsa" in kinds:
                sp_past_first(sp)
            sp.dma_start(const[:, :], A["const"]).then_inc(const_landed, 16)
            sp.dma_start(gains[:, :, :], A["gains"]).then_inc(const_landed, 16)
            sp.dma_start(x[:, :, :], A["x_t"]).then_inc(x_landed, 16)
            if "sc" in kinds:
                sp_sc_load(sp)
            for n in range(RAW):
                sp_chunk(sp, n)
            if "nsa" in kinds:
                sp_past_rest(sp)
            for st in stages:
                sp_stream(sp, st)
                if st["kind"] in sp_after:
                    sp_after[st["kind"]](sp)
                if st["kind"] == "mix_out":
                    sp_store[st["mixer"]](sp)
            for half in range(2):
                tiles = slice(KT // 2 * half, KT // 2 * (half + 1))
                sp.wait_ge(y_ready, KT // 2 * (half + 1))
                sp.dma_start(O["y_t"][:, tiles, :], x[:, tiles, :]).then_inc(stored, 16)
            sp.wait_ge(stored, 32)
            for s in mix_stored.values():
                sp.wait_ge(s, 16)
            if "swa" in kinds:
                sp.wait_ge(swa_passed, 16)
            if "nsa" in kinds:
                sp.wait_ge(win_passed, 16)

        @block.tensor
        def _(pe):
            for name in pe_primed:
                pe.nop().then_inc(name, PRIME)
            if "nsa" in kinds:
                pe_past(pe)
            pe.wait_ge(const_landed, 32)
            for st in stages:
                pe_stage[st["kind"]](pe, st)
            pe_final(pe)

        @block.scalar
        def _(act):
            act.nop().then_inc(silu_ready, 2)
            act.nop().then_inc(hhi_ready, 2)
            if "cm" in kinds:
                act.nop().then_inc(gelu_ready, 2)
            for name in act_primed:
                act.nop().then_inc(name, PRIME)
            if "nsa" in kinds:
                act_past(act, 0)
            act_x_in(act)
            for n in range(RAW):
                act_split(act, n)
            if "nsa" in kinds:
                act_past(act, 1)
            for st in stages:
                if st["kind"] == "ffn_in":
                    guard(act, st)
                act_stage[st["kind"]](act, st)
            act_std(act, final_norm)

        @block.vector
        def _(dve):
            if kinds & {"swa", "nsa"}:
                dve.nop().then_inc(rot_sin, 2)
            for name in dve_primed:
                dve.nop().then_inc(name, PRIME)
            if "nsa" in kinds:
                dve_past(dve)
            dve_x_in(dve)
            for n in range(RAW):
                dve_split(dve, n)
            for st in stages:
                dve_stage[st["kind"]](dve, st)
            dve_final(dve)

        @block.gpsimd
        def _(pool):
            pool.nop().then_inc(prod_ready, 2)
            pool.nop().then_inc(hlo_ready, 2)
            if kinds & {"swa", "nsa"}:
                pool.nop().then_inc(rope_ready, 2)
            for name in pool_primed:
                pool.nop().then_inc(name, PRIME)
            if "nsa" in kinds:
                pool_past(pool)
            pool_x_in(pool)
            for st in stages:
                if st["kind"] == "ffn_in":
                    guard(pool, st)
                pool_stage[st["kind"]](pool, st)


def feature_major(a):
    return np.ascontiguousarray(a.reshape(a.shape[0], -1, P).transpose(2, 1, 0))


def chunks_of(w, k0=0, k=KT):
    c = w[P * k0:P * (k0 + k)].reshape(k, P, -1, CW).transpose(2, 1, 0, 3)
    out = np.zeros((c.shape[0], P, KT, CW), w.dtype)
    out[:, :, 0:k] = c
    return out.reshape(c.shape[0], P, KT * CW)


def lay_out(inputs, schedule):
    v = {k: np.asarray(a) for k, a in inputs.items()}
    ins = {"const": CONST}
    heads = np.concatenate([np.arange(HD * q, HD * q + HD) for q in HEAD_ORDER])
    mixers = {"cm": 0, "swa": 1, "sc": 2, "nsa": 3}
    stream, norms = [], []
    for s in schedule:
        if s[0] == "ffn":
            w_in, w_out = v["ffn_in"][s[1], s[2]], v["ffn_out"][s[1], s[2]]
            gate, up = chunks_of(w_in[:, :FF]), chunks_of(w_in[:, FF:])
            stream.append(np.stack([gate, up], 1).reshape(-1, P, KT * CW))
            stream.append(np.stack([chunks_of(w_out, 0), chunks_of(w_out, 8), chunks_of(w_out, 16, 6)], 1)
                          .reshape(-1, P, KT * CW))
            norms.append(v["norm_g"][s[1], 2 * s[2]])
            continue
        norms.append(v["norm_g"][mixers[s[0]], 1])
        if s[0] == "cm":
            stream += [chunks_of(v["cm_w_in"]), chunks_of(v["cm_w_out"])]
        elif s[0] == "swa":
            w = v["swa_w_qkv"]
            stream += [chunks_of(w[:, D:]), chunks_of(w[:, heads]), chunks_of(v["swa_w_o"][heads])]
        elif s[0] == "sc":
            w = chunks_of(v["sc_w_in"]).reshape(3, 4, P, KT * CW).transpose(1, 0, 2, 3).reshape(12, P, KT * CW)
            stream += [w, chunks_of(v["sc_w_out"])]
        else:
            w = v["nsa_w_in"]
            gates = np.concatenate([w[:, D + 768:], np.zeros((D, CW - 48), w.dtype)], 1)
            stream += [chunks_of(w[:, D:D + 768]), chunks_of(gates), chunks_of(w[:, heads]), chunks_of(v["nsa_w_o"][heads])]
    norms.append(v["final_norm_g"])
    ins["stream"] = np.concatenate(stream, 0)
    gains = np.zeros((P, 14, KT), np.float32)
    for n, a in enumerate(norms):
        gains[:, n] = a.reshape(KT, P).T
    gains[:, 13] = v["cm_norm_g"].reshape(KT, P).T
    ins["gains"] = gains
    ins["x_t"] = feature_major(np.concatenate([v["x_prompt"][0], v["x_sample"].reshape(NS_TOK, D)], 0))
    ins["ws_t"] = np.ascontiguousarray(v["cm_w_s"].transpose(2, 0, 1))
    ws_s = np.zeros((NS_TOK, 4, NS_TOK), np.float32)
    for b in range(NB):
        ws_s[NQ * b:NQ * b + NQ, :, NQ * b:NQ * b + NQ] = v["cm_w_s"][:, :NQ, :NQ].transpose(2, 0, 1)
    ins["ws_s_t"] = ws_s
    bs = np.concatenate([v["cm_b_s"], v["cm_b_s"]] + [v["cm_b_s"][:, :NQ]] * NB, 1)
    ins["bs"] = np.ascontiguousarray(np.broadcast_to(bs[None], (P,) + bs.shape))
    ins["conv_w"] = np.ascontiguousarray(v["sc_conv_w"].reshape(3, KT, P).transpose(2, 0, 1))
    ins["conv_prev"] = feature_major(v["state_conv"].reshape(2 * NB, D))
    for name, cache in (("swa", v["cache_swa_kv"]), ("win", v["cache_nsa_win_kv"])):
        kv = cache.reshape(NB, P, 2, P)
        ins[name + "_k"] = np.ascontiguousarray(kv[:, :, 0].transpose(2, 0, 1))
        ins[name + "_v"] = np.ascontiguousarray(kv[:, :, 1].transpose(1, 0, 2))
        ins[name + "_old"] = np.ascontiguousarray(cache.reshape(NB, P, 2 * P))
    sinks = v["swa_sinks"]
    ins["sinks"] = np.concatenate([np.tile(sinks[None], (P, 1)), np.repeat(sinks, NQ)[:, None]], 1)
    pool = v["cache_nsa_kv"]
    n_pool = pool.shape[0]
    pairs = pool[:, :, 0:2].reshape(n_pool, N_PAIR, 2, 2, 2, HD).transpose(0, 2, 5, 3, 4, 1)
    ins["pool_cmp"] = np.ascontiguousarray(pairs.reshape(n_pool, P, 2 * P))
    k_t = pool[:, :, 2].reshape(n_pool, P, P).transpose(0, 2, 1)
    ins["pool_sel"] = np.concatenate([k_t, pool[:, :, 3].reshape(n_pool, P, P)], 2)
    ins["pages"] = np.ascontiguousarray(v["page_table"].reshape(1, -1))
    ins["cmp_w1"] = np.ascontiguousarray(v["nsa_cmp_w1"].reshape(2, 16, P, 256).transpose(2, 0, 1, 3))
    ins["cmp_pe"] = np.ascontiguousarray(v["nsa_cmp_pe"].reshape(2, 16, P).transpose(2, 0, 1))
    w2 = np.zeros((P, 2, 2, 2, P), np.float32)
    for grp in range(2):
        w2[:, :, :, grp, HD * grp:HD * grp + HD] = v["nsa_cmp_w2"].reshape(2, 2, P, HD).transpose(2, 0, 1, 3)
    ins["cmp_w2"] = w2
    return ins


OUTS = {
    "y_t": (P, KT, T), "cm_v": (P, KT, NS_TOK), "conv_end": (P, KT, 2 + 2 * NB), "swa_kv": (P, 2, T),
    "swa_passed": (NB, P - NQ, 2 * P), "nsa_kv": (P, 6, T), "win_passed": (NB, P - NQ, 2 * P),
}


def assemble(got):
    def rows(a):
        return a.transpose(2, 1, 0).reshape(a.shape[2], -1)

    y = rows(got["y_t"])
    out = [y[:NP_TOK].reshape(1, NP_TOK, D), y[NP_TOK:].reshape(NB, NQ, D),
           rows(got["cm_v"]).reshape(NB, NQ, D)]
    swa = rows(got["swa_kv"])
    out.append(swa[NP_TOK - P:NP_TOK].reshape(1, P, 2, 2, HD))
    out.append(np.concatenate([got["swa_passed"], swa[NP_TOK:].reshape(NB, NQ, 2 * P)], 1).reshape(NB, P, 2, 2, HD))
    end = rows(got["conv_end"])
    out += [end[0:2].reshape(1, 2, D), end[2:].reshape(NB, 2, D)]
    nsa = rows(got["nsa_kv"])
    out += [nsa[:NP_TOK, :4 * P].reshape(1, NP_TOK, 4, 2, HD), nsa[NP_TOK:, :4 * P].reshape(NB, NQ, 4, 2, HD)]
    win = nsa[:, 4 * P:]
    out.append(win[NP_TOK - P:NP_TOK].reshape(1, P, 2, 2, HD))
    out.append(np.concatenate([got["win_passed"], win[NP_TOK:].reshape(NB, NQ, 2 * P)], 1).reshape(NB, P, 2, 2, HD))
    return tuple(np.ascontiguousarray(a) for a in out)


def kernel(**inputs):
    import concourse.bacc as bacc
    from concourse.bass_utils import run_bass_kernel_spmd

    nc = bacc.Bacc("TRN2", target_bir_lowering=False, num_devices=1)
    arrays = lay_out(inputs, SCHEDULE)
    A = {n: nc.dram_tensor(n, a.shape, mybir.dt.from_np(a.dtype), kind="ExternalInput").ap() for n, a in arrays.items()}
    O = {n: nc.dram_tensor("out_" + n, s, F32, kind="ExternalOutput").ap() for n, s in OUTS.items()}
    program(nc, A, O, SCHEDULE)
    results = run_bass_kernel_spmd(nc, [arrays], core_ids=[0]).results[0]
    return assemble({n: results["out_" + n] for n in OUTS})
```
